# Optimizing a Trainium2 kernel written in Bass

```python
import math
import jax, jax.numpy as jnp
from jax import lax
import numpy as np

D_MODEL = 1024
BATCH = 1
SEQ = 1024
DEPTH = 1

EPS = 1e-6
MEM_LEN = 256
RET_HEADS = 4
RET_DK = 128
RET_DV = 128
RET_QK_WIDTH = RET_HEADS * RET_DK
RET_V_WIDTH = RET_HEADS * RET_DV
RET_CHUNK = 128
ROPE_BASE = 10000.0
S5_GROUPS = 16
S5_GROUP_DIM = 16
S5_STATE = 64
S5_WIDTH = S5_GROUPS * S5_GROUP_DIM
S5_DT_MIN = 0.001
S5_DT_MAX = 0.1
MEM_HEADS = 4
MEM_HEAD_DIM = 64
MEM_WIDTH = MEM_HEADS * MEM_HEAD_DIM
N_BRANCHES = 3
IN_SPLITS = (RET_QK_WIDTH, RET_QK_WIDTH, RET_V_WIDTH, RET_V_WIDTH, S5_WIDTH, MEM_WIDTH, N_BRANCHES * D_MODEL)
IN_COLS = sum(IN_SPLITS)
PEER_HEADS = 8
PEER_NKEYS = 128
PEER_EXPERTS = PEER_NKEYS * PEER_NKEYS
PEER_QDIM = 256
PEER_HALF = PEER_QDIM // 2
PEER_TOPK = 16
PEER_BLOCK = 128

kernel_name = "hybrid_retention_s5_memattn_peer_block"

def _rms_norm(x, gain):
    xf = x.astype(jnp.float32)
    y = xf * lax.rsqrt(jnp.mean(xf * xf, axis=-1, keepdims=True) + EPS)
    return (y * gain.astype(jnp.float32)).astype(x.dtype)

def _rope(x, positions):
    half = x.shape[-1] // 2
    inv_freq = ROPE_BASE ** (-jnp.arange(half, dtype=jnp.float32) / half)
    ang = positions.astype(jnp.float32)[..., None] * inv_freq
    cos = jnp.cos(ang)[:, :, None, :]
    sin = jnp.sin(ang)[:, :, None, :]
    xf = x.astype(jnp.float32)
    x1, x2 = xf[..., :half], xf[..., half:]
    return jnp.concatenate([x1 * cos - x2 * sin, x1 * sin + x2 * cos], axis=-1)

def _retention(q, k, v):
    bsz, seq, nh, dk = q.shape
    dv = v.shape[-1]
    c = RET_CHUNK
    nc = seq // c
    log_gamma = jnp.log1p(-jnp.exp2(-5.0 - jnp.arange(nh, dtype=jnp.float32)))
    pos = jnp.arange(c, dtype=jnp.float32)
    rel = pos[:, None] - pos[None, :]
    decay_intra = jnp.exp(jnp.where((rel >= 0)[None], rel[None] * log_gamma[:, None, None], -jnp.inf))
    q = q.reshape(bsz, nc, c, nh, dk)
    k = k.reshape(bsz, nc, c, nh, dk)
    v = v.reshape(bsz, nc, c, nh, dv)
    scores = jnp.einsum("bnihd,bnjhd->bnhij", q, k) * decay_intra
    inner = jnp.einsum("bnhij,bnjhe->bnihe", scores, v)
    k_dec = k * jnp.exp((c - 1.0 - pos)[:, None] * log_gamma[None, :])[:, :, None]
    kv = jnp.einsum("bnjhd,bnjhe->nbhde", k_dec, v)
    chunk_decay = jnp.exp(c * log_gamma)[None, :, None, None]

    def step(state, kv_n):
        return state * chunk_decay + kv_n, state

    _, prev = lax.scan(step, jnp.zeros((bsz, nh, dk, dv), jnp.float32), kv)
    q_dec = q * jnp.exp((pos + 1.0)[:, None] * log_gamma[None, :])[:, :, None]
    cross = jnp.einsum("bnihd,nbhde->bnihe", q_dec, prev)
    return (inner + cross).reshape(bsz, seq, nh, dv)

def _complex_linear_op(e1, e2):
    ar1, ai1, br1, bi1 = e1
    ar2, ai2, br2, bi2 = e2
    return (ar2 * ar1 - ai2 * ai1,
            ar2 * ai1 + ai2 * ar1,
            ar2 * br1 - ai2 * bi1 + br2,
            ar2 * bi1 + ai2 * br1 + bi2)

def _s5(u, a_re, a_im, log_dt, b_re, b_im, c_re, c_im, d, w_glu):
    bsz, seq, _ = u.shape
    f32 = jnp.float32
    uf = u.astype(f32).reshape(bsz, seq, S5_GROUPS, S5_GROUP_DIM)
    a_re = a_re.astype(f32)
    a_im = a_im.astype(f32)
    dt = jnp.exp(log_dt.astype(f32))[:, None]
    mag = jnp.exp(a_re * dt)
    lam_re = mag * jnp.cos(a_im * dt)
    lam_im = mag * jnp.sin(a_im * dt)
    den = a_re * a_re + a_im * a_im
    nr = lam_re - 1.0
    ni = lam_im
    cr = ((nr * a_re + ni * a_im) / den)[..., None]
    ci = ((ni * a_re - nr * a_im) / den)[..., None]
    b_re = b_re.astype(f32)
    b_im = b_im.astype(f32)
    bb_re = cr * b_re - ci * b_im
    bb_im = cr * b_im + ci * b_re
    bu_re = jnp.einsum("bsgh,gph->bsgp", uf, bb_re)
    bu_im = jnp.einsum("bsgh,gph->bsgp", uf, bb_im)
    la_re = jnp.broadcast_to(lam_re, bu_re.shape)
    la_im = jnp.broadcast_to(lam_im, bu_im.shape)
    _, _, x_re, x_im = lax.associative_scan(_complex_linear_op, (la_re, la_im, bu_re, bu_im), axis=1)
    y = (jnp.einsum("bsgp,ghp->bsgh", x_re, c_re.astype(f32))
         - jnp.einsum("bsgp,ghp->bsgh", x_im, c_im.astype(f32)))
    y = y.reshape(bsz, seq, S5_WIDTH) + d.astype(f32) * u.astype(f32)
    y = jax.nn.gelu(y)
    lin, gate = jnp.split(y @ w_glu.astype(f32), 2, axis=-1)
    return lin * jax.nn.sigmoid(gate)

def _memory_attention(q, k, v):
    bsz, seq = q.shape[0], q.shape[1]
    scores = jnp.einsum("bshd,bmhd->bhsm", q.astype(jnp.float32), k.astype(jnp.float32)) * (MEM_HEAD_DIM ** -0.5)
    p = jax.nn.softmax(scores, axis=-1)
    out = jnp.einsum("bhsm,bmhd->bshd", p, v.astype(jnp.float32))
    return out.reshape(bsz, seq, MEM_WIDTH)

def _peer(xn, w_q, keys, u_exp, v_exp):
    bsz, seq, dm = xn.shape
    t = bsz * seq
    xt = xn.reshape(t, dm)
    q = (xt @ w_q).reshape(t, PEER_HEADS, 2, PEER_HALF)
    s = jnp.einsum("thcd,hcnd->thcn", q, keys).astype(jnp.float32)
    s_top, i_top = lax.top_k(s, PEER_TOPK)
    cand_s = (s_top[:, :, 0, :, None] + s_top[:, :, 1, None, :]).reshape(t, PEER_HEADS, PEER_TOPK * PEER_TOPK)
    cand_i = (i_top[:, :, 0, :, None] * PEER_NKEYS + i_top[:, :, 1, None, :]).reshape(t, PEER_HEADS, PEER_TOPK * PEER_TOPK)
    s_fin, sel = lax.top_k(cand_s, PEER_TOPK)
    idx = jnp.take_along_axis(cand_i, sel, axis=-1)
    w = jax.nn.softmax(s_fin, axis=-1)
    nb = t // PEER_BLOCK

    def expert_block(args):
        xb, ib, wb = args
        ug = jnp.take(u_exp, ib, axis=0)
        vg = jnp.take(v_exp, ib, axis=0)
        hid = jnp.einsum("td,thkd->thk", xb, ug).astype(jnp.float32)
        act = jax.nn.gelu(hid) * wb
        return jnp.einsum("thk,thkd->td", act, vg.astype(jnp.float32))

    out = lax.map(expert_block, (xt.reshape(nb, PEER_BLOCK, dm),
                                 idx.reshape(nb, PEER_BLOCK, PEER_HEADS, PEER_TOPK),
                                 w.reshape(nb, PEER_BLOCK, PEER_HEADS, PEER_TOPK)))
    return out.reshape(bsz, seq, dm)

def setup_inputs(seed: int = 0) -> dict:
    key = jax.random.key(seed)
    ks = jax.random.split(key, 32)
    f32 = jnp.float32

    def nrm(k, shape, scale):
        return jax.random.normal(k, shape, f32) * scale

    def gain(k, shape):
        return 1.0 + 0.01 * jax.random.normal(k, shape, f32)

    x = nrm(ks[0], (BATCH, SEQ, D_MODEL), 1.0)
    mem = nrm(ks[1], (BATCH, MEM_LEN, D_MODEL), 1.0)
    positions = jnp.arange(SEQ, dtype=jnp.int32)[None, :] + jax.random.randint(ks[2], (BATCH, 1), 0, SEQ, dtype=jnp.int32)
    norm_mix = gain(ks[3], (DEPTH, D_MODEL))
    w_in = nrm(ks[4], (DEPTH, D_MODEL, IN_COLS), D_MODEL ** -0.5)
    norm_mem = gain(ks[5], (DEPTH, D_MODEL))
    w_mem_kv = nrm(ks[6], (DEPTH, D_MODEL, 2 * MEM_WIDTH), D_MODEL ** -0.5)
    s5_a_re = -0.5 + 0.01 * jax.random.normal(ks[7], (DEPTH, S5_GROUPS, S5_STATE), f32)
    s5_a_im = math.pi * jnp.arange(S5_STATE, dtype=f32) + 0.01 * jax.random.normal(ks[8], (DEPTH, S5_GROUPS, S5_STATE), f32)
    s5_log_dt = jax.random.uniform(ks[9], (DEPTH, S5_GROUPS), f32, minval=math.log(S5_DT_MIN), maxval=math.log(S5_DT_MAX))
    s5_b_re = nrm(ks[10], (DEPTH, S5_GROUPS, S5_STATE, S5_GROUP_DIM), (2 * S5_GROUP_DIM) ** -0.5)
    s5_b_im = nrm(ks[11], (DEPTH, S5_GROUPS, S5_STATE, S5_GROUP_DIM), (2 * S5_GROUP_DIM) ** -0.5)
    s5_c_re = nrm(ks[12], (DEPTH, S5_GROUPS, S5_GROUP_DIM, S5_STATE), S5_STATE ** -0.5)
    s5_c_im = nrm(ks[13], (DEPTH, S5_GROUPS, S5_GROUP_DIM, S5_STATE), S5_STATE ** -0.5)
    s5_d = nrm(ks[14], (DEPTH, S5_WIDTH), 1.0)
    s5_w_glu = nrm(ks[15], (DEPTH, S5_WIDTH, 2 * S5_WIDTH), S5_WIDTH ** -0.5)
    w_branch_ret = nrm(ks[16], (DEPTH, RET_V_WIDTH, D_MODEL), RET_V_WIDTH ** -0.5)
    w_branch_s5 = nrm(ks[17], (DEPTH, S5_WIDTH, D_MODEL), S5_WIDTH ** -0.5)
    w_branch_mem = nrm(ks[18], (DEPTH, MEM_WIDTH, D_MODEL), MEM_WIDTH ** -0.5)
    w_out = nrm(ks[19], (DEPTH, D_MODEL, D_MODEL), D_MODEL ** -0.5)
    norm_ffn = gain(ks[20], (DEPTH, D_MODEL))
    peer_w_q = nrm(ks[21], (DEPTH, D_MODEL, PEER_HEADS * PEER_QDIM), D_MODEL ** -0.5)
    peer_keys = nrm(ks[22], (DEPTH, PEER_HEADS, 2, PEER_NKEYS, PEER_HALF), PEER_HALF ** -0.5)
    peer_u = nrm(ks[23], (DEPTH, PEER_EXPERTS, D_MODEL), D_MODEL ** -0.5)
    peer_v = nrm(ks[24], (DEPTH, PEER_EXPERTS, D_MODEL), PEER_HEADS ** -0.5)
    norm_final = gain(ks[25], (D_MODEL,))
    return {"x": x, "mem": mem, "positions": positions, "norm_mix": norm_mix, "w_in": w_in,
            "norm_mem": norm_mem, "w_mem_kv": w_mem_kv, "s5_a_re": s5_a_re, "s5_a_im": s5_a_im,
            "s5_log_dt": s5_log_dt, "s5_b_re": s5_b_re, "s5_b_im": s5_b_im, "s5_c_re": s5_c_re,
            "s5_c_im": s5_c_im, "s5_d": s5_d, "s5_w_glu": s5_w_glu, "w_branch_ret": w_branch_ret,
            "w_branch_s5": w_branch_s5, "w_branch_mem": w_branch_mem, "w_out": w_out,
            "norm_ffn": norm_ffn, "peer_w_q": peer_w_q, "peer_keys": peer_keys, "peer_u": peer_u,
            "peer_v": peer_v, "norm_final": norm_final}

def reference(x, mem, positions, norm_mix, w_in, norm_mem, w_mem_kv, s5_a_re, s5_a_im,
              s5_log_dt, s5_b_re, s5_b_im, s5_c_re, s5_c_im, s5_d, s5_w_glu, w_branch_ret,
              w_branch_s5, w_branch_mem, w_out, norm_ffn, peer_w_q, peer_keys, peer_u,
              peer_v, norm_final):
    bsz, seq, _ = x.shape
    offsets = [int(o) for o in np.cumsum(IN_SPLITS)[:-1]]
    h = x
    for l in range(DEPTH):
        n = _rms_norm(h, norm_mix[l])
        z = n @ w_in[l]
        q_r, k_r, v_r, g_r, u_s5, q_m, gates = jnp.split(z, offsets, axis=-1)
        q_r = _rope(q_r.reshape(bsz, seq, RET_HEADS, RET_DK), positions)
        k_r = _rope(k_r.reshape(bsz, seq, RET_HEADS, RET_DK), positions) * (RET_DK ** -0.5)
        v_r = v_r.reshape(bsz, seq, RET_HEADS, RET_DV).astype(jnp.float32)
        ret = _retention(q_r, k_r, v_r)
        ret = ret * lax.rsqrt(jnp.mean(ret * ret, axis=-1, keepdims=True) + EPS)
        ret = ret.reshape(bsz, seq, RET_V_WIDTH) * jax.nn.silu(g_r.astype(jnp.float32))
        ssm = _s5(u_s5, s5_a_re[l], s5_a_im[l], s5_log_dt[l], s5_b_re[l], s5_b_im[l],
                  s5_c_re[l], s5_c_im[l], s5_d[l], s5_w_glu[l])
        mem_n = _rms_norm(mem, norm_mem[l])
        k_m, v_m = jnp.split(mem_n @ w_mem_kv[l], 2, axis=-1)
        mattn = _memory_attention(q_m.reshape(bsz, seq, MEM_HEADS, MEM_HEAD_DIM),
                                  k_m.reshape(bsz, MEM_LEN, MEM_HEADS, MEM_HEAD_DIM),
                                  v_m.reshape(bsz, MEM_LEN, MEM_HEADS, MEM_HEAD_DIM))
        gate_r, gate_s, gate_m = jnp.split(jax.nn.sigmoid(gates.astype(jnp.float32)), N_BRANCHES, axis=-1)
        merged = (gate_r * (ret @ w_branch_ret[l])
                  + gate_s * (ssm @ w_branch_s5[l])
                  + gate_m * (mattn @ w_branch_mem[l]))
        h = h + (merged @ w_out[l]).astype(h.dtype)
        h = h + _peer(_rms_norm(h, norm_ffn[l]), peer_w_q[l], peer_keys[l], peer_u[l], peer_v[l]).astype(h.dtype)
    return _rms_norm(h, norm_final)


_drawn_inputs = setup_inputs


def setup_inputs(seed=0):
    import zlib

    import numpy as np

    out = dict(_drawn_inputs(seed))
    spreads = {}
    factors = {'norm_mix': 3.79,
     'norm_mem': 8.0,
     's5_a_re': 200.0,
     'norm_ffn': 25.651,
     'norm_final': 175.963,
     's5_a_im': 46.952,
     's5_log_dt': 48.456,
     's5_b_re': 62.024,
     's5_b_im': 60.752,
     's5_c_re': 62.536,
     's5_c_im': 61.664}
    for name, (base, spread) in spreads.items():
        noise = np.random.default_rng([zlib.crc32(name.encode()), seed]).standard_normal(out[name].shape)
        drawn = base * np.exp(spread * noise) if base else spread * noise
        out[name] = __import__('jax').numpy.asarray(drawn.astype(out[name].dtype))
    for name, factor in factors.items():
        out[name] = (out[name] * factor).astype(out[name].dtype)
    return out
```

```python
import math
from contextlib import ExitStack

import numpy as np
import concourse.bass as bass
from concourse import mybir

F32 = mybir.dt.float32
BF16 = mybir.dt.bfloat16
I32 = mybir.dt.int32
U32 = mybir.dt.uint32
ALU = mybir.AluOpType
ACT = mybir.ActivationFunctionType
AX = mybir.AxisListType

P = 128
SEQ, D = 1024, 1024
TB = SEQ // P
KD = D // P
MEM = 256
EPS = 1e-6
HALF = 512
RH, RD = 4, 128
S5T = 8
MH, MD = 4, 64
Q0, K0, V0, G0, U0, GATE0 = 0, 512, 1024, 1536, 2048, 2560
MAGIC = 12582912.0
TWO_PI_HI, TWO_PI_MID, TWO_PI_LO = 6.28125, 0.0019350051879882812, 3.0199159819e-07
PI_BELOW = 3.1415925

GAMMA = [1.0 - 2.0 ** (-5.0 - h) for h in range(RH)]


def constants():
    i = np.arange(P)
    decay = np.zeros((P, RH, P))
    kfac, qfac = np.zeros((P, RH)), np.zeros((P, RH))
    for h, g in enumerate(GAMMA):
        decay[:, h, :] = np.where(i[:, None] <= i[None, :], (g ** -(i + 1.0))[:, None], 0.0) * RD ** -0.5
        kfac[:, h] = g ** (P - 1.0 - i) * RD ** -0.5
        qfac[:, h] = g ** (i + 1.0)
    inv = (10000.0 ** (-np.arange(64, dtype=np.float32) / np.float32(64))).astype(np.float32)
    rows = [np.eye(P), decay.reshape(P, RH * P), kfac, qfac, np.tile(inv, (P, 1)),
            np.tile(np.arange(P, dtype=np.float64), (P, 1)),
            np.tile(np.arange(50, dtype=np.float64), (P, 1))]
    return np.ascontiguousarray(np.concatenate(rows, 1).astype(np.float32))


C_ID, C_DEC, C_KF, C_QF, C_INV, C_IOTA, C_IOTA50 = 0, 128, 640, 644, 648, 712, 840
C_COLS = 890


def mixer_steps():
    main = [("z", ct, hf) for ct in range(4) for hf in range(2)]
    for hp in range(2):
        for tb in range(TB):
            main += [("qk", hp, tb), ("vg", hp, tb)]
    for dh in range(2):
        for br in range(3):
            main += [("gate", dh, br, tb) for tb in range(TB)]
    first = 8
    extra = {}

    def put(slot, job):
        extra.setdefault(slot, []).append(job)

    for hp in range(2):
        for tb in range(TB):
            at = 2 * (first + hp * 16 + 2 * tb)
            put(at + 4, ("turn", hp, tb))
            put(at + 6, ("score", hp, tb))
            put(at + 7, ("mix", hp, tb))
            put(at + 8, ("flip", hp, tb))
    chain = [(tb, mp) for tb in range(TB) for mp in range(2)]
    for c, (tb, mp) in enumerate(chain):
        for k, name in enumerate(("ascore", "aturn", "amix", "aflip")):
            put(2 * first + 1 + 4 * c + k, (name, tb, mp))
    for s in range(S5T):
        for hf in range(2):
            put(2 * first + 6 * s + 3 * hf, ("bu", s, hf))
            put(2 * first + 6 * s + 3 * hf + 6, ("y", s, hf))
    glu = 2 * first + 6 * S5T + 8
    put(glu, ("glu", 0))
    put(glu + 2, ("glu", 1))
    steps = [("xturn", tb, kh) for tb in range(TB) for kh in range(2)]
    steps += [("mturn", mt, kh) for mt in range(2) for kh in range(2)]
    steps += [("bturn", s) for s in range(0, S5T, 2)]
    pre = len(steps)
    for m, unit in enumerate(main):
        steps.append(unit)
        if m == 3:
            steps += [("mk", 0), ("mk", 1), ("mv", 0), ("mv", 1)]
        for at in (2 * m, 2 * m + 1):
            steps += extra.pop(at, [])
        if unit[0] == "gate" and unit[2] == 2 and unit[3] >= 2:
            steps.append(("gturn", unit[1], unit[3] - 2))
            if unit[3] == TB - 1:
                if unit[1] == 1:
                    steps += [("gturn", 1, TB - 2), ("gturn", 1, TB - 1)]
        if unit[0] == "gate" and unit[1] == 1 and unit[2] == 0 and unit[3] < 2:
            steps.append(("gturn", 0, TB - 2 + unit[3]))
    assert not extra, extra
    steps += [("out", dh, tb) for dh in range(2) for tb in range(TB)]
    return steps


MAIN = ("z", "qk", "vg", "gate")
OWN_BANK = ("bu", "y")


def build_mixer(nc, ins, h_sb, mem_map):
    steps = mixer_steps()
    main_no = {s: n for n, s in enumerate([s for s in steps if s[0] in MAIN])}
    misc_no = {s: n for n, s in enumerate([s for s in steps if s[0] not in MAIN + OWN_BANK])}
    gate_no = {s: n for n, s in enumerate([s for s in steps if s[0] == "gate"])}
    bu_no = {s: n for n, s in enumerate([s for s in steps if s[0] == "bu"])}
    chain_no = {(tb, mp): 2 * tb + mp for tb in range(TB) for mp in range(2)}
    turn_no = {(hp, tb): hp * TB + tb for hp in range(2) for tb in range(TB)}

    ctx = ExitStack()
    ctx.enter_context(nc.allow_non_contiguous_dma("small parameter columns"))
    at = {k: v for k, v in mem_map.items()}

    def sb(region, name, shape, dt=F32):
        size = int(np.prod(shape[1:])) * (2 if dt == BF16 else 4)
        off = at[region]
        at[region] = off + (size + 31) // 32 * 32
        assert at[region] <= mem_map[region] + mem_map[region + "_size"], (region, name, at[region] - mem_map[region])
        return nc.alloc_sbuf_tensor_at(name, shape, dt, offset=off)

    def sem(name):
        return ctx.enter_context(nc.semaphore(name))

    con = sb("const", "con", [P, C_COLS])
    small = sb("const", "small", [P, 40, 8])
    gains = sb("const", "gains", [P, 2, KD])
    stat = sb("const", "stat", [P, 64])
    nT = sb("nt", "nT", [P, KD, SEQ])
    wring = [sb("w", f"w{i}", [P, KD, HALF]) for i in range(3)]
    zT = sb("zt", "zT", [P, 4, SEQ])
    memT = sb("ret", "memT", [P, KD, MEM])
    mem_x = sb("ret", "mem_x", [P, 2, D])
    at["ret"] = mem_map["ret"]
    retT = sb("ret", "retT", [P, RH, SEQ])
    bbT = sb("s5c", "bbT", [P, 2, S5T, P])
    cT = sb("s5c", "cT", [P, 2, S5T, P])
    wglu = sb("s5c", "wglu", [P, 2, 512])
    at["s5c"] = mem_map["s5c"]
    merged = sb("s5c", "merged", [P, TB, HALF])
    xs = sb("wbr", "xs", [P, TB, D])
    at["wbr"] = mem_map["wbr"]
    tab = sb("wbr", "tab", [P, 2, SEQ])
    prod = sb("wbr", "prod", [P, 4, HALF])
    ysc = sb("wbr", "ysc", [P, 2, 2, HALF])
    kmT = sb("wbr", "kmT", [P, 2, 2, MEM])
    rope = sb("wbr", "rope", [P, 2, TB, 64])
    at["wbr"] = mem_map["wbr"]
    wbr = sb("wbr", "wbr", [P, 8, D])
    bsrc = sb("tmp", "bsrc", [P, 2, S5T, P])
    bbuf = sb("tmp", "bbuf", [P, 2, S5T, P])
    wbig = sb("tmp", "wbig", [P, S5T, P])
    at["tmp"] = mem_map["tmp"]
    qk = sb("tmp", "qk", [P, 2, HALF])
    vg = sb("tmp", "vg", [P, 3, HALF])
    qkr = sb("tmp", "qkr", [P, HALF])
    kdec = sb("tmp", "kdec", [P, 2, 256])
    qkT = sb("tmp", "qkT", [P, 2, HALF])
    sT = sb("tmp", "sT", [P, 256])
    ret = sb("tmp", "ret", [P, 256])
    state = sb("tmp", "state", [P, RH, P])
    psc = sb("tmp", "psc", [P, HALF])
    pT = sb("tmp", "pT", [P, HALF])
    mo = sb("tmp", "mo", [P, P])
    vm = sb("tmp", "vm", [P, 2, MEM])
    rsq = sb("tmp", "rsq", [P, 256])
    at["tmp"] = mem_map["tmp"]
    merT_lo = sb("tmp", "merT_lo", [P, 4, SEQ])
    gp = sb("tmp", "gp", [P, 2, HALF])
    xr = sb("tmp", "xr", [P, 2, HALF])
    at["zt"] = mem_map["zt"]
    merT_hi = sb("zt", "merT_hi", [P, 4, SEQ])
    sg = sb("sg", "sg", [P, 2, HALF])
    rt = sb("sg", "rt", [P, 4, 256])

    main_ps = [ctx.enter_context(nc.psum_tensor(f"main{i}", [P, HALF], F32)) for i in range(2)]
    misc_ps = [ctx.enter_context(nc.psum_tensor(f"misc{i}", [P, HALF], F32)) for i in range(2)]
    bu_ps = [ctx.enter_context(nc.psum_tensor(f"bu{i}", [P, HALF], F32)) for i in range(2)]
    p_ps = bu_ps
    y_ps = [ctx.enter_context(nc.psum_tensor(f"y{i}", [P, HALF], F32)) for i in range(2)]

    x_in = [sem(f"x_in{i}") for i in range(TB)]
    con_in = sem("con_in")
    par_in = sem("par_in")
    b_in = sem("b_in")
    c_in = sem("c_in")
    mem_in = sem("mem_in")
    w_in_ready = [sem(f"w_ready{i}") for i in range(3)]
    wbr_in = sem("wbr_in")
    xr_in = [sem(f"xr_in{i}") for i in range(2)]
    sq_done = sem("sq_done")
    rs_done = sem("rs_done")
    n_ready = sem("n_ready")
    main_full, main_out = sem("main_full"), sem("main_out")
    misc_full, misc_out = sem("misc_full"), sem("misc_out")
    p_full, p_out = sem("p_full"), sem("p_out")
    bu_full, bu_out = sem("bu_full"), sem("bu_out")
    y_full = sem("y_full")
    xst_ready = sem("xst_ready")
    half_ready = sem("half_ready")
    bb_ready = sem("bb_ready")
    cneg_ready = sem("cneg_ready")
    ydu_ready = sem("ydu_ready")
    gelu_ready = sem("gelu_ready")
    exp_ready = sem("exp_ready")
    gsig_ready = sem("gsig_ready")
    lam_ready = sem("lam_ready")
    ang_ready = sem("ang_ready")
    rope_ready = sem("rope_ready")
    rot_done = sem("rot_done")
    kdec_done = sem("kdec_done")
    vgate_done = sem("vgate_done")
    ret_done = sem("ret_done")
    retraw_done = sem("retraw_done")
    sg_ready = sem("sg_ready")
    glu_tanh = sem("glu_tanh")
    merged_done = sem("merged_done")
    dchain, pchain, achain = sem("dve_step"), sem("pool_step"), sem("act_step")

    loads = [("mem", None, ("mv", 1)), ("z", None, ("z", 3, 1)),
             ("qk", 0, ("qk", 0, TB - 1)), ("vg", 0, ("vg", 0, TB - 1)),
             ("qk", 1, ("qk", 1, TB - 1)), ("vg", 1, ("vg", 1, TB - 1))]
    loads += [("gate", (dh, br), ("gate", dh, br, TB - 1)) for dh in range(2) for br in range(3)]
    loads += [("out", dh, ("out", dh, TB - 1)) for dh in range(2)]
    load_no = {(k, a): n for n, (k, a, _) in enumerate(loads)}

    def weights(eng, kind, arg):
        n = load_no[(kind, arg)]
        eng.wait_ge(w_in_ready[n % 3], 16 * WCOUNT[n])
        return wring[n % 3]

    WCOUNT, per = [], [0, 0, 0]
    for n, (k, _, _) in enumerate(loads):
        per[n % 3] += 2 if k in ("qk", "vg") else 1
        WCOUNT.append(per[n % 3])

    def done_by_pe(eng, step):
        if step[0] in MAIN:
            eng.wait_ge(main_full, main_no[step] + 1)
        else:
            eng.wait_ge(misc_full, misc_no[step] + 1)

    SC = {"ct": 0, "ln": 1}
    block = ctx.enter_context(nc.Block())

    @block.sync
    def _(sp):
        sp.dma_start(con[:, :], ins["consts"]).then_inc(con_in, 16)
        for tb in range(TB):
            sp.dma_start(xs[:, tb, :], ins["x"][tb * P:(tb + 1) * P, :]).then_inc(x_in[tb], 16)
        w_in = ins["w_in"].rearrange("(k p) n -> p k n", p=P)
        w_out = ins["w_out"].rearrange("(k p) n -> p k n", p=P)

        def load(n):
            kind, arg, _ = loads[n]
            if n >= 3:
                done_by_pe(sp, loads[n - 3][2])
            buf, ready = wring[n % 3], w_in_ready[n % 3]
            if kind == "mem":
                sp.dma_start(buf[:, :, :], ins["w_mem_kv"].rearrange("(k p) n -> p k n", p=P)).then_inc(ready, 16)
            elif kind == "z":
                sp.dma_start(buf[:, :, :], w_in[:, :, U0:U0 + HALF]).then_inc(ready, 16)
            elif kind in ("qk", "vg"):
                for i, base in enumerate((Q0, K0) if kind == "qk" else (V0, G0)):
                    sp.dma_start(buf[:, :, 256 * i:256 * i + 256],
                                 w_in[:, :, base + 256 * arg:base + 256 * arg + 256]).then_inc(ready, 16)
            elif kind == "gate":
                dh, br = arg
                col = GATE0 + (1, 2, 0)[br] * D + dh * HALF
                sp.dma_start(buf[:, :, :], w_in[:, :, col:col + HALF]).then_inc(ready, 16)
            else:
                sp.dma_start(buf[:, :, :], w_out[:, :, arg * HALF:(arg + 1) * HALF]).then_inc(ready, 16)

        for n in range(6):
            if n == 2:
                sp.wait_ge(sq_done, TB + 2)
            load(n)
        done_by_pe(sp, ("glu", 1))
        done_by_pe(sp, ("ascore", TB - 1, 1))
        sp.wait_ge(rot_done, 2 * TB)
        kt = 0
        for name, rows in (("w_branch_ret", 4), ("w_branch_s5", 2), ("w_branch_mem", 2)):
            sp.dma_start(wbr[:, kt:kt + rows, :], ins[name].rearrange("(k p) n -> p k n", p=P)).then_inc(wbr_in, 16)
            kt += rows
        for n in range(6, len(loads)):
            load(n)
        for n in range(2 * TB):
            dh, tb = divmod(n, TB)
            if n >= 2:
                sp.wait_ge(misc_out, misc_no[("out", *divmod(n - 2, TB))] + 1)
            sp.dma_start(xr[:, n % 2, :],
                         ins["x"][tb * P:(tb + 1) * P, dh * HALF:(dh + 1) * HALF]).then_inc(xr_in[n % 2], 16)

    (S_ARE, S_AIM, S_LDT, S_DT, S_MAG, S_TH, S_COS, S_SIN, S_LRE, S_LIM, S_DEN, S_CR, S_CI,
     S_T0, S_T1, S_T2, S_T3, S_D, S_POS, S_CN, S_SN, S_POSI) = range(22)

    @block.gpsimd
    def _(pool):
        for k, name in ((S_ARE, "s5_a_re"), (S_AIM, "s5_a_im"), (S_LDT, "s5_log_dt"), (S_D, "s5_d")):
            n = ins[name].shape[1]
            pool.dma_start(small[:, k, 0:n], ins[name]).then_inc(par_in, 16)
        pool.dma_start(small[:, S_POSI, :].bitcast(I32), ins["positions"]).then_inc(par_in, 16)
        for k, name in enumerate(("norm_mix", "norm_mem")):
            pool.dma_start(gains[:, k, :], ins[name]).then_inc(par_in, 16)
        pool.dma_start(mem_x[:, :, :], ins["mem"].rearrange("(b p) n -> p b n", p=P)).then_inc(mem_in, 16)
        for k, name in enumerate(("s5_b_re", "s5_b_im")):
            pool.dma_start(bsrc[:, k, :, :], ins[name]).then_inc(b_in, 16)
        for k, name in enumerate(("s5_c_re", "s5_c_im")):
            pool.dma_start(cT[:, k, :, :], ins[name]).then_inc(c_in, 16)
        pool.dma_start(wglu[:, :, :], ins["s5_w_glu"].rearrange("(k p) n -> p k n", p=P)).then_inc(c_in, 16)
        chain = 0

        def link(i):
            nonlocal chain
            i.then_inc(pchain, 1)
            chain += 1
            pool.wait_ge(pchain, chain)

        link(pool.memset(stat[:, 32:48], -0.5))
        for n in range(TB + 2):
            pool.wait_ge(sq_done, n + 1)
            link(pool.tensor_scalar(stat[:, n:n + 1], stat[:, n:n + 1], 1.0 / D, EPS, ALU.mult, ALU.add))
            pool.tensor_tensor(stat[:, 16 + n:17 + n], stat[:, n:n + 1], stat[:, 32:33], ALU.pow).then_inc(rs_done, 1)
        pool.wait_ge(rope_ready, 2)

        def rotate(hp, tb):
            n = turn_no[(hp, tb)]
            pool.wait_ge(main_out, main_no[("qk", hp, tb)] + 1)
            if n >= 1:
                php, ptb = divmod(n - 1, TB)
                done_by_pe(pool, ("turn", php, ptb))
            src = qk[:, n % 2, :].rearrange("p (h c d) -> p h c d", h=4, c=2)
            dst = qkr[:, :].rearrange("p (h c d) -> p h c d", h=4, c=2)
            cos = rope[:, 0, tb, :].unsqueeze(1).to_broadcast([P, 4, 64])
            sin = rope[:, 1, tb, :].unsqueeze(1).to_broadcast([P, 4, 64])
            t = [rt[:, i, :].rearrange("p (h d) -> p h d", h=4) for i in range(4)]
            pool.tensor_tensor(t[0], src[:, :, 0, :], cos, ALU.mult)
            pool.tensor_tensor(t[1], src[:, :, 1, :], sin, ALU.mult)
            pool.tensor_tensor(t[2], src[:, :, 0, :], sin, ALU.mult)
            link(pool.tensor_tensor(t[3], src[:, :, 1, :], cos, ALU.mult))
            pool.tensor_tensor(dst[:, :, 0, :], t[0], t[1], ALU.subtract)
            pool.tensor_tensor(dst[:, :, 1, :], t[2], t[3], ALU.add).then_inc(rot_done, 1)
            pool.wait_ge(rot_done, n + 1)
            if n >= 2:
                done_by_pe(pool, ("mix", *divmod(n - 2, TB)))
            kf = con[:, C_KF + 2 * hp:C_KF + 2 * hp + 2].unsqueeze(2).to_broadcast([P, 2, P])
            pool.tensor_tensor(kdec[:, n % 2, :].rearrange("p (h d) -> p h d", h=2),
                               qkr[:, 256:512].rearrange("p (h d) -> p h d", h=2), kf,
                               ALU.mult).then_inc(kdec_done, 1)

        def gate_value(hp, tb):
            n = turn_no[(hp, tb)]
            pool.wait_ge(gsig_ready, n + 1)
            pool.wait_ge(main_out, main_no[("vg", hp, tb)] + 1)
            th = sg[:, n % 2, 0:256]
            link(pool.tensor_scalar(th, th, 1.0, 0.5, ALU.add, ALU.mult))
            g = vg[:, n % 3, 256:512]
            pool.tensor_tensor(g, g, th, ALU.mult).then_inc(vgate_done, 1)

        def normed(hp, tb):
            n = turn_no[(hp, tb)]
            pool.wait_ge(retraw_done, n + 1)
            s2, s3 = stat[:, 48:50], stat[:, 50:52]
            link(pool.tensor_scalar(s2, s2, 1.0 / RD, EPS, ALU.mult, ALU.add))
            link(pool.tensor_tensor(s3, s2, stat[:, 32:34], ALU.pow))
            g = vg[:, n % 3, 256:512]
            link(pool.tensor_tensor(g.rearrange("p (h d) -> p h d", h=2), g.rearrange("p (h d) -> p h d", h=2),
                                    s3.unsqueeze(2).to_broadcast([P, 2, P]), ALU.mult))
            pool.tensor_tensor(ret[:, :], ret[:, :], g, ALU.mult).then_inc(ret_done, 1)

        for s in steps:
            if s[0] == "qk":
                rotate(s[1], s[2])
            if s[0] == "vg":
                gate_value(s[1], s[2])
            if s[0] == "mix":
                normed(s[1], s[2])
            if s[0] == "gate" and s[2] > 0:
                _, dh, br, tb = s
                n = gate_no[s]
                pool.wait_ge(p_out, n + 1)
                pool.tensor_tensor(merged[:, tb, :], merged[:, tb, :], gp[:, n % 2, :], ALU.add).then_inc(merged_done, 1)

    @block.scalar
    def _(act):
        chain = 0

        def link(i):
            nonlocal chain
            i.then_inc(achain, 1)
            chain += 1
            act.wait_ge(achain, chain)

        def squares(n, src):
            junk = prod_x[:, n % 2, :]
            act.activation(junk, src, ACT.Square, accum_out=stat[:, n:n + 1]).then_inc(sq_done, 1)

        prod_x = wring[2][:, 0:4, :].rearrange("p (a b) n -> p a (b n)", a=2)
        for tb in range(TB):
            act.wait_ge(x_in[tb], 16)
            if tb >= 2:
                act.wait_ge(sq_done, tb - 1)
            squares(tb, xs[:, tb, :])
        act.wait_ge(mem_in, 16)
        for m in range(2):
            act.wait_ge(sq_done, TB + m - 1)
            squares(TB + m, mem_x[:, m, :])
        act.wait_ge(par_in, 16 * 7)
        sm = lambda k: small[:, k, :]
        act.activation(sm(S_DT), sm(S_LDT), ACT.Exp).then_inc(lam_ready, 1)
        act.wait_ge(ang_ready, 1)
        act.activation(sm(S_MAG), sm(S_T0), ACT.Exp).then_inc(lam_ready, 1)
        act.wait_ge(ang_ready, 2)
        act.activation(sm(S_SIN), sm(S_T1), ACT.Sin).then_inc(lam_ready, 1)
        act.activation(sm(S_COS), sm(S_T2), ACT.Sin).then_inc(lam_ready, 1)
        act.wait_ge(rope_ready, 1)
        act.activation(rope[:, :, :, :], rope[:, :, :, :], ACT.Sin).then_inc(rope_ready, 1)

        for s in steps:
            if s[0] in MAIN:
                m = main_no[s]
                act.wait_ge(main_full, m + 1)
                src = main_ps[m % 2][:, :]
            if s[0] == "z":
                _, ct, hf = s
                act.activation(zT[:, ct, hf * HALF:(hf + 1) * HALF], src, ACT.Copy).then_inc(main_out, 1)
            elif s[0] == "qk":
                n = turn_no[(s[1], s[2])]
                if n >= 2:
                    act.wait_ge(rot_done, n - 1)
                act.activation(qk[:, n % 2, :], src, ACT.Copy).then_inc(main_out, 1)
            elif s[0] == "vg":
                n = turn_no[(s[1], s[2])]
                if n >= 3:
                    done_by_pe(act, ("mix", *divmod(n - 3, TB)))
                    act.wait_ge(ret_done, n - 2)
                if n >= 2:
                    act.wait_ge(vgate_done, n - 1)
                act.activation(sg[:, n % 2, 0:256], src[:, 256:512], ACT.Tanh, scale=0.5).then_inc(gsig_ready, 1)
                act.activation(vg[:, n % 3, :], src, ACT.Copy).then_inc(main_out, 1)
            elif s[0] == "gate":
                n = gate_no[s]
                if n >= 2:
                    act.wait_ge(p_out, n - 1)
                else:
                    act.wait_ge(vgate_done, 2 * TB)
                act.activation(sg[:, n % 2, :], src, ACT.Tanh, scale=0.5).then_inc(main_out, 1)
            elif s[0] == "ascore":
                act.wait_ge(misc_out, misc_no[s] + 1)
                act.activation(psc[:, :], psc[:, :], ACT.Exp, scale=MD ** -0.5).then_inc(exp_ready, 1)
            elif s[0] == "y" and s[1] % 4 == 3:
                ct, hf = s[1] // 4, s[2]
                act.wait_ge(ydu_ready, 2 * ct + hf + 1)
                u = zT[:, ct, hf * HALF:(hf + 1) * HALF]
                act.activation(u, u, ACT.Gelu_apprx_tanh).then_inc(gelu_ready, 1)
            elif s[0] == "glu":
                hf = s[1]
                done_by_pe(act, s)
                for o, ps in enumerate((misc_ps[misc_no[s] % 2], bu_ps[1])):
                    act.activation(zT[:, o, hf * HALF:(hf + 1) * HALF], ps[:, :], ACT.Tanh, scale=0.5).then_inc(glu_tanh, 1)

    @block.tensor
    def _(pe):
        ident = con[:, C_ID:C_ID + P]

        def free(s):
            n = misc_no[s]
            if n >= 2:
                pe.wait_ge(misc_out, n - 1)
            return misc_ps[n % 2]

        def main_free(s):
            m = main_no[s]
            if m >= 2:
                pe.wait_ge(main_out, m - 1)
            return main_ps[m % 2]

        pe.wait_ge(con_in, 16)
        for s in steps:
            k = s[0]
            if k == "xturn":
                _, tb, kh = s
                ps = free(s)
                pe.wait_ge(n_ready, tb + 1)
                for i in range(4):
                    mm = pe.transpose(ps[:, i * P:(i + 1) * P], xs[:, tb, (4 * kh + i) * P:(4 * kh + i + 1) * P], ident)
                mm.then_inc(misc_full, 1)
            elif k == "mturn":
                _, mt, kh = s
                ps = free(s)
                pe.wait_ge(n_ready, TB + mt + 1)
                for i in range(4):
                    mm = pe.transpose(ps[:, i * P:(i + 1) * P], mem_x[:, mt, (4 * kh + i) * P:(4 * kh + i + 1) * P], ident)
                mm.then_inc(misc_full, 1)
            elif k == "bturn":
                ps = free(s)
                pe.wait_ge(bb_ready, 1)
                for i in range(4):
                    mm = pe.transpose(ps[:, i * P:(i + 1) * P], bbuf[:, i // 2, s[1] + i % 2, :], ident)
                mm.then_inc(misc_full, 1)
            elif k == "z":
                _, ct, hf = s
                w = weights(pe, "z", None)
                ps = main_free(s)
                pe.wait_ge(misc_out, misc_no[("xturn", 4 * hf + 3, 1)] + 1)
                for kd in range(KD):
                    mm = pe.matmul(ps[:, :], w[:, kd, ct * P:(ct + 1) * P], nT[:, kd, hf * HALF:(hf + 1) * HALF],
                                   start=kd == 0, stop=kd == KD - 1)
                mm.then_inc(main_full, 1)
            elif k in ("qk", "vg"):
                _, hp, tb = s
                w = weights(pe, k, hp)
                ps = main_free(s)
                for kd in range(KD):
                    mm = pe.matmul(ps[:, :], nT[:, kd, tb * P:(tb + 1) * P], w[:, kd, :],
                                   start=kd == 0, stop=kd == KD - 1)
                mm.then_inc(main_full, 1)
            elif k == "mk":
                w = weights(pe, "mem", None)
                ps = free(s)
                pe.wait_ge(misc_out, misc_no[("mturn", 1, 1)] + 1)
                for kd in range(KD):
                    mm = pe.matmul(ps[:, 0:MEM], w[:, kd, s[1] * P:(s[1] + 1) * P], memT[:, kd, :],
                                   start=kd == 0, stop=kd == KD - 1)
                mm.then_inc(misc_full, 1)
            elif k == "mv":
                w = weights(pe, "mem", None)
                ps = free(s)
                for kd in range(KD):
                    mm = pe.matmul(ps[:, 0:256], memT[:, kd, s[1] * P:(s[1] + 1) * P], w[:, kd, 256:512],
                                   start=kd == 0, stop=kd == KD - 1)
                mm.then_inc(misc_full, 1)
            elif k == "turn":
                _, hp, tb = s
                ps = free(s)
                pe.wait_ge(rot_done, turn_no[(hp, tb)] + 1)
                for i in range(4):
                    mm = pe.transpose(ps[:, i * P:(i + 1) * P], qkr[:, i * P:(i + 1) * P], ident)
                mm.then_inc(misc_full, 1)
            elif k == "score":
                _, hp, tb = s
                n = turn_no[(hp, tb)]
                ps = free(s)
                pe.wait_ge(misc_out, misc_no[("turn", hp, tb)] + 1)
                for h in range(2):
                    mm = pe.matmul(ps[:, h * P:(h + 1) * P], qkT[:, n % 2, 256 + h * P:256 + (h + 1) * P],
                                   qkT[:, n % 2, h * P:(h + 1) * P], start=True, stop=True)
                mm.then_inc(misc_full, 1)
            elif k == "mix":
                _, hp, tb = s
                n = turn_no[(hp, tb)]
                ps = free(s)
                pe.wait_ge(misc_out, misc_no[("score", hp, tb)] + 1)
                pe.wait_ge(kdec_done, n + 1)
                pe.wait_ge(main_out, main_no[("vg", hp, tb)] + 1)
                for h in range(2):
                    v = vg[:, n % 3, h * P:(h + 1) * P]
                    pe.matmul(ps[:, h * P:(h + 1) * P], sT[:, h * P:(h + 1) * P], v, start=True, stop=tb == 0)
                    if tb:
                        pe.matmul(ps[:, h * P:(h + 1) * P], qkT[:, n % 2, h * P:(h + 1) * P],
                                  state[:, 2 * hp + h, :], start=False, stop=True)
                    mm = pe.matmul(ps[:, 256 + h * P:256 + (h + 1) * P], kdec[:, n % 2, h * P:(h + 1) * P], v,
                                   start=True, stop=True)
                mm.then_inc(misc_full, 1)
            elif k == "flip":
                _, hp, tb = s
                ps = free(s)
                pe.wait_ge(ret_done, turn_no[(hp, tb)] + 1)
                for h in range(2):
                    mm = pe.transpose(ps[:, h * P:(h + 1) * P], ret[:, h * P:(h + 1) * P], ident)
                mm.then_inc(misc_full, 1)
            elif k == "ascore":
                _, tb, mp = s
                ps = free(s)
                pe.wait_ge(main_out, main_no[("z", 3, 1)] + 1)
                pe.wait_ge(misc_out, misc_no[("mv", 1)] + 1)
                for h in range(2):
                    mm = pe.matmul(ps[:, h * MEM:(h + 1) * MEM],
                                   zT[:, 2 + mp, tb * P:(tb + 1) * P], kmT[:, mp, h, :], start=True, stop=True)
                mm.then_inc(misc_full, 1)
            elif k == "aturn":
                _, tb, mp = s
                ps = free(s)
                pe.wait_ge(exp_ready, chain_no[(tb, mp)] + 1)
                for i in range(4):
                    mm = pe.transpose(ps[:, i * P:(i + 1) * P], psc[:, i * P:(i + 1) * P], ident)
                mm.then_inc(misc_full, 1)
            elif k == "amix":
                _, tb, mp = s
                ps = free(s)
                pe.wait_ge(misc_out, misc_no[("aturn", tb, mp)] + 1)
                for h in range(2):
                    for mt in range(2):
                        mm = pe.matmul(ps[:, h * MD:(h + 1) * MD], pT[:, (2 * h + mt) * P:(2 * h + mt + 1) * P],
                                       vm[:, mt, (2 * mp + h) * MD:(2 * mp + h + 1) * MD],
                                       start=mt == 0, stop=mt == 1)
                mm.then_inc(misc_full, 1)
            elif k == "aflip":
                _, tb, mp = s
                ps = free(s)
                pe.wait_ge(misc_out, misc_no[("amix", tb, mp)] + 1)
                pe.transpose(ps[:, 0:P], mo[:, :], ident).then_inc(misc_full, 1)
            elif k == "bu":
                _, st, hf = s
                n = bu_no[s]
                if n:
                    pe.wait_ge(bu_out, n)
                pe.wait_ge(misc_out, misc_no[("bturn", 6)] + 1)
                pe.wait_ge(main_out, main_no[("z", 1, 1)] + 1)
                for c in range(2):
                    mm = pe.matmul(bu_ps[c][:, :], bbT[:, c, st, :], zT[:, st // 4, hf * HALF:(hf + 1) * HALF],
                                   start=True, stop=True)
                mm.then_inc(bu_full, 1)
            elif k == "y":
                _, st, hf = s
                pe.wait_ge(xst_ready, 2 * st + hf + 1)
                pe.wait_ge(cneg_ready, 1)
                if st == 4:
                    pe.wait_ge(ydu_ready, hf + 1)
                for c in range(2):
                    mm = pe.matmul(y_ps[hf][:, :], cT[:, c, st, :], ysc[:, hf, c, :],
                                   start=st % 4 == 0 and c == 0, stop=st % 4 == 3 and c == 1)
                mm.then_inc(y_full, 1)
            elif k == "glu":
                hf = s[1]
                ps = free(s)
                pe.wait_ge(gelu_ready, 4)
                if hf:
                    pe.wait_ge(misc_out, misc_no[("glu", 0)] + 1)
                for bank, col in ((ps, 2), (bu_ps[1], 3), (bu_ps[0], 0), (y_ps[hf], 1)):
                    for c in range(2):
                        mm = pe.matmul(bank[:, :], wglu[:, c, col * P:(col + 1) * P],
                                       zT[:, c, hf * HALF:(hf + 1) * HALF], start=c == 0, stop=c == 1)
                mm.then_inc(misc_full, 1)
            elif k == "gate":
                _, dh, br, tb = s
                n = gate_no[s]
                w = weights(pe, "gate", (dh, br))
                ps = main_free(s)
                for kd in range(KD):
                    mm = pe.matmul(ps[:, :], nT[:, kd, tb * P:(tb + 1) * P], w[:, kd, :],
                                   start=kd == 0, stop=kd == KD - 1)
                mm.then_inc(main_full, 1)
                pe.wait_ge(wbr_in, 48)
                if n >= 2:
                    pe.wait_ge(p_out, n - 1)
                src, first, rows = ((zT[:, 0:2, :], 4, 2), (zT[:, 2:4, :], 6, 2), (retT, 0, 4))[br]
                if tb == 0 and dh == 0:
                    last = (("glu", 1), ("aflip", TB - 1, 1), ("flip", 1, TB - 1))[br]
                    pe.wait_ge(misc_out, misc_no[last] + 1)
                for i in range(rows):
                    mm = pe.matmul(p_ps[n % 2][:, :], src[:, i, tb * P:(tb + 1) * P],
                                   wbr[:, first + i, dh * HALF:(dh + 1) * HALF], start=i == 0, stop=i == rows - 1)
                mm.then_inc(p_full, 1)
            elif k == "gturn":
                _, dh, tb = s
                ps = free(s)
                pe.wait_ge(merged_done, dh * 2 * TB + TB + tb + 1)
                for i in range(4):
                    mm = pe.transpose(ps[:, i * P:(i + 1) * P], merged[:, tb, i * P:(i + 1) * P], ident)
                mm.then_inc(misc_full, 1)
            elif k == "out":
                _, dh, tb = s
                w = weights(pe, "out", dh)
                ps = free(s)
                pe.wait_ge(misc_out, misc_no[("gturn", 1, TB - 1)] + 1)
                for kd in range(KD):
                    src = merT_lo if kd < 4 else merT_hi
                    mm = pe.matmul(ps[:, :], src[:, kd % 4, tb * P:(tb + 1) * P], w[:, kd, :],
                                   start=kd == 0, stop=kd == KD - 1)
                mm.then_inc(misc_full, 1)


    @block.vector
    def _(dve):
        chain = 0

        def link(i):
            nonlocal chain
            i.then_inc(dchain, 1)
            chain += 1
            dve.wait_ge(dchain, chain)

        sm = lambda k: small[:, k, :]
        tt, ts, stt = dve.tensor_tensor, dve.tensor_scalar, dve.scalar_tensor_tensor

        def reduced(dst_sin, dst_cos, ang, tmp):
            link(ts(tmp, ang, 1.0 / (2.0 * math.pi), MAGIC, ALU.mult, ALU.add))
            link(ts(tmp, tmp, -MAGIC, None, ALU.add))
            link(stt(dst_sin, tmp, -TWO_PI_HI, ang, ALU.mult, ALU.add))
            link(stt(dst_sin, tmp, -TWO_PI_MID, dst_sin, ALU.mult, ALU.add))
            link(stt(dst_sin, tmp, -TWO_PI_LO, dst_sin, ALU.mult, ALU.add))
            link(ts(dst_sin, dst_sin, PI_BELOW, -PI_BELOW, ALU.min, ALU.max))
            link(stt(dst_cos, dst_sin, -1.0, dst_sin, ALU.mult, ALU.max))
            return ts(dst_cos, dst_cos, -1.0, math.pi / 2, ALU.mult, ALU.add)

        for n in range(TB):
            dve.wait_ge(rs_done, n + 1)
            ts(xs[:, n, :], xs[:, n, :], stat[:, 16 + n:17 + n], None, ALU.mult).then_inc(n_ready, 1)
        for m in range(2):
            dve.wait_ge(rs_done, TB + m + 1)
            ts(mem_x[:, m, :], mem_x[:, m, :], stat[:, 24 + m:25 + m], None, ALU.mult).then_inc(n_ready, 1)

        dve.wait_ge(par_in, 16 * 7)
        dve.wait_ge(con_in, 16)
        for s in [s for s in steps if s[0] in ("xturn", "mturn")]:
            n = misc_no[s]
            dve.wait_ge(misc_full, n + 1)
            _, b, kh = s
            dst = (nT if s[0] == "xturn" else memT)[:, 4 * kh:4 * kh + 4, b * P:(b + 1) * P]
            g = gains[:, 0 if s[0] == "xturn" else 1, 4 * kh:4 * kh + 4].unsqueeze(2).to_broadcast([P, 4, P])
            tt(dst, misc_ps[n % 2][:, :].rearrange("p (k t) -> p k t", k=4), g, ALU.mult).then_inc(misc_out, 1)

        dve.wait_ge(lam_ready, 1)
        tt(sm(S_T0), sm(S_ARE), sm(S_DT), ALU.mult).then_inc(ang_ready, 1)
        link(tt(sm(S_TH), sm(S_AIM), sm(S_DT), ALU.mult))
        reduced(sm(S_T1), sm(S_T2), sm(S_TH), sm(S_T3)).then_inc(ang_ready, 1)
        link(dve.tensor_copy(sm(S_POS), sm(S_POSI).bitcast(I32)))
        ang = prod[:, 0, :].rearrange("p (b f) -> p b f", b=TB)
        tmp = prod[:, 1, :].rearrange("p (b f) -> p b f", b=TB)
        inv = con[:, C_INV:C_INV + 64].unsqueeze(1).to_broadcast([P, TB, 64])
        pos = sm(S_POS).unsqueeze(2).to_broadcast([P, TB, 64])
        link(tt(ang, pos, inv, ALU.mult))
        reduced(rope[:, 1, :, :], rope[:, 0, :, :], ang, tmp).then_inc(rope_ready, 1)
        dve.wait_ge(lam_ready, 4)
        link(tt(sm(S_LRE), sm(S_MAG), sm(S_COS), ALU.mult))
        link(tt(sm(S_LIM), sm(S_MAG), sm(S_SIN), ALU.mult))
        link(ts(sm(S_LRE), sm(S_LRE), -1.0, None, ALU.add))
        link(tt(sm(S_T0), sm(S_ARE), sm(S_ARE), ALU.mult))
        link(tt(sm(S_T3), sm(S_AIM), sm(S_AIM), ALU.mult))
        link(tt(sm(S_DEN), sm(S_T0), sm(S_T3), ALU.add))
        link(dve.reciprocal(sm(S_DEN), sm(S_DEN)))
        link(tt(sm(S_T0), sm(S_LRE), sm(S_ARE), ALU.mult))
        link(tt(sm(S_T3), sm(S_LIM), sm(S_AIM), ALU.mult))
        link(tt(sm(S_T0), sm(S_T0), sm(S_T3), ALU.add))
        link(tt(sm(S_CR), sm(S_T0), sm(S_DEN), ALU.mult))
        link(tt(sm(S_T0), sm(S_LIM), sm(S_ARE), ALU.mult))
        link(tt(sm(S_T3), sm(S_LRE), sm(S_AIM), ALU.mult))
        link(tt(sm(S_T0), sm(S_T0), sm(S_T3), ALU.subtract))
        link(tt(sm(S_CI), sm(S_T0), sm(S_DEN), ALU.mult))
        dve.wait_ge(b_in, 32)
        cr = sm(S_CR).unsqueeze(2).to_broadcast([P, S5T, P])
        ci = sm(S_CI).unsqueeze(2).to_broadcast([P, S5T, P])
        big = wbig[:, :, :]
        tt(bbuf[:, 0, :, :], bsrc[:, 0, :, :], cr, ALU.mult)
        link(tt(big, bsrc[:, 1, :, :], ci, ALU.mult))
        link(tt(bbuf[:, 0, :, :], bbuf[:, 0, :, :], big, ALU.subtract))
        tt(bbuf[:, 1, :, :], bsrc[:, 1, :, :], cr, ALU.mult)
        link(tt(big, bsrc[:, 0, :, :], ci, ALU.mult))
        tt(bbuf[:, 1, :, :], bbuf[:, 1, :, :], big, ALU.add).then_inc(bb_ready, 1)
        dve.wait_ge(c_in, 48)
        ts(cT[:, 1, :, :], cT[:, 1, :, :], -1.0, None, ALU.mult).then_inc(cneg_ready, 1)

        def tables(st):
            if st:
                dve.wait_ge(xst_ready, 2 * st)
            cn, sn, t2 = small[:, S_CN, 0:1], small[:, S_SN, 0:1], small[:, S_T0, 0:2]
            c, sn_t = tab[:, 0, :], tab[:, 1, :]
            dve.memset(c[:, 0:1], 1.0)
            dve.memset(sn_t[:, 0:1], 0.0)
            dve.tensor_copy(cn, small[:, S_COS, st:st + 1])
            link(dve.tensor_copy(sn, small[:, S_SIN, st:st + 1]))
            n = 1
            while n < SEQ:
                tmp_c, tmp_s = prod[:, 0, 0:n], prod[:, 1, 0:n]
                ts(tmp_c, sn_t[:, 0:n], sn, None, ALU.mult)
                link(ts(tmp_s, c[:, 0:n], sn, None, ALU.mult))
                stt(c[:, n:2 * n], c[:, 0:n], cn, tmp_c, ALU.mult, ALU.subtract)
                link(stt(sn_t[:, n:2 * n], sn_t[:, 0:n], cn, tmp_s, ALU.mult, ALU.add))
                if 2 * n < SEQ:
                    tt(t2[:, 0:1], sn, sn, ALU.mult)
                    link(tt(t2[:, 1:2], cn, sn, ALU.mult))
                    link(stt(cn, cn, cn, t2[:, 0:1], ALU.mult, ALU.subtract))
                    link(ts(sn, t2[:, 1:2], 2.0, None, ALU.mult))
                n *= 2

        def copy_out(s, dst, cols=HALF):
            n = misc_no[s]
            dve.wait_ge(misc_full, n + 1)
            dve.tensor_copy(dst, misc_ps[n % 2][:, 0:cols]).then_inc(misc_out, 1)

        for s in steps:
            k = s[0]
            if k == "bturn":
                n = misc_no[s]
                dve.wait_ge(misc_full, n + 1)
                dve.tensor_copy(bbT[:, :, s[1]:s[1] + 2, :],
                                misc_ps[n % 2][:, :].rearrange("p (c s q) -> p c s q", c=2, s=2)).then_inc(misc_out, 1)
            elif k == "mk":
                n = misc_no[s]
                link(dve.memset(kmT[:, s[1], :, :], 0.0))
                dve.wait_ge(misc_full, n + 1)
                for h in range(2):
                    rows = slice(h * MD, (h + 1) * MD)
                    i = dve.tensor_copy(kmT[rows, s[1], h, :], misc_ps[n % 2][rows, 0:MEM])
                i.then_inc(misc_out, 1)
            elif k == "mv":
                copy_out(s, vm[:, s[1], :], 256)
            elif k == "turn":
                _, hp, tb = s
                n = turn_no[(hp, tb)]
                if n >= 2:
                    done_by_pe(dve, ("mix", *divmod(n - 2, TB)))
                if n == 0:
                    done_by_pe(dve, ("bturn", 6))
                copy_out(s, qkT[:, n % 2, :])
            elif k == "score":
                _, hp, tb = s
                n = turn_no[(hp, tb)]
                if n:
                    done_by_pe(dve, ("mix", *divmod(n - 1, TB)))
                dve.wait_ge(misc_full, misc_no[s] + 1)
                dec = con[:, C_DEC + 2 * hp * P:C_DEC + (2 * hp + 2) * P]
                tt(sT[:, :], misc_ps[misc_no[s] % 2][:, 0:256], dec, ALU.mult).then_inc(misc_out, 1)
            elif k == "mix":
                _, hp, tb = s
                n = turn_no[(hp, tb)]
                if n:
                    done_by_pe(dve, ("flip", *divmod(n - 1, TB)))
                dve.wait_ge(misc_full, misc_no[s] + 1)
                ps = misc_ps[misc_no[s] % 2]
                qf = con[:, C_QF + 2 * hp:C_QF + 2 * hp + 2].unsqueeze(2).to_broadcast([P, 2, P])
                tt(ret[:, :].rearrange("p (h d) -> p h d", h=2), ps[:, 0:256].rearrange("p (h d) -> p h d", h=2), qf,
                   ALU.mult)
                for h in range(2):
                    kv, st = ps[:, 256 + h * P:256 + (h + 1) * P], state[:, 2 * hp + h, :]
                    if tb == 0:
                        i = dve.tensor_copy(st, kv)
                    else:
                        i = stt(st, st, GAMMA[2 * hp + h] ** P, kv, ALU.mult, ALU.add)
                i.then_inc(misc_out, 1)
                dve.wait_ge(misc_out, misc_no[s] + 1)
                link(tt(rsq[:, :], ret[:, :], ret[:, :], ALU.mult))
                dve.tensor_reduce(stat[:, 48:50], rsq[:, :].rearrange("p (h d) -> p h d", h=2), AX.X,
                                  ALU.add).then_inc(retraw_done, 1)
            elif k == "flip":
                _, hp, tb = s
                n = misc_no[s]
                dve.wait_ge(misc_full, n + 1)
                dve.tensor_copy(retT[:, 2 * hp:2 * hp + 2, tb * P:(tb + 1) * P],
                                misc_ps[n % 2][:, 0:256].rearrange("p (h t) -> p h t", h=2)).then_inc(misc_out, 1)
            elif k == "ascore":
                _, tb, mp = s
                c = chain_no[(tb, mp)]
                dve.wait_ge(misc_full, misc_no[s] + 1)
                ps = misc_ps[misc_no[s] % 2][:, :].rearrange("p (h m) -> p h m", h=2)
                link(dve.tensor_reduce(stat[:, 52:54], ps, AX.X, ALU.max))
                tt(psc[:, :].rearrange("p (h m) -> p h m", h=2), ps,
                   stat[:, 52:54].unsqueeze(2).to_broadcast([P, 2, MEM]), ALU.subtract).then_inc(misc_out, 1)
            elif k == "aturn":
                _, tb, mp = s
                dve.wait_ge(exp_ready, chain_no[(tb, mp)] + 1)
                link(dve.tensor_reduce(stat[:, 54:56], psc[:, :].rearrange("p (h m) -> p h m", h=2), AX.X, ALU.add))
                link(dve.reciprocal(stat[:, 56:58], stat[:, 54:56]))
                copy_out(s, pT[:, :])
            elif k == "amix":
                n = misc_no[s]
                dve.wait_ge(misc_full, n + 1)
                tt(mo[:, :].rearrange("p (h d) -> p h d", h=2), misc_ps[n % 2][:, 0:P].rearrange("p (h d) -> p h d", h=2),
                   stat[:, 56:58].unsqueeze(2).to_broadcast([P, 2, MD]), ALU.mult).then_inc(misc_out, 1)
            elif k == "aflip":
                _, tb, mp = s
                copy_out(s, zT[:, 2 + mp, tb * P:(tb + 1) * P], P)
            elif k == "bu":
                _, st, hf = s
                if hf == 0:
                    tables(st)
                n = bu_no[s]
                c, sn_t = tab[:, 0, hf * HALF:(hf + 1) * HALF], tab[:, 1, hf * HALF:(hf + 1) * HALF]
                dve.wait_ge(bu_full, n + 1)
                tt(prod[:, 0, :], bu_ps[0][:, :], c, ALU.mult)
                tt(prod[:, 1, :], bu_ps[1][:, :], sn_t, ALU.mult)
                tt(prod[:, 2, :], bu_ps[1][:, :], c, ALU.mult)
                tt(prod[:, 3, :], bu_ps[0][:, :], sn_t, ALU.mult).then_inc(bu_out, 1)
                dve.wait_ge(bu_out, n + 1)
                tt(prod[:, 0, :], prod[:, 0, :], prod[:, 1, :], ALU.add)
                link(tt(prod[:, 2, :], prod[:, 2, :], prod[:, 3, :], ALU.subtract))
                if st:
                    dve.wait_ge(y_full, 2 * (st - 1) + hf + 1)
                mag = small[:, S_MAG, st:st + 1].to_broadcast([P, HALF])
                for c2 in range(2):
                    init = 0.0 if hf == 0 else small[:, S_CN + c2, 1:2]
                    i = dve.tensor_tensor_scan(ysc[:, hf, c2, :], mag, prod[:, 2 * c2, :], init, ALU.mult, ALU.add)
                link(i)
                if hf == 0:
                    for c2 in range(2):
                        dve.tensor_copy(small[:, S_CN + c2, 1:2], ysc[:, hf, c2, HALF - 1:HALF])
                tt(prod[:, 0, :], ysc[:, hf, 0, :], c, ALU.mult)
                tt(prod[:, 1, :], ysc[:, hf, 1, :], sn_t, ALU.mult)
                tt(prod[:, 2, :], ysc[:, hf, 0, :], sn_t, ALU.mult)
                link(tt(prod[:, 3, :], ysc[:, hf, 1, :], c, ALU.mult))
                link(tt(ysc[:, hf, 0, :], prod[:, 0, :], prod[:, 1, :], ALU.subtract))
                tt(ysc[:, hf, 1, :], prod[:, 2, :], prod[:, 3, :], ALU.add).then_inc(xst_ready, 1)
                dve.wait_ge(xst_ready, n + 1)
            elif k == "y" and s[1] % 4 == 3:
                ct, hf = s[1] // 4, s[2]
                dve.wait_ge(y_full, 2 * s[1] + hf + 1)
                u = zT[:, ct, hf * HALF:(hf + 1) * HALF]
                stt(u, u, small[:, S_D, ct:ct + 1], y_ps[hf][:, :], ALU.mult, ALU.add).then_inc(ydu_ready, 1)
            elif k == "glu":
                hf = s[1]
                dve.wait_ge(glu_tanh, 2 * hf + 2)
                done_by_pe(dve, s)
                both = zT[:, 0:2, hf * HALF:(hf + 1) * HALF]
                link(ts(both, both, 1.0, 0.5, ALU.add, ALU.mult))
                for o, bank in enumerate((bu_ps[0], y_ps[hf])):
                    d = zT[:, o, hf * HALF:(hf + 1) * HALF]
                    i = tt(d, d, bank[:, :], ALU.mult)
                i.then_inc(misc_out, 1)
            elif k == "gate":
                _, dh, br, tb = s
                n = gate_no[s]
                dve.wait_ge(p_full, n + 1)
                dve.wait_ge(main_out, main_no[s] + 1)
                if br == 0:
                    if dh:
                        done_by_pe(dve, ("gturn", 0, tb))
                    elif tb == 0:
                        done_by_pe(dve, ("glu", 1))
                    dst = merged[:, tb, :]
                else:
                    if (dh, br, tb) == (0, 1, 0):
                        done_by_pe(dve, ("flip", 1, TB - 1))
                        done_by_pe(dve, ("aflip", TB - 1, 1))
                    if n - TB * (dh + 1) >= 2:
                        dve.wait_ge(merged_done, n - TB * (dh + 1) - 1)
                    dst = gp[:, n % 2, :]
                i = stt(dst, sg[:, n % 2, :], 1.0, p_ps[n % 2][:, :], ALU.add, ALU.mult)
                i.then_inc(p_out, 1)
            elif k == "gturn":
                _, dh, tb = s
                n = misc_no[s]
                dve.wait_ge(misc_full, n + 1)
                dst = (merT_lo, merT_hi)[dh][:, :, tb * P:(tb + 1) * P]
                ts(dst, misc_ps[n % 2][:, :].rearrange("p (k t) -> p k t", k=4), 0.5, None, ALU.mult).then_inc(misc_out, 1)
            elif k == "out":
                _, dh, tb = s
                n = misc_no[s]
                j = dh * TB + tb
                dve.wait_ge(misc_full, n + 1)
                dve.wait_ge(xr_in[j % 2], 16 * (j // 2 + 1))
                tt(h_sb[:, tb, dh * HALF:(dh + 1) * HALF], misc_ps[n % 2][:, :], xr[:, j % 2, :],
                   ALU.add).then_inc(misc_out, 1)
    ctx.close()


PH, PK, NK = 8, 16, 128
HC = 2 * PH
PAIRS = [(0, 1, 16), (1, 1, 8), (2, 1, 5), (3, 1, 4), (4, 1, 3), (5, 3, 2), (8, 8, 1)]
NCAND = sum(na * nb for _, na, nb in PAIRS)
NEG = -3.0e38
CH = NK
GT = 16
WT = 64
CG = 4


def build_scores(nc, ins, h_sb, xh, xl, s_sb, mem_map):
    ctx = ExitStack()
    at = dict(mem_map)

    def sb(region, name, shape, dt=F32):
        size = int(np.prod(shape[1:])) * (2 if dt == BF16 else 4)
        off = at[region]
        at[region] = off + (size + 31) // 32 * 32
        assert at[region] <= mem_map[region] + mem_map[region + "_size"], (region, name)
        return nc.alloc_sbuf_tensor_at(name, shape, dt, offset=off)

    def sem(name):
        return ctx.enter_context(nc.semaphore(name))

    ident = sb("const", "ident2", [P, P])
    gain = sb("const", "gain2", [P, KD])
    stat = sb("const", "stat2", [P, 64])
    xnT = sb("xnt", "xnT", [P, KD, SEQ])
    wq = [sb("wq", f"wq{i}", [P, KD, 256]) for i in range(2)]
    keys = sb("keys", "keys", [P, HC, NK])
    qT = sb("qt", "qT", [P, 2, SEQ])
    xn = nc.alloc_sbuf_tensor_at("xn", [P, 2, D], F32, offset=mem_map["s"])
    junk = nc.alloc_sbuf_tensor_at("junk2", [P, 2, D], F32, offset=mem_map["s"] + 8192)
    main_ps = [ctx.enter_context(nc.psum_tensor(f"q_ps{i}", [P, HALF], F32)) for i in range(2)]
    misc_ps = [ctx.enter_context(nc.psum_tensor(f"t_ps{i}", [P, HALF], F32)) for i in range(2)]
    par_in, keys_in = sem("par2_in"), sem("keys_in")
    wq_in = [sem(f"wq_in{i}") for i in range(2)]
    sq_done, rs_done, xn_ready = sem("sq2_done"), sem("rs2_done"), sem("xn_ready")
    turned, turned_out = sem("turned"), sem("turned_out")
    hi_done, lo_done = sem("xh_done"), sem("xl_done")
    q_full, q_out = sem("q_full"), sem("q_out")
    s_full, s_out = sem("s_full"), sem("s_out")
    half_set, pstep = sem("half_set"), sem("pool_step2")
    turns = [(tb, kh) for tb in range(TB) for kh in range(2)]
    block = ctx.enter_context(nc.Block())

    @block.sync
    def _(sp):
        sp.dma_start(ident[:, :], ins["consts"][:, 0:P]).then_inc(par_in, 16)
        sp.dma_start(gain[:, :], ins["norm_ffn"]).then_inc(par_in, 16)
        w = ins["peer_w_q"].rearrange("(k p) n -> p k n", p=P)
        for n in range(HC // 2):
            if n >= 2:
                sp.wait_ge(q_full, 4 * (n - 1))
            sp.dma_start(wq[n % 2][:, :, :], w[:, :, n * 256:(n + 1) * 256]).then_inc(wq_in[n % 2], 16)
            if n == 0:
                sp.dma_start(keys[:, :, :], ins["peer_keys"]).then_inc(keys_in, 16)

    @block.gpsimd
    def _(pool):
        pool.memset(stat[:, 32:33], -0.5).then_inc(half_set, 1)
        pool.wait_ge(half_set, 1)
        for tb in range(TB):
            pool.wait_ge(sq_done, tb + 1)
            pool.tensor_scalar(stat[:, tb:tb + 1], stat[:, tb:tb + 1], 1.0 / D, EPS, ALU.mult, ALU.add).then_inc(pstep, 1)
            pool.wait_ge(pstep, tb + 1)
            pool.tensor_tensor(stat[:, 16 + tb:17 + tb], stat[:, tb:tb + 1], stat[:, 32:33], ALU.pow).then_inc(rs_done, 1)
        for n, (tb, kh) in enumerate(turns):
            pool.wait_ge(hi_done, n + 1)
            part = (slice(None), slice(4 * kh, 4 * kh + 4), slice(tb * P, (tb + 1) * P))
            pool.tensor_tensor(xl[part], xnT[part], xh[part], ALU.subtract).then_inc(lo_done, 1)

    @block.scalar
    def _(act):
        for tb in range(TB):
            if tb >= 2:
                act.wait_ge(sq_done, tb - 1)
            act.activation(junk[:, tb % 2, :], h_sb[:, tb, :], ACT.Square, accum_out=stat[:, tb:tb + 1]).then_inc(sq_done, 1)
        for n, (tb, kh) in enumerate(turns):
            act.wait_ge(turned_out, n + 1)
            part = (slice(None), slice(4 * kh, 4 * kh + 4), slice(tb * P, (tb + 1) * P))
            act.activation(xh[part], xnT[part], ACT.Copy).then_inc(hi_done, 1)
        for hc in range(HC):
            for hf in range(2):
                n = 2 * hc + hf
                act.wait_ge(q_full, n + 1)
                if hc >= 2:
                    act.wait_ge(s_full, 2 * (hc - 1))
                act.activation(qT[:, hc % 2, hf * HALF:(hf + 1) * HALF], main_ps[n % 2][:, :], ACT.Copy).then_inc(q_out, 1)

    @block.tensor
    def _(pe):
        pe.wait_ge(par_in, 32)
        for n, (tb, kh) in enumerate(turns):
            pe.wait_ge(xn_ready, tb + 1)
            if n >= 2:
                pe.wait_ge(turned_out, n - 1)
            for i in range(4):
                mm = pe.transpose(misc_ps[n % 2][:, i * P:(i + 1) * P],
                                  xn[:, tb % 2, (4 * kh + i) * P:(4 * kh + i + 1) * P], ident[:, :])
            mm.then_inc(turned, 1)

        def scores(hc):
            pe.wait_ge(keys_in, 16)
            for g in range(2):
                n = 2 * hc + g
                if n >= 2:
                    pe.wait_ge(s_out, n - 1)
                else:
                    pe.wait_ge(turned_out, 2 * TB)
                pe.wait_ge(q_out, 2 * hc + g + 1)
                for i in range(4):
                    tb = 4 * g + i
                    mm = pe.matmul(misc_ps[n % 2][:, i * P:(i + 1) * P], qT[:, hc % 2, tb * P:(tb + 1) * P],
                                   keys[:, hc, :], start=True, stop=True)
                mm.then_inc(s_full, 1)

        for hc in range(HC):
            for hf in range(2):
                n = 2 * hc + hf
                pe.wait_ge(wq_in[hc // 2 % 2], 16 * (hc // 4 + 1))
                pe.wait_ge(turned_out, 8 * hf + 8)
                if n >= 2:
                    pe.wait_ge(q_out, n - 1)
                for kd in range(KD):
                    mm = pe.matmul(main_ps[n % 2][:, :], wq[hc // 2 % 2][:, kd, (hc % 2) * P:(hc % 2 + 1) * P],
                                   xnT[:, kd, hf * HALF:(hf + 1) * HALF], start=kd == 0, stop=kd == KD - 1)
                mm.then_inc(q_full, 1)
            if hc:
                scores(hc - 1)
        scores(HC - 1)

    @block.vector
    def _(dve):
        dve.wait_ge(par_in, 32)

        def norm(tb):
            dve.wait_ge(rs_done, tb + 1)
            if tb >= 2:
                dve.wait_ge(turned, 2 * (tb - 1))
            dve.tensor_scalar(xn[:, tb % 2, :], h_sb[:, tb, :], stat[:, 16 + tb:17 + tb], None, ALU.mult).then_inc(xn_ready, 1)

        norm(0)
        for n, (tb, kh) in enumerate(turns):
            if kh == 0 and tb + 1 < TB:
                norm(tb + 1)
            dve.wait_ge(turned, n + 1)
            dve.tensor_tensor(xnT[:, 4 * kh:4 * kh + 4, tb * P:(tb + 1) * P],
                              misc_ps[n % 2][:, :].rearrange("p (k t) -> p k t", k=4),
                              gain[:, 4 * kh:4 * kh + 4].unsqueeze(2).to_broadcast([P, 4, P]),
                              ALU.mult).then_inc(turned_out, 1)
        for hc in range(HC):
            for g in range(2):
                n = 2 * hc + g
                dve.wait_ge(s_full, n + 1)
                dve.tensor_copy(s_sb[:, 4 * g:4 * g + 4, hc, :],
                                misc_ps[n % 2][:, :].rearrange("p (b n) -> p b n", b=4)).then_inc(s_out, 1)
    ctx.close()


def build_hidden(nc, ins, xh, xl, s_sb, g_dram, w_dram, mem_map):
    ctx = ExitStack()
    at = dict(mem_map)

    def sb(region, name, shape, dt=F32):
        size = int(np.prod(shape[1:])) * (2 if dt == BF16 else 4)
        off = at[region]
        at[region] = off + (size + 31) // 32 * 32
        assert at[region] <= mem_map[region] + mem_map[region + "_size"], (region, name)
        return nc.alloc_sbuf_tensor_at(name, shape, dt, offset=off)

    def sem(name):
        return ctx.enter_context(nc.semaphore(name))

    con = sb("const", "con3", [P, C_COLS - C_IOTA])
    ident = sb("const", "ident3", [P, P])
    iota = sb("const", "iota_bf", [P, P], BF16)
    iota50 = con[:, C_IOTA50 - C_IOTA:C_IOTA50 - C_IOTA + NCAND]
    u_in = [sb("u", f"u_in{i}", [P, KD, P]) for i in range(2)]
    u_hi = [sb("u", f"u_hi{i}", [P, KD, P], BF16) for i in range(2)]
    u_lo = [sb("u", f"u_lo{i}", [P, KD, P], BF16) for i in range(2)]
    g_out = [sb("g", f"g_out{i}", [P, SEQ]) for i in range(2)]
    codeT = sb("sel", "codeT", [P, SEQ])
    rowT = sb("sel", "rowT", [P, SEQ])
    wT = sb("sel", "wT", [P, SEQ])
    whT = sb("sel", "whT", [P, SEQ])
    sc = sb("hot", "sc", [P, HC, NK])
    top = sb("hot", "top", [P, HC, PK])
    topi = sb("hot", "topi", [P, HC, PK], U32)
    topf = sb("hot", "topf", [P, HC, PK])
    cand = sb("hot", "cand", [P, PH, NCAND])
    code = sb("hot", "code", [P, PH, NCAND])
    fin = sb("hot", "fin", [P, PH, PK])
    posi = sb("hot", "posi", [P, PH, PK], U32)
    posf = sb("hot", "posf", [P, PH, PK])
    wrow = sb("hot", "wrow", [P, PH, PK])
    crow = sb("hot", "crow", [P, PH, PK])
    wsum = sb("hot", "wsum", [P, 2, PH])
    match = sb("hot", "match", [P, 2, PK, NCAND])
    at["hot"] = mem_map["hot"]
    hot = [[sb("hot", f"hot_{n}{i}", [P, GT, P], BF16) for n in ("ihi", "ilo", "j")] for i in range(2)]
    wbuf = [nc.alloc_sbuf_tensor_at(f"wbuf{i}", [P, NK, WT], F32, offset=mem_map["s"] + i * NK * WT * 4) for i in range(2)]
    hid_ps = [ctx.enter_context(nc.psum_tensor(f"hid_ps{i}", [P, 2, HALF], F32)) for i in range(2)]
    w_ps = [ctx.enter_context(nc.psum_tensor(f"w_ps{i}", [P, HALF], F32)) for i in range(4)]

    one = sb("const", "one", [P, KD])
    par_in, iota_ready, one_ready = sem("par3_in"), sem("iota_ready"), sem("one_ready")
    u_loaded = [sem(f"u_loaded{i}") for i in range(2)]
    u_cast, u_ready = sem("u_cast"), sem("u_ready")
    hid_full, hid_out = sem("hid_full"), sem("hid_out")
    g_stored = [sem(f"g_stored{i}") for i in range(2)]
    w_stored = [sem(f"w_stored{i}") for i in range(2)]
    fin_ready, exp_ready = sem("fin_ready"), sem("fin_exp")
    sel_ready, sel_turned, sel_out = sem("sel_ready"), sem("sel_turned"), sem("sel_out")
    hot_ready, w_full, w_out = sem("hot_ready"), sem("w_full"), sem("w_out")
    step = sem("dve_step3")
    SEL = CH // 2 // TB
    block = ctx.enter_context(nc.Block())

    @block.sync
    def _(sp):
        sp.dma_start(con[:, :], ins["consts"][:, C_IOTA:C_COLS]).then_inc(par_in, 16)
        sp.dma_start(ident[:, :], ins["consts"][:, 0:P]).then_inc(par_in, 16)
        with sp.Fori(0, CH // 2) as i:
            for u in range(2):
                sp.wait_ge(u_ready, 2 * i + u + 1)
                sp.dma_start(u_in[u][:, :, :], ins["peer_u"][2 * i + u]).then_inc(u_loaded[u], 16)

    @block.gpsimd
    def _(pool):
        pool.sem_inc(u_ready, 2)
        pool.memset(one[:, :], 1.0).then_inc(one_ready, 1)
        pool.wait_ge(one_ready, 1)
        with pool.Fori(0, CH // 2) as i:
            for u in range(2):
                pool.wait_ge(u_loaded[u], 16 * i + 16)
                pool.wait_ge(hid_full, 2 * i + u + 1)
                pool.tensor_tensor(u_hi[u][:, :, :], u_in[u][:, :, :],
                                   one[:, :].unsqueeze(2).to_broadcast([P, KD, P]), ALU.mult).then_inc(u_cast, 1)
                pool.wait_ge(u_cast, 2 * i + u + 1)
                pool.tensor_tensor(u_lo[u][:, :, :], u_in[u][:, :, :], u_hi[u][:, :, :],
                                   ALU.subtract).then_inc(u_ready, 1)

    @block.scalar
    def _(act):
        act.sem_inc(hid_out, 2)
        act.sem_inc(w_out, 4)
        act.sem_inc(sel_out, 1)
        for i in range(2):
            act.sem_inc(g_stored[i], 16)
            act.sem_inc(w_stored[i], 16)

        def gelu(c, pair, u):
            act.wait_ge(hid_full, c + 3)
            act.wait_ge(g_stored[u], 16 * pair + 16)
            act.activation(g_out[u][:, :], hid_ps[u][:, :, :].rearrange("p a b -> p (a b)"),
                           ACT.Gelu_apprx_tanh).then_inc(hid_out, 1)
            act.wait_ge(hid_out, c + 3)
            act.dma_start(g_dram[c], g_out[u][:, :]).then_inc(g_stored[u], 16)

        with act.Fori(0, TB) as tb:
            for v in range(SEL):
                gelu(tb * SEL + v, tb * (SEL // 2) + v // 2, v % 2)
                if v == SEL - 2:
                    act.wait_ge(fin_ready, tb + 1)
                    act.activation(wrow[:, :, :], wrow[:, :, :], ACT.Exp).then_inc(exp_ready, 1)
            act.wait_ge(sel_turned, tb + 2)
            act.activation(codeT[:, bass.ts(tb, P)], w_ps[0][:, 0:P], ACT.Copy)
            act.activation(wT[:, bass.ts(tb, P)], w_ps[0][:, P:2 * P], ACT.Copy).then_inc(sel_out, 1)
        with act.Fori(0, CH // 2 // 8) as it:
            for v in range(8):
                gelu(CH // 2 + 8 * it + v, CH // 4 + 4 * it + v // 2, v % 2)
                b = v // 4
                if v % 4 == 0:
                    act.wait_ge(w_stored[b], 16 * it + 16)
                for k in range(4):
                    act.wait_ge(w_full, 8 + 4 * (8 * it + v) + k + 1)
                    t0 = GT * (v % 4) + 4 * k
                    act.activation(wbuf[b][:, :, t0:t0 + 4],
                                   w_ps[k][:, :].rearrange("p (t j) -> p j t", t=4), ACT.Copy).then_inc(w_out, 1)
                if v % 4 == 3:
                    act.wait_ge(w_out, 4 + 4 * (8 * it + v) + 4)
                    act.dma_start(w_dram[2 * it + b], wbuf[b][:, :, :]).then_inc(w_stored[b], 16)
        for i in range(2):
            act.wait_ge(g_stored[i], 16 + 16 * (CH // 2))
            act.wait_ge(w_stored[i], 16 + 16 * (SEQ // WT // 2))

    @block.tensor
    def _(pe):
        pe.sem_inc(hid_full, 2)
        pe.sem_inc(w_full, 8)
        pe.sem_inc(sel_turned, 1)
        pe.wait_ge(par_in, 32)

        def hidden(c, u):
            pe.wait_ge(u_ready, c + 3)
            pe.wait_ge(hid_out, c + 1)
            for hf in range(2):
                cols = slice(hf * HALF, (hf + 1) * HALF)
                for kd in range(KD):
                    pe.matmul(hid_ps[u][:, hf, :], u_hi[u][:, kd, :], xh[:, kd, cols], start=kd == 0, stop=False)
                    pe.matmul(hid_ps[u][:, hf, :], u_hi[u][:, kd, :], xl[:, kd, cols], start=False, stop=False)
                    mm = pe.matmul(hid_ps[u][:, hf, :], u_lo[u][:, kd, :], xh[:, kd, cols], start=False,
                                   stop=kd == KD - 1)
            mm.then_inc(hid_full, 1)

        with pe.Fori(0, TB) as tb:
            for v in range(SEL):
                hidden(tb * SEL + v, v % 2)
            pe.wait_ge(sel_ready, tb + 1)
            pe.wait_ge(sel_out, tb + 1)
            pe.transpose(w_ps[0][:, 0:P], crow[:, :, :].rearrange("p h k -> p (h k)"), ident[:, :])
            pe.transpose(w_ps[0][:, P:2 * P], wrow[:, :, :].rearrange("p h k -> p (h k)"),
                         ident[:, :]).then_inc(sel_turned, 1)
        pe.wait_ge(sel_out, TB + 1)
        with pe.Fori(0, CH // 2 // 8) as it:
            for v in range(8):
                hidden(CH // 2 + 8 * it + v, v % 2)
                g = 8 * it + v
                hi, lo, hj = hot[v % 2]
                pe.wait_ge(hot_ready, g + 1)
                for k in range(4):
                    pe.wait_ge(w_out, 4 * g + k + 1)
                    for i in range(4):
                        t = 4 * k + i
                        dst = w_ps[k][:, i * P:(i + 1) * P]
                        pe.matmul(dst, hi[:, t, :], hj[:, t, :], start=True, stop=False)
                        mm = pe.matmul(dst, lo[:, t, :], hj[:, t, :], start=False, stop=True)
                    mm.then_inc(w_full, 1)

    @block.vector
    def _(dve):
        tt, ts = dve.tensor_tensor, dve.tensor_scalar
        dve.wait_ge(par_in, 32)
        dve.tensor_copy(iota[:, :], con[:, 0:P]).then_inc(iota_ready, 1)
        with dve.Fori(0, TB) as tb:
            n = 0

            def link(i):
                nonlocal n
                i.then_inc(step, 1)
                n += 1
                dve.wait_ge(step, n)

            def top16(src, vals, idx, rows):
                for r in rows:
                    i = dve.max(vals[:, r, 0:8], src[:, r, :])
                link(i)
                for r in rows:
                    i = dve.max_index(idx[:, r, 0:8], vals[:, r, 0:8], src[:, r, :])
                link(i)
                for r in rows:
                    i = dve.match_replace(src[:, r, :], vals[:, r, 0:8], src[:, r, :], NEG)
                link(i)
                for r in rows:
                    i = dve.max(vals[:, r, 8:16], src[:, r, :])
                link(i)
                for r in rows:
                    i = dve.max_index(idx[:, r, 8:16], vals[:, r, 8:16], src[:, r, :])
                link(i)

            link(dve.tensor_copy(sc[:, :, :], s_sb[:, bass.ds(tb, 1), :, :].rearrange("p o h n -> p (o h) n")))
            top16(sc, top, topi, range(HC))
            link(dve.tensor_copy(topf[:, :, :], topi[:, :, :]))
            v4 = top[:, :, :].rearrange("p (h c) k -> p h c k", c=2)
            i4 = topf[:, :, :].rearrange("p (h c) k -> p h c k", c=2)
            link(ts(i4[:, :, 0, :], i4[:, :, 0, :], float(NK), None, ALU.mult))
            dve.wait_ge(sel_turned, tb + 1)
            off = 0
            for a, na, nb in PAIRS:
                for dst, src in ((cand, v4), (code, i4)):
                    out = dst[:, :, off:off + na * nb].rearrange("p h (a b) -> p h a b", a=na)
                    x = src[:, :, 0, a:a + na].unsqueeze(3).to_broadcast([P, PH, na, nb])
                    y = src[:, :, 1, 0:nb].unsqueeze(2).to_broadcast([P, PH, na, nb])
                    i = tt(out, x, y, ALU.add)
                off += na * nb
            link(i)
            top16(cand, fin, posi, range(PH))
            tt(wrow[:, :, :], fin[:, :, :], fin[:, :, 0:1].to_broadcast([P, PH, PK]), ALU.subtract).then_inc(fin_ready, 1)
            link(dve.tensor_copy(posf[:, :, :], posi[:, :, :]))
            for h in range(0, PH, 2):
                link(tt(match[:, :, :, :], posf[:, h:h + 2, :].unsqueeze(3).to_broadcast([P, 2, PK, NCAND]),
                        iota50.unsqueeze(1).unsqueeze(1).to_broadcast([P, 2, PK, NCAND]), ALU.is_equal))
                link(tt(match[:, :, :, :], match[:, :, :, :],
                        code[:, h:h + 2, :].unsqueeze(2).to_broadcast([P, 2, PK, NCAND]), ALU.mult))
                link(dve.tensor_reduce(crow[:, h:h + 2, :], match[:, :, :, :], AX.X, ALU.add))
            dve.wait_ge(exp_ready, tb + 1)
            link(dve.tensor_reduce(wsum[:, 0, :], wrow[:, :, :], AX.X, ALU.add))
            link(dve.reciprocal(wsum[:, 1, :], wsum[:, 0, :]))
            dve.sem_clear(step)
            tt(wrow[:, :, :], wrow[:, :, :], wsum[:, 1, :].unsqueeze(2).to_broadcast([P, PH, PK]),
               ALU.mult).then_inc(sel_ready, 1)
        dve.wait_ge(sel_out, TB + 1)
        base = [0]

        def link(i):
            i.then_inc(step, 1)
            base[0] += 1
            dve.wait_ge(step, base[0])

        link(ts(rowT[:, :], codeT[:, :], 1.0 / NK, -(NK - 1) / (2.0 * NK), ALU.mult, ALU.add))
        link(ts(rowT[:, :], rowT[:, :], MAGIC, None, ALU.add))
        link(ts(rowT[:, :], rowT[:, :], -MAGIC, None, ALU.add))
        link(dve.scalar_tensor_tensor(codeT[:, :], rowT[:, :], -float(NK), codeT[:, :], ALU.mult, ALU.add))
        half = hot[0][0][:, 0:8, :].rearrange("p a b -> p (a b)")
        link(dve.tensor_copy(half, wT[:, :]))
        link(dve.tensor_copy(whT[:, :], half))
        link(tt(wT[:, :], wT[:, :], whT[:, :], ALU.subtract))
        with dve.Fori(0, CH // 2 // 2) as q:
            for b in range(2):
                hi, lo, hj = hot[b]
                dve.wait_ge(w_full, 4 * (2 * q + b) + 4)
                for i in range(GT):
                    t = (2 * q + b) * GT + i
                    at_t = lambda x: x[:, bass.ds(t, 1)]
                    ts(hi[:, i, :], iota[:, :], at_t(rowT), at_t(whT), ALU.is_equal, ALU.mult)
                    ts(lo[:, i, :], iota[:, :], at_t(rowT), at_t(wT), ALU.is_equal, ALU.mult)
                    last = ts(hj[:, i, :], iota[:, :], at_t(codeT), None, ALU.is_equal)
                last.then_inc(hot_ready, 1)
    ctx.close()


def build_output(nc, ins, h_sb, g_dram, w_dram, out, mem_map):
    ctx = ExitStack()
    at = dict(mem_map)

    def sb(region, name, shape, dt=F32):
        size = int(np.prod(shape[1:])) * (2 if dt == BF16 else 4)
        off = at[region]
        at[region] = off + (size + 31) // 32 * 32
        assert at[region] <= mem_map[region] + mem_map[region + "_size"], (region, name)
        return nc.alloc_sbuf_tensor_at(name, shape, dt, offset=off)

    def sem(name):
        return ctx.enter_context(nc.semaphore(name))

    stat = sb("const", "stat4", [P, 64])
    gain = sb("const", "gain4", [P, D])
    NW = SEQ // WT
    w_sb = [sb("b", f"w_sb{i}", [P, NW, CG, WT]) for i in range(2)]
    g_sb = [sb("b", f"g_sb{i}", [P, CG, SEQ]) for i in range(2)]
    v_sb = [sb("b", f"v_sb{i}", [P, CG, D]) for i in range(2)]
    a_hi, a_lo, v_hi, v_lo = ([sb("b", f"{n}{i}", [P, CG, SEQ], BF16) for i in range(2)]
                              for n in ("a_hi", "a_lo", "v_hi", "v_lo"))
    ps = [ctx.enter_context(nc.psum_tensor(f"o_ps{i}", [P, HALF], F32)) for i in range(8)]
    gain_in = sem("gain4_in")
    loaded = [sem(f"gwv_loaded{i}") for i in range(2)]
    act_made = sem("act_made")
    ahi_made, alo_made = sem("ahi_made"), sem("alo_made")
    vhi_made, vlo_made = sem("vhi_made"), sem("vlo_made")
    o_full, o_out = sem("o_full"), sem("o_out")
    sq_done, rs_done, y_ready = sem("sq4_done"), sem("rs4_done"), sem("y_ready")
    half_set, pstep, dstep = sem("half_set4"), sem("pool_step4"), sem("dve_step4")
    stored = sem("y_stored")
    NG = CH // CG
    TILES = 2 * TB
    block = ctx.enter_context(nc.Block())

    @block.sync
    def _(sp):
        sp.dma_start(gain[:, :], ins["norm_final"].partition_broadcast(P)).then_inc(gain_in, 16)
        with sp.Fori(0, NG // 2) as i:
            for b in range(2):
                q = 2 * i + b
                sp.wait_ge(alo_made, CG * q + CG)
                sp.wait_ge(vlo_made, CG * q + CG)
                sp.dma_start(v_sb[b][:, :, :], ins["peer_v"][bass.ds(CG * q, CG)].rearrange("c p n -> p c n")).then_inc(loaded[b], 16)
                sp.dma_start(g_sb[b][:, :, :], g_dram[bass.ds(CG * q, CG)].rearrange("c p n -> p c n")).then_inc(loaded[b], 16)
                sp.dma_start(w_sb[b][:, :, :, :].rearrange("p g c t -> p g (c t)"),
                             w_dram[:, :, bass.ds(CG * q, CG), :].rearrange("g p c t -> p g (c t)")).then_inc(loaded[b], 16)
        for tb in range(TB):
            sp.wait_ge(y_ready, tb + 1)
            sp.dma_start(out[tb * P:(tb + 1) * P, :], h_sb[:, tb, :]).then_inc(stored, 16)
        sp.wait_ge(stored, 16 * TB)

    @block.gpsimd
    def _(pool):
        pool.sem_inc(vlo_made, 2 * CG)
        pool.memset(stat[:, 32:33], -0.5).then_inc(half_set, 1)
        pool.wait_ge(half_set, 1)
        with pool.Fori(0, NG // 2) as i:
            for b in range(2):
                q = 2 * i + b
                for c in range(CG):
                    pool.wait_ge(vhi_made, CG * q + c + 1)
                    pool.tensor_tensor(v_lo[b][:, c, :], v_sb[b][:, c, :], v_hi[b][:, c, :],
                                       ALU.subtract).then_inc(vlo_made, 1)
        for tb in range(TB):
            pool.wait_ge(sq_done, tb + 1)
            pool.tensor_scalar(stat[:, tb:tb + 1], stat[:, tb:tb + 1], 1.0 / D, EPS, ALU.mult, ALU.add).then_inc(pstep, 1)
            pool.wait_ge(pstep, tb + 1)
            pool.tensor_tensor(stat[:, 16 + tb:17 + tb], stat[:, tb:tb + 1], stat[:, 32:33], ALU.pow).then_inc(rs_done, 1)

    @block.scalar
    def _(act):
        with act.Fori(0, NG // 2) as i:
            for b in range(2):
                q = 2 * i + b
                act.wait_ge(loaded[b], 48 * i + 48)
                act.wait_ge(o_full, TILES * q + TILES)
                for c in range(CG):
                    act.activation(v_hi[b][:, c, :], v_sb[b][:, c, :], ACT.Copy).then_inc(vhi_made, 1)
                for c in range(CG):
                    act.wait_ge(act_made, CG * q + c + 1)
                    act.activation(a_hi[b][:, c, :], g_sb[b][:, c, :], ACT.Copy).then_inc(ahi_made, 1)
        for tb in range(TB):
            act.wait_ge(o_out, 8 + (NG - 1) * TILES + 2 * tb + 2)
            if tb == 0:
                act.wait_ge(o_full, TILES * NG + 2 * TILES)
            if tb >= 4:
                act.wait_ge(sq_done, tb - 3)
            act.activation(v_sb[0][:, tb % 4, :], h_sb[:, tb, :], ACT.Square, accum_out=stat[:, tb:tb + 1]).then_inc(sq_done, 1)

    @block.tensor
    def _(pe):
        pe.sem_inc(o_full, 2 * TILES)
        with pe.Fori(0, NG // 2) as i:
            for b in range(2):
                q = 2 * i + b
                pe.wait_ge(vlo_made, CG * q + 3 * CG)
                pe.wait_ge(alo_made, CG * q + 3 * CG)
                for n in range(TILES):
                    tb, hf = divmod(n, 2)
                    tok, col = slice(tb * P, (tb + 1) * P), slice(hf * HALF, (hf + 1) * HALF)
                    pe.wait_ge(o_out, TILES * q + n + 1)
                    bank = ps[n % 8][:, :]
                    for c in range(CG):
                        pe.matmul(bank, a_hi[b][:, c, tok], v_hi[b][:, c, col], start=c == 0, stop=False)
                        pe.matmul(bank, a_hi[b][:, c, tok], v_lo[b][:, c, col], start=False, stop=False)
                        mm = pe.matmul(bank, a_lo[b][:, c, tok], v_hi[b][:, c, col], start=False, stop=c == CG - 1)
                    mm.then_inc(o_full, 1)

    @block.vector
    def _(dve):
        dve.sem_inc(o_out, 8)
        dve.sem_inc(alo_made, 2 * CG)

        def activations(q, i, b):
            dve.wait_ge(loaded[b], 48 * i + 48)
            dve.wait_ge(o_full, TILES * q + TILES)
            for c in range(CG):
                g = g_sb[b][:, c, :].rearrange("p (g t) -> p g t", g=NW)
                dve.tensor_tensor(g, g, w_sb[b][:, :, c, :], ALU.mult).then_inc(act_made, 1)
            for c in range(CG):
                dve.wait_ge(ahi_made, CG * q + c + 1)
                dve.tensor_tensor(a_lo[b][:, c, :], g_sb[b][:, c, :], a_hi[b][:, c, :], ALU.subtract).then_inc(alo_made, 1)

        def join(q, tiles):
            for n in tiles:
                tb, hf = divmod(n, 2)
                acc = h_sb[:, tb, hf * HALF:(hf + 1) * HALF]
                dve.wait_ge(o_full, TILES * q + 2 * TILES + n + 1)
                dve.tensor_tensor(acc, acc, ps[n % 8][:, :], ALU.add).then_inc(o_out, 1)

        activations(0, 0, 0)
        with dve.Fori(0, NG // 2 - 1) as i:
            activations(2 * i + 1, i, 1)
            join(2 * i, range(TILES))
            activations(2 * i + 2, i + 1, 0)
            join(2 * i + 1, range(TILES))
        activations(NG - 1, NG // 2 - 1, 1)
        join(NG - 2, range(TILES))
        join(NG - 1, range(TILES))
        dve.wait_ge(gain_in, 16)
        for tb in range(TB):
            dve.wait_ge(rs_done, tb + 1)
            dve.scalar_tensor_tensor(h_sb[:, tb, :], h_sb[:, tb, :], stat[:, 16 + tb:17 + tb], gain[:, :],
                                     ALU.mult, ALU.mult).then_inc(y_ready, 1)
    ctx.close()


BASE = 16512


def regions(*parts):
    out, at = {}, BASE
    for name, kib in parts:
        out[name], out[name + "_size"] = at, int(kib * 1024)
        at += int(kib * 1024)
    assert at <= 229344
    return out


MIX_MAP = regions(("const", 5.75), ("nt", 32), ("w", 48), ("zt", 16), ("ret", 16), ("s5c", 20),
                  ("wbr", 32), ("tmp", 30), ("sg", 8))
SCORE_MAP = regions(("const", 5.75), ("nt", 32), ("xhl", 32), ("s", 64), ("xnt", 32), ("wq", 16),
                    ("keys", 8), ("qt", 8))
HIDDEN_MAP = regions(("const", 5.75), ("nt", 32), ("xhl", 32), ("s", 64), ("u", 16), ("g", 8),
                     ("sel", 16), ("hot", 24))
OUT_MAP = regions(("const", 5.75), ("nt", 32), ("b", 160))


def build_program(nc, ins, out):
    h_sb = nc.alloc_sbuf_tensor_at("h", [P, TB, D], F32, offset=MIX_MAP["nt"])
    xh = nc.alloc_sbuf_tensor_at("xh", [P, KD, SEQ], BF16, offset=SCORE_MAP["xhl"])
    xl = nc.alloc_sbuf_tensor_at("xl", [P, KD, SEQ], BF16, offset=SCORE_MAP["xhl"] + KD * SEQ * 2)
    s_sb = nc.alloc_sbuf_tensor_at("scores", [P, TB, HC, NK], F32, offset=SCORE_MAP["s"])
    g_dram = nc.dram_tensor("g_scratch", [CH, P, SEQ], F32).ap()
    w_dram = nc.dram_tensor("w_scratch", [SEQ // WT, P, NK, WT], F32).ap()
    build_mixer(nc, ins, h_sb, MIX_MAP)
    build_scores(nc, ins, h_sb, xh, xl, s_sb, SCORE_MAP)
    build_hidden(nc, ins, xh, xl, s_sb, g_dram, w_dram, HIDDEN_MAP)
    build_output(nc, ins, h_sb, g_dram, w_dram, out, OUT_MAP)


def columns(a):
    return a.reshape(-1, P).T


def s5_blocks(a):
    out = np.zeros((P, S5T, P), a.dtype)
    for group in range(a.shape[0]):
        s, g = divmod(group, 2)
        c = 32 * (s % 4) + 16 * g
        out[64 * g:64 * g + 64, s, c:c + 16] = a[group]
    return out


def layout(a):
    g = {n: a[n][0] for n in ("x", "mem", "w_in", "w_mem_kv", "s5_w_glu", "w_branch_ret", "w_branch_s5",
                              "w_branch_mem", "w_out", "peer_w_q")}
    g["norm_final"] = a["norm_final"]
    for n in ("positions", "norm_mix", "norm_mem", "norm_ffn", "s5_d"):
        g[n] = columns(a[n][0])
    for n in ("s5_a_re", "s5_a_im"):
        g[n] = columns(a[n][0].reshape(-1))
    g["s5_log_dt"] = columns(np.repeat(a["s5_log_dt"][0], 64))
    for n in ("s5_b_re", "s5_b_im"):
        g[n] = s5_blocks(a[n][0])
    for n in ("s5_c_re", "s5_c_im"):
        g[n] = s5_blocks(a[n][0].transpose(0, 2, 1))
    g["peer_keys"] = a["peer_keys"][0].reshape(HC, NK, P).transpose(2, 0, 1)
    g["peer_u"] = a["peer_u"][0].reshape(NK, NK, KD, P).transpose(1, 3, 2, 0)
    g["peer_v"] = a["peer_v"][0].reshape(NK, NK, D).transpose(1, 0, 2)
    g["consts"] = constants()
    return {n: np.ascontiguousarray(v) for n, v in g.items()}


def kernel(**inputs):
    import concourse.bacc as bacc
    from concourse.bass_utils import run_bass_kernel_spmd

    nc = bacc.Bacc("TRN2", target_bir_lowering=False, num_devices=1)
    arrays = layout({n: np.asarray(v) for n, v in inputs.items()})
    ins = {n: nc.dram_tensor("in_" + n, v.shape, mybir.dt.from_np(v.dtype), kind="ExternalInput").ap()
           for n, v in arrays.items()}
    out = nc.dram_tensor("out", [SEQ, D], F32, kind="ExternalOutput").ap()
    build_program(nc, ins, out)
    r = run_bass_kernel_spmd(nc, [{"in_" + n: v for n, v in arrays.items()}], core_ids=[0])
    return r.results[0]["out"].reshape(1, SEQ, D)
```

```python
import math
from contextlib import ExitStack

import numpy as np
import concourse.bass as bass
from concourse import mybir

F32 = mybir.dt.float32
BF16 = mybir.dt.bfloat16
I32 = mybir.dt.int32
U32 = mybir.dt.uint32
ALU = mybir.AluOpType
ACT = mybir.ActivationFunctionType
AX = mybir.AxisListType

P = 128
SEQ, D = 1024, 1024
TB = SEQ // P
KD = D // P
MEM = 256
EPS = 1e-6
HALF = 512
RH, RD = 4, 128
S5T = 8
MH, MD = 4, 64
Q0, K0, V0, G0, U0, GATE0 = 0, 512, 1024, 1536, 2048, 2560
MAGIC = 12582912.0
TWO_PI_HI, TWO_PI_MID, TWO_PI_LO = 6.28125, 0.0019350051879882812, 3.0199159819e-07
PI_BELOW = 3.1415925

GAMMA = [1.0 - 2.0 ** (-5.0 - h) for h in range(RH)]


def constants():
    i = np.arange(P)
    decay = np.zeros((P, RH, P))
    kfac, qfac = np.zeros((P, RH)), np.zeros((P, RH))
    for h, g in enumerate(GAMMA):
        decay[:, h, :] = np.where(i[:, None] <= i[None, :], (g ** -(i + 1.0))[:, None], 0.0) * RD ** -0.5
        kfac[:, h] = g ** (P - 1.0 - i) * RD ** -0.5
        qfac[:, h] = g ** (i + 1.0)
    inv = (10000.0 ** (-np.arange(64, dtype=np.float32) / np.float32(64))).astype(np.float32)
    rows = [np.eye(P), decay.reshape(P, RH * P), kfac, qfac, np.tile(inv, (P, 1)),
            np.tile(np.arange(P, dtype=np.float64), (P, 1)),
            np.tile(np.arange(50, dtype=np.float64), (P, 1))]
    return np.ascontiguousarray(np.concatenate(rows, 1).astype(np.float32))


C_ID, C_DEC, C_KF, C_QF, C_INV, C_IOTA, C_IOTA50 = 0, 128, 640, 644, 648, 712, 840
C_COLS = 890


QUARTERS = 4


def mixer_steps():
    main = [("z", ct, hf) for hf in range(2) for ct in range(4)]
    for hp in range(2):
        for tb in range(TB):
            main += [("qk", hp, tb), ("vg", hp, tb)]
    for dh in range(2):
        for br in range(3):
            main += [("gate", dh, br, tb) for tb in range(TB)]
    first = 8
    extra = {}

    def put(slot, job):
        extra.setdefault(slot, []).append(job)

    for hp in range(2):
        for tb in range(TB):
            at = 2 * (first + hp * 16 + 2 * tb)
            put(at + 4, ("turn", hp, tb))
            put(at + 6, ("score", hp, tb))
            put(at + 7, ("mix", hp, tb))
            put(at + 8, ("flip", hp, tb))
    chain = [(tb, mp) for tb in range(TB) for mp in range(2)]
    for c, (tb, mp) in enumerate(chain):
        for k, name in enumerate(("ascore", "aturn", "amix", "aflip")):
            put(2 * first + 6 + 4 * c + k, (name, tb, mp))
    for s in range(S5T):
        at = 2 * first + 6 * s
        if s:
            put(at - 2, ("tables", s, 0))
            put(at - 1, ("tables", s, 1))
            put(at - 1, ("tables", s, 2))
        for hf in range(2):
            put(at + 2 * hf, ("bu", s, hf))
            put(at + 2 * hf + 1, ("scan", s, hf))
            put(at + 2 * hf + 2, ("states", s, hf))
            put(at + 3 * hf + 6, ("y", s, hf))
    glu = 2 * first + 6 * S5T + 8
    put(glu, ("glu", 0))
    put(glu + 2, ("glu", 1))
    last = {}
    steps = []
    plan = split_plan()

    def splits(n):
        return [("split", n, i) for i in range(4)]

    steps += [("xturn", tb, kh) for tb in range(4) for kh in range(2)] + [("param", 0)]
    for m, unit in enumerate(main):
        small = extra.pop(2 * m, []) + extra.pop(2 * m + 1, [])
        if m < first:
            steps.append(unit)
            assert not small
        else:
            n = len(small)
            pieces = plan.get(m, [])
            pieces = [None] * (QUARTERS - len(pieces)) + pieces
            for q in range(QUARTERS):
                steps.append(("open", unit, q) if q < QUARTERS - 1 else unit)
                steps += small[n * q // QUARTERS:n * (q + 1) // QUARTERS]
                steps += [pieces[q]] if pieces[q] else []
        steps += [("xturn", tb, kh) for tb in {1: (4,), 2: (5, 6), 3: (7,)}.get(m, ()) for kh in range(2)]
        if m in (1, 2):
            steps += splits(1)[2 * m - 2:2 * m]
        if m == 3:
            steps += [("param", 1)]
        if m in (4, 7):
            steps += splits(2)[:2] if m == 4 else splits(2)[2:]
        if m == 6:
            steps += [("mturn", mt, kh) for mt in range(2) for kh in range(2)]
        if m == 7:
            steps += [("bturn", s) for s in range(0, S5T, 2)] + [("tables", 0, part) for part in range(3)]
        if m == 9:
            steps += [("mk", 0), ("mk", 1), ("mv", 0), ("mv", 1)]
        if unit[0] == "gate" and unit[2] == 2 and unit[3] >= 2:
            steps.append(("gturn", unit[1], unit[3] - 2))
            if unit[3] == TB - 1:
                if unit[1] == 1:
                    steps += [("gturn", 1, TB - 2), ("gturn", 1, TB - 1)]
        if unit[0] == "gate" and unit[1] == 1 and unit[2] == 0 and unit[3] < 2:
            steps.append(("gturn", 0, TB - 2 + unit[3]))
    assert not extra, extra
    steps += [("out", dh, tb) for dh in range(2) for tb in range(TB)]
    return steps


LOADS = [("z", None, ("z", 3, 1)), ("qk", 0, ("qk", 0, TB - 1)), ("vg", 0, ("vg", 0, TB - 1)),
         ("mem", None, ("mv", 1)), ("qk", 1, ("qk", 1, TB - 1)), ("vg", 1, ("vg", 1, TB - 1))]
LOADS += [("gate", (dh, br), ("gate", dh, br, TB - 1)) for dh in range(2) for br in range(3)]
LOADS += [("out", dh, ("out", dh, TB - 1)) for dh in range(2)]
LOAD_NO = {(k, a): n for n, (k, a, _) in enumerate(LOADS)}
BUFFER = [2, 0, 1, 2, 2, 0, 1, 2, 0, 1, 2, 0, 1, 2]


def split_plan():
    plan = {}
    for m, n in ((13, 4), (25, 6), (39, 7), (43, 8), (48, 9), (56, 10), (64, 11), (72, 12), (80, 13)):
        for i in range(4):
            plan.setdefault(m + i, []).append(("split", n, i))
    plan[22] = [("split", 5, 0)]
    plan[23] = [("split", 5, i) for i in (1, 2, 3)]
    for m, row in ((37, 4), (38, 5), (39, 6), (40, 7), (44, 0), (45, 1), (46, 2), (47, 3)):
        plan.setdefault(m, []).append(("split", "br", row))
    return plan


MAIN = ("z", "qk", "vg", "gate")
OWN_BANK = ("bu", "y", "split", "param", "open", "tables", "scan", "states")


def build_mixer(nc, ins, h_sb, mem_map):
    steps = mixer_steps()
    main_no = {s: n for n, s in enumerate([s for s in steps if s[0] in MAIN])}
    misc_no = {s: n for n, s in enumerate([s for s in steps if s[0] not in MAIN + OWN_BANK])}
    gate_no = {s: n for n, s in enumerate([s for s in steps if s[0] == "gate"])}
    bu_no = {s: n for n, s in enumerate([s for s in steps if s[0] == "bu"])}
    chain_no = {(tb, mp): 2 * tb + mp for tb in range(TB) for mp in range(2)}
    turn_no = {(hp, tb): hp * TB + tb for hp in range(2) for tb in range(TB)}

    ctx = ExitStack()
    ctx.enter_context(nc.allow_non_contiguous_dma("small parameter columns"))
    at = {k: v for k, v in mem_map.items()}

    def sb(region, name, shape, dt=F32):
        size = int(np.prod(shape[1:])) * (2 if dt == BF16 else 4)
        off = at[region]
        at[region] = off + (size + 31) // 32 * 32
        assert at[region] <= mem_map[region] + mem_map[region + "_size"], (region, name, at[region] - mem_map[region])
        return nc.alloc_sbuf_tensor_at(name, shape, dt, offset=off)

    def sem(name):
        return ctx.enter_context(nc.semaphore(name))

    def again(region, skip=0):
        at[region] = mem_map[region] + skip

    con = sb("const", "con", [P, C_COLS])
    small = sb("const", "small", [P, 22, 8])
    levels = sb("const", "levels", [P, 2, 9, S5T])
    gains = sb("const", "gains", [P, 2, KD])
    stat = sb("const", "stat", [P, 64])
    nhl = sb("nt", "nhl", [P, KD, TB, 2, P], BF16)
    nT = sb("x", "nT", [P, KD, SEQ])
    again("x")
    tab = sb("x", "tab", [P, 2, HALF])
    kmT = sb("x", "kmT", [P, 2, 2, MEM])
    vm = sb("x", "vm", [P, 2, MEM])
    psc = sb("x", "psc", [P, HALF])
    qkT = sb("x", "qkT", [P, 2, HALF])
    prod = sb("x", "prod", [P, 4, HALF])
    ysc = sb("x", "ysc", [P, 2, 2, HALF])
    again("x")
    wbr = sb("x", "wbr", [P, 8, 2, D], BF16)
    wring = [sb("w", f"w{i}", [P, KD, 2, HALF], BF16) for i in range(3)]
    again("w")
    xs = sb("w", "xs", [P, TB, D])
    wfull = sb("w", "wfull", [P, KD, HALF])
    stage = sb("stage", "stage", [P, 2, 2 * HALF])
    zT = sb("zt", "zT", [P, 4, SEQ])
    again("zt")
    zhl = sb("zt", "zhl", [P, 4, TB, 2, P], BF16)
    again("zt")
    merT_hi = sb("zt", "merT_hi", [P, 4, TB, 2, P], BF16)
    memT = sb("ret", "memT", [P, KD, MEM])
    mem_x = sb("ret", "mem_x", [P, 2, D])
    again("ret")
    retT = sb("ret", "retT", [P, RH, TB, 2, P], BF16)
    bbT = sb("s5c", "bbT", [P, 2, S5T, P])
    cT = sb("s5c", "cT", [P, 2, S5T, P])
    wglu = sb("s5c", "wglu", [P, 2, 512])
    again("s5c")
    merged = sb("s5c", "merged", [P, TB, HALF])
    btab = sb("tmp", "btab", [P, 2, S5T, 16])
    rope = sb("tmp", "rope", [P, 2, TB, 64])
    bsrc = sb("tmp", "bsrc", [P, 2, S5T, P])
    btmp = sb("tmp", "btmp", [P, 2, S5T, P])
    again("tmp", 5120)
    qk = sb("tmp", "qk", [P, 2, HALF])
    vg = sb("tmp", "vg", [P, 2, HALF])
    qkr = sb("tmp", "qkr", [P, HALF])
    kdec = sb("tmp", "kdec", [P, 2, 256])
    sT = sb("tmp", "sT", [P, 256])
    ret = sb("tmp", "ret", [P, 256])
    state = sb("tmp", "state", [P, RH, P])
    pT = sb("tmp", "pT", [P, HALF])
    mo = sb("tmp", "mo", [P, P])
    junk = sb("tmp", "junk", [P, P])
    again("tmp")
    merT_lo = sb("tmp", "merT_lo", [P, 4, TB, 2, P], BF16)
    gp = sb("tmp", "gp", [P, 2, HALF])
    xr = sb("tmp", "xr", [P, 2, HALF])
    sg = sb("sg", "sg", [P, 2, HALF])
    rt = sb("sg", "rt", [P, 2, 256])

    main_ps = [ctx.enter_context(nc.psum_tensor(f"main{i}", [P, HALF], F32)) for i in range(2)]
    misc_ps = [ctx.enter_context(nc.psum_tensor(f"misc{i}", [P, HALF], F32)) for i in range(2)]
    bu_ps = [ctx.enter_context(nc.psum_tensor(f"bu{i}", [P, HALF], F32)) for i in range(2)]
    p_ps = bu_ps
    y_ps = [ctx.enter_context(nc.psum_tensor(f"y{i}", [P, HALF], F32)) for i in range(2)]

    x_in = [sem(f"x_in{i}") for i in range(TB)]
    con_in = sem("con_in")
    par_in = sem("par_in")
    gain_in = sem("gain_in")
    b_in = sem("b_in")
    c_in = sem("c_in")
    mem_in = sem("mem_in")
    wfull_in = sem("wfull_in")
    staged = [sem(f"staged{i}") for i in range(2)]
    split_hi, split_done = sem("split_hi"), sem("split_done")
    nh_done, nl_done = sem("nh_done"), sem("nl_done")
    xr_in = [sem(f"xr_in{i}") for i in range(2)]
    sq_done = sem("sq_done")
    rs_done = sem("rs_done")
    n_ready = sem("n_ready")
    main_full, main_out = sem("main_full"), sem("main_out")
    misc_full, misc_out = sem("misc_full"), sem("misc_out")
    p_full, p_out = sem("p_full"), sem("p_out")
    bu_full, bu_out = sem("bu_full"), sem("bu_out")
    y_full = sem("y_full")
    xst_ready = sem("xst_ready")
    half_ready = sem("half_ready")
    bb_ready = sem("bb_ready")
    cneg_ready = sem("cneg_ready")
    ydu_ready = sem("ydu_ready")
    gelu_ready = sem("gelu_ready")
    exp_ready = sem("exp_ready")
    gsig_ready = sem("gsig_ready")
    lam_ready = sem("lam_ready")
    ang_ready = sem("ang_ready")
    rope_ready = sem("rope_ready")
    rot_done = sem("rot_done")
    kdec_done = sem("kdec_done")
    vgate_done = sem("vgate_done")
    ret_done = sem("ret_done")
    retraw_done = sem("retraw_done")
    sg_ready = sem("sg_ready")
    glu_tanh = sem("glu_tanh")
    merged_done = sem("merged_done")
    dchain, pchain, achain = sem("dve_step"), sem("pool_step"), sem("act_step")

    split_no = {s: n for n, s in enumerate([s for s in steps if s[0] == "split"])}

    def weights(eng, kind, arg):
        n = LOAD_NO[(kind, arg)]
        eng.wait_ge(split_done, split_no[("split", n, 3)] + 1)
        return wring[BUFFER[n]]

    def branch_weights(eng, row):
        eng.wait_ge(split_done, split_no[("split", "br", row)] + 1)

    STAGED, per = {}, [0, 0]
    for s in [s for s in steps if s[0] == "split"]:
        per[split_no[s] % 2] += 2 if s[1] != "br" and LOADS[s[1]][0] in ("qk", "vg") else 1
        STAGED[s] = 16 * per[split_no[s] % 2]

    def split_target(s):
        _, n, i = s
        if n == "br":
            return wbr[:, i, 0, :], wbr[:, i, 1, :]
        w = wring[BUFFER[n]][:, 2 * i:2 * i + 2, :, :]
        return w[:, :, 0, :], w[:, :, 1, :]

    def split_source(s):
        t = stage[:, split_no[s] % 2, :]
        return t if s[1] == "br" else t.rearrange("p (k n) -> p k n", k=2)

    def target_free(eng, s):
        _, n, i = s
        if n == "br":
            for last in (("glu", 1),) if i >= 4 else (("aflip", TB - 1, 1), ("flip", 1, TB - 1)):
                eng.wait_ge(misc_out, misc_no[last] + 1)
            return
        before = [m for m in range(n) if BUFFER[m] == BUFFER[n]]
        if before:
            done_by_pe(eng, LOADS[before[-1]][2])
        if n in (1, 2):
            done_by_pe(eng, ("xturn", TB // 2 * n - 1, 1))

    def done_by_pe(eng, step):
        if step[0] in MAIN:
            eng.wait_ge(main_full, main_no[step] + 1)
        else:
            eng.wait_ge(misc_full, misc_no[step] + 1)

    SC = {"ct": 0, "ln": 1}
    (S_ARE, S_AIM, S_LDT, S_DT, S_MAG, S_TH, S_COS, S_SIN, S_LRE, S_LIM, S_DEN, S_CR, S_CI,
     S_T0, S_T1, S_T2, S_T3, S_D, S_POS, S_CN, S_SN, S_POSI) = range(22)
    block = ctx.enter_context(nc.Block())

    @block.sync
    def _(sp):
        sp.dma_start(con[:, :], ins["consts"]).then_inc(con_in, 16)
        w_in = ins["w_in"].rearrange("(k p) n -> p k n", p=P)
        w_out = ins["w_out"].rearrange("(k p) n -> p k n", p=P)
        for tb in range(TB):
            if tb == TB // 2:
                sp.dma_start(wfull[:, :, :], w_in[:, :, U0:U0 + HALF]).then_inc(wfull_in, 16)
            sp.dma_start(xs[:, tb, :], ins["x"][tb * P:(tb + 1) * P, :]).then_inc(x_in[tb], 16)
            if tb == 1:
                for k, name in ((S_ARE, "s5_a_re"), (S_AIM, "s5_a_im"), (S_LDT, "s5_log_dt"), (S_D, "s5_d")):
                    sp.dma_start(small[:, k, 0:ins[name].shape[1]], ins[name]).then_inc(par_in, 16)
                sp.dma_start(small[:, S_POSI, :].bitcast(I32), ins["positions"]).then_inc(par_in, 16)
        sp.dma_start(mem_x[:, :, :], ins["mem"].rearrange("(b p) n -> p b n", p=P)).then_inc(mem_in, 16)
        for k, name in enumerate(("s5_b_re", "s5_b_im")):
            sp.dma_start(bsrc[:, k, :, :], ins[name]).then_inc(b_in, 16)
        for k, name in enumerate(("s5_c_re", "s5_c_im")):
            sp.dma_start(cT[:, k, :, :], ins[name]).then_inc(c_in, 16)
        sp.dma_start(wglu[:, :, :], ins["s5_w_glu"].rearrange("(k p) n -> p k n", p=P)).then_inc(c_in, 16)
        branch_name = {0: ("w_branch_ret", 0), 4: ("w_branch_s5", 4), 6: ("w_branch_mem", 6)}
        for s in [s for s in steps if s[0] == "split"]:
            k = split_no[s]
            if k >= 2:
                sp.wait_ge(split_done, k - 1)
            dst, ready = stage[:, k % 2, :], staged[k % 2]
            _, n, i = s
            if n == "br":
                name, first = branch_name[0 if i < 4 else 4 if i < 6 else 6]
                sp.dma_start(dst, ins[name][(i - first) * P:(i - first + 1) * P, :]).then_inc(ready, 16)
                continue
            kind, arg, _ = LOADS[n]
            dst = dst.rearrange("p (k n) -> p k n", k=2)
            if kind in ("qk", "vg"):
                for j, base in enumerate((Q0, K0) if kind == "qk" else (V0, G0)):
                    sp.dma_start(dst[:, :, 256 * j:256 * j + 256],
                                 w_in[:, 2 * i:2 * i + 2, base + 256 * arg:base + 256 * arg + 256]).then_inc(ready, 8 * 2)
            elif kind == "gate":
                col = GATE0 + (1, 2, 0)[arg[1]] * D + arg[0] * HALF
                sp.dma_start(dst, w_in[:, 2 * i:2 * i + 2, col:col + HALF]).then_inc(ready, 16)
            else:
                sp.dma_start(dst, w_out[:, 2 * i:2 * i + 2, arg * HALF:(arg + 1) * HALF]).then_inc(ready, 16)
            if s == ("split", 2, 3):
                done_by_pe(sp, ("z", 3, 1))
                sp.dma_start(wfull[:, :, :], ins["w_mem_kv"].rearrange("(k p) n -> p k n", p=P)).then_inc(wfull_in, 16)
        for n in range(2 * TB):
            dh, tb = divmod(n, TB)
            if n >= 2:
                sp.wait_ge(misc_out, misc_no[("out", *divmod(n - 2, TB))] + 1)
            sp.dma_start(xr[:, n % 2, :],
                         ins["x"][tb * P:(tb + 1) * P, dh * HALF:(dh + 1) * HALF]).then_inc(xr_in[n % 2], 16)

    @block.gpsimd
    def _(pool):
        for k, name in enumerate(("norm_mix", "norm_mem")):
            pool.dma_start(gains[:, k, :], ins[name]).then_inc(gain_in, 16)
        chain = 0

        def link(i):
            nonlocal chain
            i.then_inc(pchain, 1)
            chain += 1
            pool.wait_ge(pchain, chain)

        link(pool.memset(stat[:, 32:48], -0.5))
        def root(n):
            pool.wait_ge(sq_done, n + 1)
            link(pool.tensor_scalar(stat[:, n:n + 1], stat[:, n:n + 1], 1.0 / D, EPS, ALU.mult, ALU.add))
            pool.tensor_tensor(stat[:, 16 + n:17 + n], stat[:, n:n + 1], stat[:, 32:33], ALU.pow).then_inc(rs_done, 1)

        for n in range(TB):
            root(n)

        for n, (_, tb, kh) in enumerate([s for s in steps if s[0] == "xturn"]):
            pool.wait_ge(nh_done, n + 1)
            pool.tensor_tensor(nhl[:, 4 * kh:4 * kh + 4, tb, 1, :], nT[:, 4 * kh:4 * kh + 4, tb * P:(tb + 1) * P],
                               nhl[:, 4 * kh:4 * kh + 4, tb, 0, :], ALU.subtract).then_inc(nl_done, 1)
        root(TB)
        root(TB + 1)
        pool.wait_ge(rope_ready, 2)

        def rotate(hp, tb):
            n = turn_no[(hp, tb)]
            pool.wait_ge(main_out, main_no[("qk", hp, tb)] + 1)
            if n >= 1:
                done_by_pe(pool, ("turn", *divmod(n - 1, TB)))
                pool.wait_ge(kdec_done, n)
            src = qk[:, n % 2, :].rearrange("p (h c d) -> p h c d", h=4, c=2)
            dst = qkr[:, :].rearrange("p (h c d) -> p h c d", h=4, c=2)
            cos = rope[:, 0, tb, :].unsqueeze(1).to_broadcast([P, 4, 64])
            sin = rope[:, 1, tb, :].unsqueeze(1).to_broadcast([P, 4, 64])
            t = [rt[:, i, :].rearrange("p (h d) -> p h d", h=4) for i in range(2)]
            pool.tensor_tensor(dst[:, :, 0, :], src[:, :, 0, :], cos, ALU.mult)
            pool.tensor_tensor(dst[:, :, 1, :], src[:, :, 0, :], sin, ALU.mult)
            pool.tensor_tensor(t[0], src[:, :, 1, :], sin, ALU.mult)
            link(pool.tensor_tensor(t[1], src[:, :, 1, :], cos, ALU.mult))
            pool.tensor_tensor(dst[:, :, 0, :], dst[:, :, 0, :], t[0], ALU.subtract)
            pool.tensor_tensor(dst[:, :, 1, :], dst[:, :, 1, :], t[1], ALU.add).then_inc(rot_done, 1)

        def gate_value(hp, tb):
            n = turn_no[(hp, tb)]
            pool.wait_ge(gsig_ready, n + 1)
            pool.wait_ge(main_out, main_no[("vg", hp, tb)] + 1)
            th = sg[:, n % 2, 0:256]
            link(pool.tensor_scalar(th, th, 1.0, 0.5, ALU.add, ALU.mult))
            g = vg[:, n % 2, 256:512]
            pool.tensor_tensor(g, g, th, ALU.mult).then_inc(vgate_done, 1)

        def normed(hp, tb):
            n = turn_no[(hp, tb)]
            pool.wait_ge(retraw_done, 2 * n + 2)
            s2, s3 = stat[:, 48:50], stat[:, 50:52]
            link(pool.tensor_scalar(s2, s2, 1.0 / RD, EPS, ALU.mult, ALU.add))
            link(pool.tensor_tensor(s3, s2, stat[:, 32:34], ALU.pow))
            g = vg[:, n % 2, 256:512]
            link(pool.tensor_tensor(g.rearrange("p (h d) -> p h d", h=2), g.rearrange("p (h d) -> p h d", h=2),
                                    s3.unsqueeze(2).to_broadcast([P, 2, P]), ALU.mult))
            pool.tensor_tensor(ret[:, :], ret[:, :], g, ALU.mult).then_inc(ret_done, 1)

        for s in steps:
            if s[0] == "qk":
                rotate(s[1], s[2])
            if s[0] == "vg":
                gate_value(s[1], s[2])
            if s[0] == "mix":
                normed(s[1], s[2])
            if s[0] == "gate" and s[2] > 0:
                _, dh, br, tb = s
                n = gate_no[s]
                pool.wait_ge(p_out, n + 1)
                pool.tensor_tensor(merged[:, tb, :], merged[:, tb, :], gp[:, n % 2, :], ALU.add).then_inc(merged_done, 1)

    @block.scalar
    def _(act):
        chain = 0

        def link(i):
            nonlocal chain
            i.then_inc(achain, 1)
            chain += 1
            act.wait_ge(achain, chain)

        def squares(n, src):
            act.activation(zT[:, n % 2, :], src, ACT.Square, accum_out=stat[:, n:n + 1]).then_inc(sq_done, 1)

        for tb in range(TB):
            act.wait_ge(x_in[tb], 16)
            if tb >= 2:
                act.wait_ge(sq_done, tb - 1)
            squares(tb, xs[:, tb, :])

        sm = lambda k: small[:, k, :]

        def memory_squares():
            act.wait_ge(mem_in, 16)
            act.wait_ge(rope_ready, 1)
            for m in range(2):
                act.activation(btmp[:, m, :, :].rearrange("p s q -> p (s q)"), mem_x[:, m, :], ACT.Square,
                               accum_out=stat[:, TB + m:TB + m + 1]).then_inc(sq_done, 1)

        def parameters():
            act.wait_ge(par_in, 16 * 5)
            act.activation(sm(S_DT), sm(S_LDT), ACT.Exp).then_inc(lam_ready, 1)
            act.wait_ge(ang_ready, 1)
            act.activation(sm(S_MAG), sm(S_T0), ACT.Exp).then_inc(lam_ready, 1)
            act.wait_ge(ang_ready, 2)
            act.activation(sm(S_SIN), sm(S_T1), ACT.Sin).then_inc(lam_ready, 1)
            act.activation(sm(S_COS), sm(S_T2), ACT.Sin).then_inc(lam_ready, 1)
            act.wait_ge(rope_ready, 1)
            act.activation(rope[:, :, :, :], rope[:, :, :, :], ACT.Sin).then_inc(rope_ready, 1)

        for s in steps:
            if s[0] == "param":
                (parameters, memory_squares)[s[1]]()
            if s[0] == "split":
                k = split_no[s]
                target_free(act, s)
                act.wait_ge(staged[k % 2], STAGED[s])
                act.activation(split_target(s)[0], split_source(s), ACT.Copy).then_inc(split_hi, 1)
            if s[0] == "xturn":
                _, tb, kh = s
                act.wait_ge(misc_out, misc_no[s] + 1)
                act.activation(nhl[:, 4 * kh:4 * kh + 4, tb, 0, :], nT[:, 4 * kh:4 * kh + 4, tb * P:(tb + 1) * P],
                               ACT.Copy).then_inc(nh_done, 1)
            if s[0] in MAIN:
                m = main_no[s]
                act.wait_ge(main_full, m + 1)
                src = main_ps[m % 2][:, :]
            if s[0] == "z":
                _, ct, hf = s
                act.wait_ge(sq_done, TB)
                act.activation(zT[:, ct, hf * HALF:(hf + 1) * HALF], src, ACT.Copy).then_inc(main_out, 1)
            elif s[0] == "qk":
                n = turn_no[(s[1], s[2])]
                if n >= 2:
                    act.wait_ge(rot_done, n - 1)
                if n == 0:
                    done_by_pe(act, ("bturn", S5T - 2))
                act.activation(qk[:, n % 2, :], src, ACT.Copy).then_inc(main_out, 1)
            elif s[0] == "vg":
                n = turn_no[(s[1], s[2])]
                if n >= 2:
                    done_by_pe(act, ("mix", *divmod(n - 2, TB)))
                    act.wait_ge(ret_done, n - 1)
                    act.wait_ge(vgate_done, n - 1)
                act.activation(sg[:, n % 2, 0:256], src[:, 256:512], ACT.Tanh, scale=0.5).then_inc(gsig_ready, 1)
                act.activation(vg[:, n % 2, :], src, ACT.Copy).then_inc(main_out, 1)
            elif s[0] == "gate":
                n = gate_no[s]
                if n >= 2:
                    act.wait_ge(p_out, n - 1)
                else:
                    act.wait_ge(vgate_done, 2 * TB)
                act.activation(sg[:, n % 2, :], src, ACT.Tanh, scale=0.5).then_inc(main_out, 1)
            elif s[0] == "turn":
                _, hp, tb = s
                n = turn_no[(hp, tb)]
                act.wait_ge(rot_done, n + 1)
                if n >= 2:
                    done_by_pe(act, ("mix", *divmod(n - 2, TB)))
                for h in range(2):
                    i = act.activation(kdec[:, n % 2, h * P:(h + 1) * P], qkr[:, 256 + h * P:256 + (h + 1) * P], ACT.Copy,
                                       scale=con[:, C_KF + 2 * hp + h:C_KF + 2 * hp + h + 1])
                i.then_inc(kdec_done, 1)
            elif s[0] == "mix":
                _, hp, tb = s
                n = turn_no[(hp, tb)]
                done_by_pe(act, s)
                if n:
                    done_by_pe(act, ("flip", *divmod(n - 1, TB)))
                for h in range(2):
                    src = misc_ps[misc_no[s] % 2][:, h * P:(h + 1) * P]
                    qf = con[:, C_QF + 2 * hp + h:C_QF + 2 * hp + h + 1]
                    act.activation(ret[:, h * P:(h + 1) * P], src, ACT.Copy, scale=qf)
                    if n or h:
                        act.wait_ge(retraw_done, 2 * n + h)
                    act.activation(junk[:, :], src, ACT.Square, scale=qf, accum_out=stat[:, 48 + h:49 + h]).then_inc(retraw_done, 1)
            elif s[0] == "ascore":
                act.wait_ge(misc_out, misc_no[s] + 1)
                act.activation(psc[:, :], psc[:, :], ACT.Exp, scale=MD ** -0.5).then_inc(exp_ready, 1)
            elif s[0] == "y" and s[1] % 4 == 3:
                ct, hf = s[1] // 4, s[2]
                act.wait_ge(ydu_ready, 2 * ct + hf + 1)
                u = zT[:, ct, hf * HALF:(hf + 1) * HALF]
                act.activation(u, u, ACT.Gelu_apprx_tanh).then_inc(gelu_ready, 1)
            elif s[0] == "glu":
                hf = s[1]
                done_by_pe(act, s)
                for o, ps in enumerate((misc_ps[misc_no[s] % 2], bu_ps[1])):
                    act.activation(zT[:, o, hf * HALF:(hf + 1) * HALF], ps[:, :], ACT.Tanh, scale=0.5).then_inc(glu_tanh, 1)

    @block.tensor
    def _(pe):
        ident = con[:, C_ID:C_ID + P]

        def free(s):
            n = misc_no[s]
            if n >= 2:
                pe.wait_ge(misc_out, n - 1)
            return misc_ps[n % 2]

        def main_free(s):
            m = main_no[s]
            if m >= 2:
                pe.wait_ge(main_out, m - 1)
            return main_ps[m % 2]

        def three(ps, a, b, first, last):
            pe.matmul(ps, a(0), b(0), start=first, stop=False)
            pe.matmul(ps, a(0), b(1), start=False, stop=False)
            return pe.matmul(ps, a(1), b(0), start=False, stop=last)

        def projection(unit, q):
            kind, arg, tb = unit[0], unit[1:-1], unit[-1]
            if q == 0:
                pe.wait_ge(nl_done, 2 * TB)
                main_free(unit)
                weights(pe, kind, arg[0] if kind != "gate" else arg)
            w = wring[BUFFER[LOAD_NO[(kind, arg[0] if kind != "gate" else arg)]]]
            ps = main_ps[main_no[unit] % 2]
            for kd in range(q * KD // QUARTERS, (q + 1) * KD // QUARTERS):
                mm = three(ps[:, :], lambda i: nhl[:, kd, tb, i, :], lambda i: w[:, kd, i, :], kd == 0, kd == KD - 1)
            return mm

        pe.wait_ge(con_in, 16)
        for s in steps:
            k = s[0]
            if k == "xturn":
                _, tb, kh = s
                ps = free(s)
                pe.wait_ge(n_ready, tb + 1)
                for i in range(4):
                    mm = pe.transpose(ps[:, i * P:(i + 1) * P], xs[:, tb, (4 * kh + i) * P:(4 * kh + i + 1) * P], ident)
                mm.then_inc(misc_full, 1)
            elif k == "mturn":
                _, mt, kh = s
                ps = free(s)
                pe.wait_ge(n_ready, TB + mt + 1)
                for i in range(4):
                    mm = pe.transpose(ps[:, i * P:(i + 1) * P], mem_x[:, mt, (4 * kh + i) * P:(4 * kh + i + 1) * P], ident)
                mm.then_inc(misc_full, 1)
            elif k == "bturn":
                ps = free(s)
                pe.wait_ge(bb_ready, 1)
                for i in range(4):
                    mm = pe.transpose(ps[:, i * P:(i + 1) * P], bsrc[:, i // 2, s[1] + i % 2, :], ident)
                mm.then_inc(misc_full, 1)
            elif k == "z":
                _, ct, hf = s
                w = wfull
                pe.wait_ge(wfull_in, 16)
                ps = main_free(s)
                pe.wait_ge(misc_out, misc_no[("xturn", 4 * hf + 3, 1)] + 1)
                for kd in range(KD):
                    mm = pe.matmul(ps[:, :], w[:, kd, ct * P:(ct + 1) * P], nT[:, kd, hf * HALF:(hf + 1) * HALF],
                                   start=kd == 0, stop=kd == KD - 1)
                mm.then_inc(main_full, 1)
            elif k == "open":
                projection(*s[1:])
            elif k in ("qk", "vg"):
                projection(s, QUARTERS - 1).then_inc(main_full, 1)
            elif k == "mk":
                w = wfull
                pe.wait_ge(wfull_in, 32)
                ps = free(s)
                pe.wait_ge(misc_out, misc_no[("mturn", 1, 1)] + 1)
                for kd in range(KD):
                    mm = pe.matmul(ps[:, 0:MEM], w[:, kd, s[1] * P:(s[1] + 1) * P], memT[:, kd, :],
                                   start=kd == 0, stop=kd == KD - 1)
                mm.then_inc(misc_full, 1)
            elif k == "mv":
                w = wfull
                pe.wait_ge(wfull_in, 32)
                ps = free(s)
                for kd in range(KD):
                    mm = pe.matmul(ps[:, 0:256], memT[:, kd, s[1] * P:(s[1] + 1) * P], w[:, kd, 256:512],
                                   start=kd == 0, stop=kd == KD - 1)
                mm.then_inc(misc_full, 1)
            elif k == "turn":
                _, hp, tb = s
                ps = free(s)
                pe.wait_ge(rot_done, turn_no[(hp, tb)] + 1)
                for i in range(4):
                    mm = pe.transpose(ps[:, i * P:(i + 1) * P], qkr[:, i * P:(i + 1) * P], ident)
                mm.then_inc(misc_full, 1)
            elif k == "score":
                _, hp, tb = s
                n = turn_no[(hp, tb)]
                ps = free(s)
                pe.wait_ge(misc_out, misc_no[("turn", hp, tb)] + 1)
                for h in range(2):
                    mm = pe.matmul(ps[:, h * P:(h + 1) * P], qkT[:, n % 2, 256 + h * P:256 + (h + 1) * P],
                                   qkT[:, n % 2, h * P:(h + 1) * P], start=True, stop=True)
                mm.then_inc(misc_full, 1)
            elif k == "mix":
                _, hp, tb = s
                n = turn_no[(hp, tb)]
                ps = free(s)
                pe.wait_ge(misc_out, misc_no[("score", hp, tb)] + 1)
                pe.wait_ge(kdec_done, n + 1)
                pe.wait_ge(main_out, main_no[("vg", hp, tb)] + 1)
                for h in range(2):
                    v = vg[:, n % 2, h * P:(h + 1) * P]
                    pe.matmul(ps[:, h * P:(h + 1) * P], sT[:, h * P:(h + 1) * P], v, start=True, stop=tb == 0)
                    if tb:
                        pe.matmul(ps[:, h * P:(h + 1) * P], qkT[:, n % 2, h * P:(h + 1) * P],
                                  state[:, 2 * hp + h, :], start=False, stop=True)
                    mm = pe.matmul(ps[:, 256 + h * P:256 + (h + 1) * P], kdec[:, n % 2, h * P:(h + 1) * P], v,
                                   start=True, stop=True)
                mm.then_inc(misc_full, 1)
            elif k == "flip":
                _, hp, tb = s
                ps = free(s)
                pe.wait_ge(ret_done, turn_no[(hp, tb)] + 1)
                for h in range(2):
                    mm = pe.transpose(ps[:, h * P:(h + 1) * P], ret[:, h * P:(h + 1) * P], ident)
                mm.then_inc(misc_full, 1)
            elif k == "ascore":
                _, tb, mp = s
                ps = free(s)
                pe.wait_ge(main_out, main_no[("z", 3, 1)] + 1)
                pe.wait_ge(misc_out, misc_no[("mv", 1)] + 1)
                for h in range(2):
                    mm = pe.matmul(ps[:, h * MEM:(h + 1) * MEM],
                                   zT[:, 2 + mp, tb * P:(tb + 1) * P], kmT[:, mp, h, :], start=True, stop=True)
                mm.then_inc(misc_full, 1)
            elif k == "aturn":
                _, tb, mp = s
                ps = free(s)
                pe.wait_ge(exp_ready, chain_no[(tb, mp)] + 1)
                for i in range(4):
                    mm = pe.transpose(ps[:, i * P:(i + 1) * P], psc[:, i * P:(i + 1) * P], ident)
                mm.then_inc(misc_full, 1)
            elif k == "amix":
                _, tb, mp = s
                ps = free(s)
                pe.wait_ge(misc_out, misc_no[("aturn", tb, mp)] + 1)
                for h in range(2):
                    for mt in range(2):
                        mm = pe.matmul(ps[:, h * MD:(h + 1) * MD], pT[:, (2 * h + mt) * P:(2 * h + mt + 1) * P],
                                       vm[:, mt, (2 * mp + h) * MD:(2 * mp + h + 1) * MD],
                                       start=mt == 0, stop=mt == 1)
                mm.then_inc(misc_full, 1)
            elif k == "aflip":
                _, tb, mp = s
                ps = free(s)
                pe.wait_ge(misc_out, misc_no[("amix", tb, mp)] + 1)
                pe.transpose(ps[:, 0:P], mo[:, :], ident).then_inc(misc_full, 1)
            elif k == "bu":
                _, st, hf = s
                n = bu_no[s]
                if n:
                    pe.wait_ge(bu_out, n)
                pe.wait_ge(misc_out, misc_no[("bturn", 6)] + 1)
                pe.wait_ge(main_out, main_no[("z", 3, 1)] + 1)
                for c in range(2):
                    mm = pe.matmul(bu_ps[c][:, :], bbT[:, c, st, :], zT[:, st // 4, hf * HALF:(hf + 1) * HALF],
                                   start=True, stop=True)
                mm.then_inc(bu_full, 1)
            elif k == "y":
                _, st, hf = s
                pe.wait_ge(xst_ready, 2 * st + hf + 1)
                pe.wait_ge(cneg_ready, 1)
                if st == 4:
                    pe.wait_ge(ydu_ready, hf + 1)
                for c in range(2):
                    mm = pe.matmul(y_ps[hf][:, :], cT[:, c, st, :], ysc[:, hf, c, :],
                                   start=st % 4 == 0 and c == 0, stop=st % 4 == 3 and c == 1)
                mm.then_inc(y_full, 1)
            elif k == "glu":
                hf = s[1]
                ps = free(s)
                pe.wait_ge(gelu_ready, 4)
                if hf:
                    pe.wait_ge(misc_out, misc_no[("glu", 0)] + 1)
                for bank, col in ((ps, 2), (bu_ps[1], 3), (bu_ps[0], 0), (y_ps[hf], 1)):
                    for c in range(2):
                        mm = pe.matmul(bank[:, :], wglu[:, c, col * P:(col + 1) * P],
                                       zT[:, c, hf * HALF:(hf + 1) * HALF], start=c == 0, stop=c == 1)
                mm.then_inc(misc_full, 1)
            elif k == "gate":
                _, dh, br, tb = s
                n = gate_no[s]
                projection(s, QUARTERS - 1).then_inc(main_full, 1)
                if n >= 2:
                    pe.wait_ge(p_out, n - 1)
                src, first, rows = ((zhl[:, 0:2], 4, 2), (zhl[:, 2:4], 6, 2), (retT, 0, 4))[br]
                if tb == 0 and dh == 0:
                    last = (("glu", 1), ("aflip", TB - 1, 1), ("flip", 1, TB - 1))[br]
                    pe.wait_ge(misc_out, misc_no[last] + 1)
                    branch_weights(pe, first + rows - 1)
                cols = slice(dh * HALF, (dh + 1) * HALF)
                for i in range(rows):
                    mm = three(p_ps[n % 2][:, :], lambda c: src[:, i, tb, c, :], lambda c: wbr[:, first + i, c, cols],
                               i == 0, i == rows - 1)
                mm.then_inc(p_full, 1)
            elif k == "gturn":
                _, dh, tb = s
                ps = free(s)
                pe.wait_ge(merged_done, dh * 2 * TB + TB + tb + 1)
                for i in range(4):
                    mm = pe.transpose(ps[:, i * P:(i + 1) * P], merged[:, tb, i * P:(i + 1) * P], ident)
                mm.then_inc(misc_full, 1)
            elif k == "out":
                _, dh, tb = s
                w = weights(pe, "out", dh)
                ps = free(s)
                pe.wait_ge(misc_out, misc_no[("gturn", 1, TB - 1)] + 1)
                for kd in range(KD):
                    src = merT_lo if kd < 4 else merT_hi
                    mm = three(ps[:, :], lambda i: src[:, kd % 4, tb, i, :], lambda i: w[:, kd, i, :],
                               kd == 0, kd == KD - 1)
                mm.then_inc(misc_full, 1)


    @block.vector
    def _(dve):
        chain = 0

        def link(i):
            nonlocal chain
            i.then_inc(dchain, 1)
            chain += 1
            dve.wait_ge(dchain, chain)

        sm = lambda k: small[:, k, :]
        tt, ts, stt = dve.tensor_tensor, dve.tensor_scalar, dve.scalar_tensor_tensor

        def reduced(dst_sin, dst_cos, ang, tmp):
            link(ts(tmp, ang, 1.0 / (2.0 * math.pi), MAGIC, ALU.mult, ALU.add))
            link(ts(tmp, tmp, -MAGIC, None, ALU.add))
            link(stt(dst_sin, tmp, -TWO_PI_HI, ang, ALU.mult, ALU.add))
            link(stt(dst_sin, tmp, -TWO_PI_MID, dst_sin, ALU.mult, ALU.add))
            link(stt(dst_sin, tmp, -TWO_PI_LO, dst_sin, ALU.mult, ALU.add))
            link(ts(dst_sin, dst_sin, PI_BELOW, -PI_BELOW, ALU.min, ALU.max))
            link(stt(dst_cos, dst_sin, -1.0, dst_sin, ALU.mult, ALU.max))
            return ts(dst_cos, dst_cos, -1.0, math.pi / 2, ALU.mult, ALU.add)

        def norm(tb):
            dve.wait_ge(rs_done, tb + 1)
            ts(xs[:, tb, :], xs[:, tb, :], stat[:, 16 + tb:17 + tb], None, ALU.mult).then_inc(n_ready, 1)

        def parameters():
            dve.wait_ge(lam_ready, 1)
            tt(sm(S_T0), sm(S_ARE), sm(S_DT), ALU.mult).then_inc(ang_ready, 1)
            link(tt(sm(S_TH), sm(S_AIM), sm(S_DT), ALU.mult))
            reduced(sm(S_T1), sm(S_T2), sm(S_TH), sm(S_T3)).then_inc(ang_ready, 1)
            link(dve.tensor_copy(sm(S_POS), sm(S_POSI).bitcast(I32)))
            ang, tmp = btmp[:, 0, :, 0:64], btmp[:, 1, :, 0:64]
            inv = con[:, C_INV:C_INV + 64].unsqueeze(1).to_broadcast([P, TB, 64])
            pos = sm(S_POS).unsqueeze(2).to_broadcast([P, TB, 64])
            link(tt(ang, pos, inv, ALU.mult))
            reduced(rope[:, 1, :, :], rope[:, 0, :, :], ang, tmp).then_inc(rope_ready, 1)
            dve.wait_ge(rope_ready, 1)
            dve.wait_ge(lam_ready, 4)
            link(tt(sm(S_LRE), sm(S_MAG), sm(S_COS), ALU.mult))
            link(tt(sm(S_LIM), sm(S_MAG), sm(S_SIN), ALU.mult))
            link(ts(sm(S_LRE), sm(S_LRE), -1.0, None, ALU.add))
            link(tt(sm(S_T0), sm(S_ARE), sm(S_ARE), ALU.mult))
            link(tt(sm(S_T3), sm(S_AIM), sm(S_AIM), ALU.mult))
            link(tt(sm(S_DEN), sm(S_T0), sm(S_T3), ALU.add))
            link(dve.reciprocal(sm(S_DEN), sm(S_DEN)))
            link(tt(sm(S_T0), sm(S_LRE), sm(S_ARE), ALU.mult))
            link(tt(sm(S_T3), sm(S_LIM), sm(S_AIM), ALU.mult))
            link(tt(sm(S_T0), sm(S_T0), sm(S_T3), ALU.add))
            link(tt(sm(S_CR), sm(S_T0), sm(S_DEN), ALU.mult))
            link(tt(sm(S_T0), sm(S_LIM), sm(S_ARE), ALU.mult))
            link(tt(sm(S_T3), sm(S_LRE), sm(S_AIM), ALU.mult))
            link(tt(sm(S_T0), sm(S_T0), sm(S_T3), ALU.subtract))
            link(tt(sm(S_CI), sm(S_T0), sm(S_DEN), ALU.mult))

        def input_matrices():
            dve.wait_ge(sq_done, TB + 2)
            dve.wait_ge(b_in, 32)
            cr = sm(S_CR).unsqueeze(2).to_broadcast([P, S5T, P])
            ci = sm(S_CI).unsqueeze(2).to_broadcast([P, S5T, P])
            re, im, t0, t1 = bsrc[:, 0, :, :], bsrc[:, 1, :, :], btmp[:, 0, :, :], btmp[:, 1, :, :]
            tt(t0, im, ci, ALU.mult)
            link(tt(t1, re, ci, ALU.mult))
            tt(re, re, cr, ALU.mult)
            link(tt(im, im, cr, ALU.mult))
            tt(re, re, t0, ALU.subtract)
            tt(im, im, t1, ALU.add).then_inc(bb_ready, 1)
            dve.wait_ge(c_in, 48)
            ts(cT[:, 1, :, :], cT[:, 1, :, :], -1.0, None, ALU.mult).then_inc(cneg_ready, 1)
            dve.tensor_copy(levels[:, 0, 0, :], sm(S_COS))
            link(dve.tensor_copy(levels[:, 1, 0, :], sm(S_SIN)))
            for k in range(8):
                cn, sn, c2, s2 = levels[:, 0, k, :], levels[:, 1, k, :], levels[:, 0, k + 1, :], levels[:, 1, k + 1, :]
                tt(sm(S_T0), sn, sn, ALU.mult)
                tt(sm(S_T1), cn, sn, ALU.mult)
                link(tt(c2, cn, cn, ALU.mult))
                tt(c2, c2, sm(S_T0), ALU.subtract)
                link(ts(s2, sm(S_T1), 2.0, None, ALU.mult))
            dve.memset(btab[:, 0, :, 0:1], 1.0)
            link(dve.memset(btab[:, 1, :, 0:1], 0.0))
            for k in range(4):
                n = 1 << k
                cn = levels[:, 0, k, :].unsqueeze(2).to_broadcast([P, S5T, n])
                sn = levels[:, 1, k, :].unsqueeze(2).to_broadcast([P, S5T, n])
                c, s_, t0, t1 = btab[:, 0, :, 0:n], btab[:, 1, :, 0:n], btmp[:, 0, :, 0:n], btmp[:, 1, :, 0:n]
                tt(t0, s_, sn, ALU.mult)
                tt(t1, c, sn, ALU.mult)
                tt(btab[:, 0, :, n:2 * n], c, cn, ALU.mult)
                link(tt(btab[:, 1, :, n:2 * n], s_, cn, ALU.mult))
                tt(btab[:, 0, :, n:2 * n], btab[:, 0, :, n:2 * n], t0, ALU.subtract)
                link(tt(btab[:, 1, :, n:2 * n], btab[:, 1, :, n:2 * n], t1, ALU.add))
            for m in range(2):
                dve.wait_ge(rs_done, TB + m + 1)
                ts(mem_x[:, m, :], mem_x[:, m, :], stat[:, 24 + m:25 + m], None, ALU.mult).then_inc(n_ready, 1)

        def tables(st, part):
            if part:
                pass
            elif st:
                dve.wait_ge(xst_ready, 2 * st)
            else:
                done_by_pe(dve, ("z", 3, 1))
                dve.wait_ge(nl_done, 2 * TB)
            c, s_ = tab[:, 0, :], tab[:, 1, :]
            if part == 0:
                link(dve.tensor_copy(tab[:, :, 0:16], btab[:, :, st, :]))
            for k in ((4, 5, 6), (7,), (8,))[part]:
                n = 1 << k
                cn, sn = levels[:, 0, k, st:st + 1], levels[:, 1, k, st:st + 1]
                tmp_c, tmp_s = prod[:, 0, 0:n], prod[:, 1, 0:n]
                ts(tmp_c, s_[:, 0:n], sn, None, ALU.mult)
                link(ts(tmp_s, c[:, 0:n], sn, None, ALU.mult))
                stt(c[:, n:2 * n], c[:, 0:n], cn, tmp_c, ALU.mult, ALU.subtract)
                link(stt(s_[:, n:2 * n], s_[:, 0:n], cn, tmp_s, ALU.mult, ALU.add))

        def pair_out(hi, lo, src, factor=None):
            if factor is None:
                link(dve.tensor_copy(hi, src))
                return tt(lo, src, hi, ALU.subtract)
            link(ts(hi, src, factor, None, ALU.mult))
            return stt(lo, src, factor, hi, ALU.mult, ALU.subtract)

        def copy_out(s, dst, cols=HALF):
            n = misc_no[s]
            dve.wait_ge(misc_full, n + 1)
            dve.tensor_copy(dst, misc_ps[n % 2][:, 0:cols]).then_inc(misc_out, 1)

        dve.wait_ge(gain_in, 16 * 2)
        norm(0)
        for s in steps:
            k = s[0]
            if k in ("xturn", "mturn"):
                n = misc_no[s]
                _, b, kh = s
                if k == "xturn" and kh == 0 and b + 1 < TB:
                    norm(b + 1)
                dve.wait_ge(misc_full, n + 1)
                dst = (nT if k == "xturn" else memT)[:, 4 * kh:4 * kh + 4, b * P:(b + 1) * P]
                g = gains[:, 0 if k == "xturn" else 1, 4 * kh:4 * kh + 4].unsqueeze(2).to_broadcast([P, 4, P])
                tt(dst, misc_ps[n % 2][:, :].rearrange("p (k t) -> p k t", k=4), g, ALU.mult).then_inc(misc_out, 1)
            elif k == "param":
                (parameters, input_matrices)[s[1]]()
            elif k == "split":
                n = split_no[s]
                dve.wait_ge(split_hi, n + 1)
                hi, lo = split_target(s)
                tt(lo, split_source(s), hi, ALU.subtract).then_inc(split_done, 1)
            elif k == "bturn":
                n = misc_no[s]
                dve.wait_ge(misc_full, n + 1)
                dve.tensor_copy(bbT[:, :, s[1]:s[1] + 2, :],
                                misc_ps[n % 2][:, :].rearrange("p (c s q) -> p c s q", c=2, s=2)).then_inc(misc_out, 1)
            elif k == "mk":
                n = misc_no[s]
                link(dve.memset(kmT[:, s[1], :, :], 0.0))
                dve.wait_ge(misc_full, n + 1)
                for h in range(2):
                    rows = slice(h * MD, (h + 1) * MD)
                    i = dve.tensor_copy(kmT[rows, s[1], h, :], misc_ps[n % 2][rows, 0:MEM])
                i.then_inc(misc_out, 1)
            elif k == "mv":
                copy_out(s, vm[:, s[1], :], 256)
            elif k == "turn":
                _, hp, tb = s
                n = turn_no[(hp, tb)]
                if n >= 2:
                    done_by_pe(dve, ("mix", *divmod(n - 2, TB)))
                copy_out(s, qkT[:, n % 2, :])
            elif k == "score":
                _, hp, tb = s
                n = turn_no[(hp, tb)]
                if n:
                    done_by_pe(dve, ("mix", *divmod(n - 1, TB)))
                dve.wait_ge(misc_full, misc_no[s] + 1)
                dec = con[:, C_DEC + 2 * hp * P:C_DEC + (2 * hp + 2) * P]
                tt(sT[:, :], misc_ps[misc_no[s] % 2][:, 0:256], dec, ALU.mult).then_inc(misc_out, 1)
            elif k == "mix":
                _, hp, tb = s
                n = turn_no[(hp, tb)]
                dve.wait_ge(misc_full, misc_no[s] + 1)
                ps = misc_ps[misc_no[s] % 2]
                dve.wait_ge(retraw_done, 2 * n + 2)
                for h in range(2):
                    kv, st = ps[:, 256 + h * P:256 + (h + 1) * P], state[:, 2 * hp + h, :]
                    if tb == 0:
                        i = dve.tensor_copy(st, kv)
                    else:
                        i = stt(st, st, GAMMA[2 * hp + h] ** P, kv, ALU.mult, ALU.add)
                i.then_inc(misc_out, 1)
            elif k == "flip":
                _, hp, tb = s
                n = misc_no[s]
                dve.wait_ge(misc_full, n + 1)
                if n == misc_no[("flip", 0, 0)]:
                    done_by_pe(dve, ("mv", 1))
                dst = retT[:, 2 * hp:2 * hp + 2, tb, :, :]
                src = misc_ps[n % 2][:, 0:256].rearrange("p (h t) -> p h t", h=2)
                pair_out(dst[:, :, 0, :], dst[:, :, 1, :], src).then_inc(misc_out, 1)
            elif k == "ascore":
                _, tb, mp = s
                c = chain_no[(tb, mp)]
                dve.wait_ge(misc_full, misc_no[s] + 1)
                ps = misc_ps[misc_no[s] % 2][:, :].rearrange("p (h m) -> p h m", h=2)
                link(dve.tensor_reduce(stat[:, 52:54], ps, AX.X, ALU.max))
                tt(psc[:, :].rearrange("p (h m) -> p h m", h=2), ps,
                   stat[:, 52:54].unsqueeze(2).to_broadcast([P, 2, MEM]), ALU.subtract).then_inc(misc_out, 1)
            elif k == "aturn":
                _, tb, mp = s
                dve.wait_ge(exp_ready, chain_no[(tb, mp)] + 1)
                link(dve.tensor_reduce(stat[:, 54:56], psc[:, :].rearrange("p (h m) -> p h m", h=2), AX.X, ALU.add))
                link(dve.reciprocal(stat[:, 56:58], stat[:, 54:56]))
                copy_out(s, pT[:, :])
            elif k == "amix":
                n = misc_no[s]
                dve.wait_ge(misc_full, n + 1)
                tt(mo[:, :].rearrange("p (h d) -> p h d", h=2), misc_ps[n % 2][:, 0:P].rearrange("p (h d) -> p h d", h=2),
                   stat[:, 56:58].unsqueeze(2).to_broadcast([P, 2, MD]), ALU.mult).then_inc(misc_out, 1)
            elif k == "aflip":
                _, tb, mp = s
                n = misc_no[s]
                dve.wait_ge(misc_full, n + 1)
                pair_out(zhl[:, 2 + mp, tb, 0, :], zhl[:, 2 + mp, tb, 1, :], misc_ps[n % 2][:, 0:P]).then_inc(misc_out, 1)
            elif k == "bu":
                _, st, hf = s
                n = bu_no[s]
                c, sn_t = tab[:, 0, :], tab[:, 1, :]
                dve.wait_ge(bu_full, n + 1)
                tt(prod[:, 0, :], bu_ps[0][:, :], c, ALU.mult)
                tt(prod[:, 1, :], bu_ps[1][:, :], sn_t, ALU.mult)
                tt(prod[:, 2, :], bu_ps[1][:, :], c, ALU.mult)
                tt(prod[:, 3, :], bu_ps[0][:, :], sn_t, ALU.mult).then_inc(bu_out, 1)
            elif k == "tables":
                tables(*s[1:])
            elif k == "scan":
                _, st, hf = s
                dve.wait_ge(bu_out, bu_no[("bu", st, hf)] + 1)
                tt(prod[:, 0, :], prod[:, 0, :], prod[:, 1, :], ALU.add)
                link(tt(prod[:, 2, :], prod[:, 2, :], prod[:, 3, :], ALU.subtract))
                if st:
                    dve.wait_ge(y_full, 2 * (st - 1) + hf + 1)
                mag = small[:, S_MAG, st:st + 1].to_broadcast([P, HALF])
                for c2 in range(2):
                    init = 0.0 if hf == 0 else small[:, S_CN + c2, 1:2]
                    i = dve.tensor_tensor_scan(ysc[:, hf, c2, :], mag, prod[:, 2 * c2, :], init, ALU.mult, ALU.add)
                link(i)
            elif k == "states":
                _, st, hf = s
                n = bu_no[("bu", st, hf)]
                c, sn_t = tab[:, 0, :], tab[:, 1, :]
                tt(prod[:, 0, :], ysc[:, hf, 0, :], c, ALU.mult)
                tt(prod[:, 1, :], ysc[:, hf, 1, :], sn_t, ALU.mult)
                tt(prod[:, 2, :], ysc[:, hf, 0, :], sn_t, ALU.mult)
                link(tt(prod[:, 3, :], ysc[:, hf, 1, :], c, ALU.mult))
                link(tt(ysc[:, hf, 0, :], prod[:, 0, :], prod[:, 1, :], ALU.subtract))
                tt(ysc[:, hf, 1, :], prod[:, 2, :], prod[:, 3, :], ALU.add).then_inc(xst_ready, 1)
                dve.wait_ge(xst_ready, n + 1)
                if hf == 0:
                    cn, sn = levels[:, 0, 0, st:st + 1], levels[:, 1, 0, st:st + 1]
                    xr_, xi_ = ysc[:, 0, 0, HALF - 1:HALF], ysc[:, 0, 1, HALF - 1:HALF]
                    tt(small[:, S_T0, 0:1], xi_, sn, ALU.mult)
                    link(tt(small[:, S_T1, 0:1], xr_, sn, ALU.mult))
                    stt(small[:, S_CN, 1:2], xr_, cn, small[:, S_T0, 0:1], ALU.mult, ALU.subtract)
                    link(stt(small[:, S_SN, 1:2], xi_, cn, small[:, S_T1, 0:1], ALU.mult, ALU.add))
            elif k == "y" and s[1] % 4 == 3:
                ct, hf = s[1] // 4, s[2]
                dve.wait_ge(y_full, 2 * s[1] + hf + 1)
                u = zT[:, ct, hf * HALF:(hf + 1) * HALF]
                stt(u, u, small[:, S_D, ct:ct + 1], y_ps[hf][:, :], ALU.mult, ALU.add).then_inc(ydu_ready, 1)
            elif k == "glu":
                hf = s[1]
                dve.wait_ge(glu_tanh, 2 * hf + 2)
                done_by_pe(dve, s)
                both = zT[:, 0:2, hf * HALF:(hf + 1) * HALF]
                link(ts(both, both, 1.0, 0.5, ALU.add, ALU.mult))
                for o, bank in enumerate((bu_ps[0], y_ps[hf])):
                    i = tt(prod[:, o, :], zT[:, o, hf * HALF:(hf + 1) * HALF], bank[:, :], ALU.mult)
                link(i)
                dst = zhl[:, 0:2, 4 * hf:4 * hf + 4, :, :]
                for o in range(2):
                    src = prod[:, o, :].rearrange("p (b t) -> p b t", b=4)
                    i = pair_out(dst[:, o, :, 0, :], dst[:, o, :, 1, :], src)
                i.then_inc(misc_out, 1)
            elif k == "gate":
                _, dh, br, tb = s
                n = gate_no[s]
                dve.wait_ge(p_full, n + 1)
                dve.wait_ge(main_out, main_no[s] + 1)
                if br == 0:
                    if dh:
                        done_by_pe(dve, ("gturn", 0, tb))
                    elif tb == 0:
                        done_by_pe(dve, ("glu", 1))
                    dst = merged[:, tb, :]
                else:
                    if (dh, br, tb) == (0, 1, 0):
                        done_by_pe(dve, ("flip", 1, TB - 1))
                        done_by_pe(dve, ("aflip", TB - 1, 1))
                    if n - TB * (dh + 1) >= 2:
                        dve.wait_ge(merged_done, n - TB * (dh + 1) - 1)
                    dst = gp[:, n % 2, :]
                i = stt(dst, sg[:, n % 2, :], 1.0, p_ps[n % 2][:, :], ALU.add, ALU.mult)
                i.then_inc(p_out, 1)
            elif k == "gturn":
                _, dh, tb = s
                n = misc_no[s]
                dve.wait_ge(misc_full, n + 1)
                dst = (merT_lo, merT_hi)[dh][:, :, tb, :, :]
                src = misc_ps[n % 2][:, :].rearrange("p (k t) -> p k t", k=4)
                pair_out(dst[:, :, 0, :], dst[:, :, 1, :], src, 0.5).then_inc(misc_out, 1)
            elif k == "out":
                _, dh, tb = s
                n = misc_no[s]
                j = dh * TB + tb
                dve.wait_ge(misc_full, n + 1)
                dve.wait_ge(xr_in[j % 2], 16 * (j // 2 + 1))
                tt(h_sb[:, tb, dh * HALF:(dh + 1) * HALF], misc_ps[n % 2][:, :], xr[:, j % 2, :],
                   ALU.add).then_inc(misc_out, 1)
    ctx.close()


PH, PK, NK = 8, 16, 128
HC = 2 * PH
PAIRS = [(0, 1, 16), (1, 1, 8), (2, 1, 5), (3, 1, 4), (4, 1, 3), (5, 3, 2), (8, 8, 1)]
NCAND = sum(na * nb for _, na, nb in PAIRS)
NEG = -3.0e38
CH = NK
GT = 16
WT = 64
CG = 4


def build_scores(nc, ins, h_sb, xh, xl, s_sb, mem_map):
    ctx = ExitStack()
    at = dict(mem_map)

    def sb(region, name, shape, dt=F32):
        size = int(np.prod(shape[1:])) * (2 if dt == BF16 else 4)
        off = at[region]
        at[region] = off + (size + 31) // 32 * 32
        assert at[region] <= mem_map[region] + mem_map[region + "_size"], (region, name)
        return nc.alloc_sbuf_tensor_at(name, shape, dt, offset=off)

    def sem(name):
        return ctx.enter_context(nc.semaphore(name))

    ident = sb("const", "ident2", [P, P])
    gain = sb("const", "gain2", [P, KD])
    stat = sb("const", "stat2", [P, 64])
    xnT = sb("xnt", "xnT", [P, KD, SEQ])
    wq = [sb("wq", f"wq{i}", [P, KD, 256]) for i in range(2)]
    keys = sb("keys", "keys", [P, HC, NK])
    qT = sb("qt", "qT", [P, 2, SEQ])
    xn = nc.alloc_sbuf_tensor_at("xn", [P, 2, D], F32, offset=mem_map["s"])
    junk = nc.alloc_sbuf_tensor_at("junk2", [P, 2, D], F32, offset=mem_map["s"] + 8192)
    main_ps = [ctx.enter_context(nc.psum_tensor(f"q_ps{i}", [P, HALF], F32)) for i in range(2)]
    misc_ps = [ctx.enter_context(nc.psum_tensor(f"t_ps{i}", [P, HALF], F32)) for i in range(2)]
    par_in, keys_in = sem("par2_in"), sem("keys_in")
    wq_in = [sem(f"wq_in{i}") for i in range(2)]
    sq_done, rs_done, xn_ready = sem("sq2_done"), sem("rs2_done"), sem("xn_ready")
    turned, turned_out = sem("turned"), sem("turned_out")
    hi_done, lo_done = sem("xh_done"), sem("xl_done")
    q_full, q_out = sem("q_full"), sem("q_out")
    s_full, s_out = sem("s_full"), sem("s_out")
    half_set, pstep = sem("half_set"), sem("pool_step2")
    turns = [(tb, kh) for tb in range(TB) for kh in range(2)]
    block = ctx.enter_context(nc.Block())

    @block.sync
    def _(sp):
        sp.dma_start(ident[:, :], ins["consts"][:, 0:P]).then_inc(par_in, 16)
        sp.dma_start(gain[:, :], ins["norm_ffn"]).then_inc(par_in, 16)
        w = ins["peer_w_q"].rearrange("(k p) n -> p k n", p=P)
        for n in range(HC // 2):
            if n >= 2:
                sp.wait_ge(q_full, 4 * (n - 1))
            sp.dma_start(wq[n % 2][:, :, :], w[:, :, n * 256:(n + 1) * 256]).then_inc(wq_in[n % 2], 16)
            if n == 0:
                sp.dma_start(keys[:, :, :], ins["peer_keys"]).then_inc(keys_in, 16)

    @block.gpsimd
    def _(pool):
        pool.memset(stat[:, 32:33], -0.5).then_inc(half_set, 1)
        pool.wait_ge(half_set, 1)
        for tb in range(TB):
            pool.wait_ge(sq_done, tb + 1)
            pool.tensor_scalar(stat[:, tb:tb + 1], stat[:, tb:tb + 1], 1.0 / D, EPS, ALU.mult, ALU.add).then_inc(pstep, 1)
            pool.wait_ge(pstep, tb + 1)
            pool.tensor_tensor(stat[:, 16 + tb:17 + tb], stat[:, tb:tb + 1], stat[:, 32:33], ALU.pow).then_inc(rs_done, 1)
        for n, (tb, kh) in enumerate(turns):
            pool.wait_ge(hi_done, n + 1)
            part = (slice(None), slice(4 * kh, 4 * kh + 4), slice(tb * P, (tb + 1) * P))
            pool.tensor_tensor(xl[part], xnT[part], xh[part], ALU.subtract).then_inc(lo_done, 1)

    @block.scalar
    def _(act):
        for tb in range(TB):
            if tb >= 2:
                act.wait_ge(sq_done, tb - 1)
            act.activation(junk[:, tb % 2, :], h_sb[:, tb, :], ACT.Square, accum_out=stat[:, tb:tb + 1]).then_inc(sq_done, 1)
        for n, (tb, kh) in enumerate(turns):
            act.wait_ge(turned_out, n + 1)
            part = (slice(None), slice(4 * kh, 4 * kh + 4), slice(tb * P, (tb + 1) * P))
            act.activation(xh[part], xnT[part], ACT.Copy).then_inc(hi_done, 1)
        for hc in range(HC):
            for hf in range(2):
                n = 2 * hc + hf
                act.wait_ge(q_full, n + 1)
                if hc >= 2:
                    act.wait_ge(s_full, 2 * (hc - 1))
                act.activation(qT[:, hc % 2, hf * HALF:(hf + 1) * HALF], main_ps[n % 2][:, :], ACT.Copy).then_inc(q_out, 1)

    @block.tensor
    def _(pe):
        pe.wait_ge(par_in, 32)
        for n, (tb, kh) in enumerate(turns):
            pe.wait_ge(xn_ready, tb + 1)
            if n >= 2:
                pe.wait_ge(turned_out, n - 1)
            for i in range(4):
                mm = pe.transpose(misc_ps[n % 2][:, i * P:(i + 1) * P],
                                  xn[:, tb % 2, (4 * kh + i) * P:(4 * kh + i + 1) * P], ident[:, :])
            mm.then_inc(turned, 1)

        def scores(hc):
            pe.wait_ge(keys_in, 16)
            for g in range(2):
                n = 2 * hc + g
                if n >= 2:
                    pe.wait_ge(s_out, n - 1)
                else:
                    pe.wait_ge(turned_out, 2 * TB)
                pe.wait_ge(q_out, 2 * hc + g + 1)
                for i in range(4):
                    tb = 4 * g + i
                    mm = pe.matmul(misc_ps[n % 2][:, i * P:(i + 1) * P], qT[:, hc % 2, tb * P:(tb + 1) * P],
                                   keys[:, hc, :], start=True, stop=True)
                mm.then_inc(s_full, 1)

        for hc in range(HC):
            for hf in range(2):
                n = 2 * hc + hf
                pe.wait_ge(wq_in[hc // 2 % 2], 16 * (hc // 4 + 1))
                pe.wait_ge(turned_out, 8 * hf + 8)
                if n >= 2:
                    pe.wait_ge(q_out, n - 1)
                for kd in range(KD):
                    mm = pe.matmul(main_ps[n % 2][:, :], wq[hc // 2 % 2][:, kd, (hc % 2) * P:(hc % 2 + 1) * P],
                                   xnT[:, kd, hf * HALF:(hf + 1) * HALF], start=kd == 0, stop=kd == KD - 1)
                mm.then_inc(q_full, 1)
            if hc:
                scores(hc - 1)
        scores(HC - 1)

    @block.vector
    def _(dve):
        dve.wait_ge(par_in, 32)

        def norm(tb):
            dve.wait_ge(rs_done, tb + 1)
            if tb >= 2:
                dve.wait_ge(turned, 2 * (tb - 1))
            dve.tensor_scalar(xn[:, tb % 2, :], h_sb[:, tb, :], stat[:, 16 + tb:17 + tb], None, ALU.mult).then_inc(xn_ready, 1)

        norm(0)
        for n, (tb, kh) in enumerate(turns):
            if kh == 0 and tb + 1 < TB:
                norm(tb + 1)
            dve.wait_ge(turned, n + 1)
            dve.tensor_tensor(xnT[:, 4 * kh:4 * kh + 4, tb * P:(tb + 1) * P],
                              misc_ps[n % 2][:, :].rearrange("p (k t) -> p k t", k=4),
                              gain[:, 4 * kh:4 * kh + 4].unsqueeze(2).to_broadcast([P, 4, P]),
                              ALU.mult).then_inc(turned_out, 1)
        for hc in range(HC):
            for g in range(2):
                n = 2 * hc + g
                dve.wait_ge(s_full, n + 1)
                dve.tensor_copy(s_sb[:, 4 * g:4 * g + 4, hc, :],
                                misc_ps[n % 2][:, :].rearrange("p (b n) -> p b n", b=4)).then_inc(s_out, 1)
    ctx.close()


def build_hidden(nc, ins, xh, xl, s_sb, g_dram, w_dram, mem_map):
    ctx = ExitStack()
    at = dict(mem_map)

    def sb(region, name, shape, dt=F32):
        size = int(np.prod(shape[1:])) * (2 if dt == BF16 else 4)
        off = at[region]
        at[region] = off + (size + 31) // 32 * 32
        assert at[region] <= mem_map[region] + mem_map[region + "_size"], (region, name)
        return nc.alloc_sbuf_tensor_at(name, shape, dt, offset=off)

    def sem(name):
        return ctx.enter_context(nc.semaphore(name))

    con = sb("const", "con3", [P, C_COLS - C_IOTA])
    ident = sb("const", "ident3", [P, P])
    iota = sb("const", "iota_bf", [P, P], BF16)
    iota50 = con[:, C_IOTA50 - C_IOTA:C_IOTA50 - C_IOTA + NCAND]
    u_in = [sb("u", f"u_in{i}", [P, KD, P]) for i in range(2)]
    u_hi = [sb("u", f"u_hi{i}", [P, KD, P], BF16) for i in range(2)]
    u_lo = [sb("u", f"u_lo{i}", [P, KD, P], BF16) for i in range(2)]
    g_out = [sb("g", f"g_out{i}", [P, SEQ]) for i in range(2)]
    codeT = sb("sel", "codeT", [P, SEQ])
    rowT = sb("sel", "rowT", [P, SEQ])
    wT = sb("sel", "wT", [P, SEQ])
    whT = sb("sel", "whT", [P, SEQ])
    sc = sb("hot", "sc", [P, HC, NK])
    top = sb("hot", "top", [P, HC, PK])
    topi = sb("hot", "topi", [P, HC, PK], U32)
    topf = sb("hot", "topf", [P, HC, PK])
    cand = sb("hot", "cand", [P, PH, NCAND])
    code = sb("hot", "code", [P, PH, NCAND])
    fin = sb("hot", "fin", [P, PH, PK])
    posi = sb("hot", "posi", [P, PH, PK], U32)
    posf = sb("hot", "posf", [P, PH, PK])
    wrow = sb("hot", "wrow", [P, PH, PK])
    crow = sb("hot", "crow", [P, PH, PK])
    wsum = sb("hot", "wsum", [P, 2, PH])
    match = sb("hot", "match", [P, 2, PK, NCAND])
    at["hot"] = mem_map["hot"]
    hot = [[sb("hot", f"hot_{n}{i}", [P, GT, P], BF16) for n in ("ihi", "ilo", "j")] for i in range(2)]
    wbuf = [nc.alloc_sbuf_tensor_at(f"wbuf{i}", [P, NK, WT], F32, offset=mem_map["s"] + i * NK * WT * 4) for i in range(2)]
    hid_ps = [ctx.enter_context(nc.psum_tensor(f"hid_ps{i}", [P, 2, HALF], F32)) for i in range(2)]
    w_ps = [ctx.enter_context(nc.psum_tensor(f"w_ps{i}", [P, HALF], F32)) for i in range(4)]

    one = sb("const", "one", [P, KD])
    par_in, iota_ready, one_ready = sem("par3_in"), sem("iota_ready"), sem("one_ready")
    u_loaded = [sem(f"u_loaded{i}") for i in range(2)]
    u_cast, u_ready = sem("u_cast"), sem("u_ready")
    hid_full, hid_out = sem("hid_full"), sem("hid_out")
    g_stored = [sem(f"g_stored{i}") for i in range(2)]
    w_stored = [sem(f"w_stored{i}") for i in range(2)]
    fin_ready, exp_ready = sem("fin_ready"), sem("fin_exp")
    sel_ready, sel_turned, sel_out = sem("sel_ready"), sem("sel_turned"), sem("sel_out")
    hot_ready, w_full, w_out = sem("hot_ready"), sem("w_full"), sem("w_out")
    step = sem("dve_step3")
    SEL = CH // 2 // TB
    block = ctx.enter_context(nc.Block())

    @block.sync
    def _(sp):
        sp.dma_start(con[:, :], ins["consts"][:, C_IOTA:C_COLS]).then_inc(par_in, 16)
        sp.dma_start(ident[:, :], ins["consts"][:, 0:P]).then_inc(par_in, 16)
        with sp.Fori(0, CH // 2) as i:
            for u in range(2):
                sp.wait_ge(u_ready, 2 * i + u + 1)
                sp.dma_start(u_in[u][:, :, :], ins["peer_u"][2 * i + u]).then_inc(u_loaded[u], 16)

    @block.gpsimd
    def _(pool):
        pool.sem_inc(u_ready, 2)
        pool.memset(one[:, :], 1.0).then_inc(one_ready, 1)
        pool.wait_ge(one_ready, 1)
        with pool.Fori(0, CH // 2) as i:
            for u in range(2):
                pool.wait_ge(u_loaded[u], 16 * i + 16)
                pool.wait_ge(hid_full, 2 * i + u + 1)
                pool.tensor_tensor(u_hi[u][:, :, :], u_in[u][:, :, :],
                                   one[:, :].unsqueeze(2).to_broadcast([P, KD, P]), ALU.mult).then_inc(u_cast, 1)
                pool.wait_ge(u_cast, 2 * i + u + 1)
                pool.tensor_tensor(u_lo[u][:, :, :], u_in[u][:, :, :], u_hi[u][:, :, :],
                                   ALU.subtract).then_inc(u_ready, 1)

    @block.scalar
    def _(act):
        act.sem_inc(hid_out, 2)
        act.sem_inc(w_out, 4)
        act.sem_inc(sel_out, 1)
        for i in range(2):
            act.sem_inc(g_stored[i], 16)
            act.sem_inc(w_stored[i], 16)

        def gelu(c, pair, u):
            act.wait_ge(hid_full, c + 3)
            act.wait_ge(g_stored[u], 16 * pair + 16)
            act.activation(g_out[u][:, :], hid_ps[u][:, :, :].rearrange("p a b -> p (a b)"),
                           ACT.Gelu_apprx_tanh).then_inc(hid_out, 1)
            act.wait_ge(hid_out, c + 3)
            act.dma_start(g_dram[c], g_out[u][:, :]).then_inc(g_stored[u], 16)

        with act.Fori(0, TB) as tb:
            for v in range(SEL):
                gelu(tb * SEL + v, tb * (SEL // 2) + v // 2, v % 2)
                if v == SEL - 2:
                    act.wait_ge(fin_ready, tb + 1)
                    act.activation(wrow[:, :, :], wrow[:, :, :], ACT.Exp).then_inc(exp_ready, 1)
            act.wait_ge(sel_turned, tb + 2)
            act.activation(codeT[:, bass.ts(tb, P)], w_ps[0][:, 0:P], ACT.Copy)
            act.activation(wT[:, bass.ts(tb, P)], w_ps[0][:, P:2 * P], ACT.Copy).then_inc(sel_out, 1)
        with act.Fori(0, CH // 2 // 8) as it:
            for v in range(8):
                gelu(CH // 2 + 8 * it + v, CH // 4 + 4 * it + v // 2, v % 2)
                b = v // 4
                if v % 4 == 0:
                    act.wait_ge(w_stored[b], 16 * it + 16)
                for k in range(4):
                    act.wait_ge(w_full, 8 + 4 * (8 * it + v) + k + 1)
                    t0 = GT * (v % 4) + 4 * k
                    act.activation(wbuf[b][:, :, t0:t0 + 4],
                                   w_ps[k][:, :].rearrange("p (t j) -> p j t", t=4), ACT.Copy).then_inc(w_out, 1)
                if v % 4 == 3:
                    act.wait_ge(w_out, 4 + 4 * (8 * it + v) + 4)
                    act.dma_start(w_dram[2 * it + b], wbuf[b][:, :, :]).then_inc(w_stored[b], 16)
        for i in range(2):
            act.wait_ge(g_stored[i], 16 + 16 * (CH // 2))
            act.wait_ge(w_stored[i], 16 + 16 * (SEQ // WT // 2))

    @block.tensor
    def _(pe):
        pe.sem_inc(hid_full, 2)
        pe.sem_inc(w_full, 8)
        pe.sem_inc(sel_turned, 1)
        pe.wait_ge(par_in, 32)

        def hidden(c, u):
            pe.wait_ge(u_ready, c + 3)
            pe.wait_ge(hid_out, c + 1)
            for hf in range(2):
                cols = slice(hf * HALF, (hf + 1) * HALF)
                for kd in range(KD):
                    pe.matmul(hid_ps[u][:, hf, :], u_hi[u][:, kd, :], xh[:, kd, cols], start=kd == 0, stop=False)
                    pe.matmul(hid_ps[u][:, hf, :], u_hi[u][:, kd, :], xl[:, kd, cols], start=False, stop=False)
                    mm = pe.matmul(hid_ps[u][:, hf, :], u_lo[u][:, kd, :], xh[:, kd, cols], start=False,
                                   stop=kd == KD - 1)
            mm.then_inc(hid_full, 1)

        with pe.Fori(0, TB) as tb:
            for v in range(SEL):
                hidden(tb * SEL + v, v % 2)
            pe.wait_ge(sel_ready, tb + 1)
            pe.wait_ge(sel_out, tb + 1)
            pe.transpose(w_ps[0][:, 0:P], crow[:, :, :].rearrange("p h k -> p (h k)"), ident[:, :])
            pe.transpose(w_ps[0][:, P:2 * P], wrow[:, :, :].rearrange("p h k -> p (h k)"),
                         ident[:, :]).then_inc(sel_turned, 1)
        pe.wait_ge(sel_out, TB + 1)
        with pe.Fori(0, CH // 2 // 8) as it:
            for v in range(8):
                hidden(CH // 2 + 8 * it + v, v % 2)
                g = 8 * it + v
                hi, lo, hj = hot[v % 2]
                pe.wait_ge(hot_ready, g + 1)
                for k in range(4):
                    pe.wait_ge(w_out, 4 * g + k + 1)
                    for i in range(4):
                        t = 4 * k + i
                        dst = w_ps[k][:, i * P:(i + 1) * P]
                        pe.matmul(dst, hi[:, t, :], hj[:, t, :], start=True, stop=False)
                        mm = pe.matmul(dst, lo[:, t, :], hj[:, t, :], start=False, stop=True)
                    mm.then_inc(w_full, 1)

    @block.vector
    def _(dve):
        tt, ts = dve.tensor_tensor, dve.tensor_scalar
        dve.wait_ge(par_in, 32)
        dve.tensor_copy(iota[:, :], con[:, 0:P]).then_inc(iota_ready, 1)
        with dve.Fori(0, TB) as tb:
            n = 0

            def link(i):
                nonlocal n
                i.then_inc(step, 1)
                n += 1
                dve.wait_ge(step, n)

            def top16(src, vals, idx, rows):
                for r in rows:
                    i = dve.max(vals[:, r, 0:8], src[:, r, :])
                link(i)
                for r in rows:
                    i = dve.max_index(idx[:, r, 0:8], vals[:, r, 0:8], src[:, r, :])
                link(i)
                for r in rows:
                    i = dve.match_replace(src[:, r, :], vals[:, r, 0:8], src[:, r, :], NEG)
                link(i)
                for r in rows:
                    i = dve.max(vals[:, r, 8:16], src[:, r, :])
                link(i)
                for r in rows:
                    i = dve.max_index(idx[:, r, 8:16], vals[:, r, 8:16], src[:, r, :])
                link(i)

            link(dve.tensor_copy(sc[:, :, :], s_sb[:, bass.ds(tb, 1), :, :].rearrange("p o h n -> p (o h) n")))
            top16(sc, top, topi, range(HC))
            link(dve.tensor_copy(topf[:, :, :], topi[:, :, :]))
            v4 = top[:, :, :].rearrange("p (h c) k -> p h c k", c=2)
            i4 = topf[:, :, :].rearrange("p (h c) k -> p h c k", c=2)
            link(ts(i4[:, :, 0, :], i4[:, :, 0, :], float(NK), None, ALU.mult))
            dve.wait_ge(sel_turned, tb + 1)
            off = 0
            for a, na, nb in PAIRS:
                for dst, src in ((cand, v4), (code, i4)):
                    out = dst[:, :, off:off + na * nb].rearrange("p h (a b) -> p h a b", a=na)
                    x = src[:, :, 0, a:a + na].unsqueeze(3).to_broadcast([P, PH, na, nb])
                    y = src[:, :, 1, 0:nb].unsqueeze(2).to_broadcast([P, PH, na, nb])
                    i = tt(out, x, y, ALU.add)
                off += na * nb
            link(i)
            top16(cand, fin, posi, range(PH))
            tt(wrow[:, :, :], fin[:, :, :], fin[:, :, 0:1].to_broadcast([P, PH, PK]), ALU.subtract).then_inc(fin_ready, 1)
            link(dve.tensor_copy(posf[:, :, :], posi[:, :, :]))
            for h in range(0, PH, 2):
                link(tt(match[:, :, :, :], posf[:, h:h + 2, :].unsqueeze(3).to_broadcast([P, 2, PK, NCAND]),
                        iota50.unsqueeze(1).unsqueeze(1).to_broadcast([P, 2, PK, NCAND]), ALU.is_equal))
                link(tt(match[:, :, :, :], match[:, :, :, :],
                        code[:, h:h + 2, :].unsqueeze(2).to_broadcast([P, 2, PK, NCAND]), ALU.mult))
                link(dve.tensor_reduce(crow[:, h:h + 2, :], match[:, :, :, :], AX.X, ALU.add))
            dve.wait_ge(exp_ready, tb + 1)
            link(dve.tensor_reduce(wsum[:, 0, :], wrow[:, :, :], AX.X, ALU.add))
            link(dve.reciprocal(wsum[:, 1, :], wsum[:, 0, :]))
            dve.sem_clear(step)
            tt(wrow[:, :, :], wrow[:, :, :], wsum[:, 1, :].unsqueeze(2).to_broadcast([P, PH, PK]),
               ALU.mult).then_inc(sel_ready, 1)
        dve.wait_ge(sel_out, TB + 1)
        base = [0]

        def link(i):
            i.then_inc(step, 1)
            base[0] += 1
            dve.wait_ge(step, base[0])

        link(ts(rowT[:, :], codeT[:, :], 1.0 / NK, -(NK - 1) / (2.0 * NK), ALU.mult, ALU.add))
        link(ts(rowT[:, :], rowT[:, :], MAGIC, None, ALU.add))
        link(ts(rowT[:, :], rowT[:, :], -MAGIC, None, ALU.add))
        link(dve.scalar_tensor_tensor(codeT[:, :], rowT[:, :], -float(NK), codeT[:, :], ALU.mult, ALU.add))
        half = hot[0][0][:, 0:8, :].rearrange("p a b -> p (a b)")
        link(dve.tensor_copy(half, wT[:, :]))
        link(dve.tensor_copy(whT[:, :], half))
        link(tt(wT[:, :], wT[:, :], whT[:, :], ALU.subtract))
        with dve.Fori(0, CH // 2 // 2) as q:
            for b in range(2):
                hi, lo, hj = hot[b]
                dve.wait_ge(w_full, 4 * (2 * q + b) + 4)
                for i in range(GT):
                    t = (2 * q + b) * GT + i
                    at_t = lambda x: x[:, bass.ds(t, 1)]
                    ts(hi[:, i, :], iota[:, :], at_t(rowT), at_t(whT), ALU.is_equal, ALU.mult)
                    ts(lo[:, i, :], iota[:, :], at_t(rowT), at_t(wT), ALU.is_equal, ALU.mult)
                    last = ts(hj[:, i, :], iota[:, :], at_t(codeT), None, ALU.is_equal)
                last.then_inc(hot_ready, 1)
    ctx.close()


def build_output(nc, ins, h_sb, g_dram, w_dram, out, mem_map):
    ctx = ExitStack()
    at = dict(mem_map)

    def sb(region, name, shape, dt=F32):
        size = int(np.prod(shape[1:])) * (2 if dt == BF16 else 4)
        off = at[region]
        at[region] = off + (size + 31) // 32 * 32
        assert at[region] <= mem_map[region] + mem_map[region + "_size"], (region, name)
        return nc.alloc_sbuf_tensor_at(name, shape, dt, offset=off)

    def sem(name):
        return ctx.enter_context(nc.semaphore(name))

    stat = sb("const", "stat4", [P, 64])
    gain = sb("const", "gain4", [P, D])
    NW = SEQ // WT
    w_sb = [sb("b", f"w_sb{i}", [P, NW, CG, WT]) for i in range(2)]
    g_sb = [sb("b", f"g_sb{i}", [P, CG, SEQ]) for i in range(2)]
    v_sb = [sb("b", f"v_sb{i}", [P, CG, D]) for i in range(2)]
    a_hi, a_lo, v_hi, v_lo = ([sb("b", f"{n}{i}", [P, CG, SEQ], BF16) for i in range(2)]
                              for n in ("a_hi", "a_lo", "v_hi", "v_lo"))
    ps = [ctx.enter_context(nc.psum_tensor(f"o_ps{i}", [P, HALF], F32)) for i in range(8)]
    gain_in = sem("gain4_in")
    loaded = [sem(f"gwv_loaded{i}") for i in range(2)]
    act_made = sem("act_made")
    ahi_made, alo_made = sem("ahi_made"), sem("alo_made")
    vhi_made, vlo_made = sem("vhi_made"), sem("vlo_made")
    o_full, o_out = sem("o_full"), sem("o_out")
    sq_done, rs_done, y_ready = sem("sq4_done"), sem("rs4_done"), sem("y_ready")
    half_set, pstep, dstep = sem("half_set4"), sem("pool_step4"), sem("dve_step4")
    stored = sem("y_stored")
    NG = CH // CG
    TILES = 2 * TB
    block = ctx.enter_context(nc.Block())

    @block.sync
    def _(sp):
        sp.dma_start(gain[:, :], ins["norm_final"].partition_broadcast(P)).then_inc(gain_in, 16)
        with sp.Fori(0, NG // 2) as i:
            for b in range(2):
                q = 2 * i + b
                sp.wait_ge(alo_made, CG * q + CG)
                sp.wait_ge(vlo_made, CG * q + CG)
                sp.dma_start(v_sb[b][:, :, :], ins["peer_v"][bass.ds(CG * q, CG)].rearrange("c p n -> p c n")).then_inc(loaded[b], 16)
                sp.dma_start(g_sb[b][:, :, :], g_dram[bass.ds(CG * q, CG)].rearrange("c p n -> p c n")).then_inc(loaded[b], 16)
                sp.dma_start(w_sb[b][:, :, :, :].rearrange("p g c t -> p g (c t)"),
                             w_dram[:, :, bass.ds(CG * q, CG), :].rearrange("g p c t -> p g (c t)")).then_inc(loaded[b], 16)
        for tb in range(TB):
            sp.wait_ge(y_ready, tb + 1)
            sp.dma_start(out[tb * P:(tb + 1) * P, :], h_sb[:, tb, :]).then_inc(stored, 16)
        sp.wait_ge(stored, 16 * TB)

    @block.gpsimd
    def _(pool):
        pool.sem_inc(vlo_made, 2 * CG)
        pool.memset(stat[:, 32:33], -0.5).then_inc(half_set, 1)
        pool.wait_ge(half_set, 1)
        with pool.Fori(0, NG // 2) as i:
            for b in range(2):
                q = 2 * i + b
                for c in range(CG):
                    pool.wait_ge(vhi_made, CG * q + c + 1)
                    pool.tensor_tensor(v_lo[b][:, c, :], v_sb[b][:, c, :], v_hi[b][:, c, :],
                                       ALU.subtract).then_inc(vlo_made, 1)
        for tb in range(TB):
            pool.wait_ge(sq_done, tb + 1)
            pool.tensor_scalar(stat[:, tb:tb + 1], stat[:, tb:tb + 1], 1.0 / D, EPS, ALU.mult, ALU.add).then_inc(pstep, 1)
            pool.wait_ge(pstep, tb + 1)
            pool.tensor_tensor(stat[:, 16 + tb:17 + tb], stat[:, tb:tb + 1], stat[:, 32:33], ALU.pow).then_inc(rs_done, 1)

    @block.scalar
    def _(act):
        with act.Fori(0, NG // 2) as i:
            for b in range(2):
                q = 2 * i + b
                act.wait_ge(loaded[b], 48 * i + 48)
                act.wait_ge(o_full, TILES * q + TILES)
                for c in range(CG):
                    act.activation(v_hi[b][:, c, :], v_sb[b][:, c, :], ACT.Copy).then_inc(vhi_made, 1)
                for c in range(CG):
                    act.wait_ge(act_made, CG * q + c + 1)
                    act.activation(a_hi[b][:, c, :], g_sb[b][:, c, :], ACT.Copy).then_inc(ahi_made, 1)
        for tb in range(TB):
            act.wait_ge(o_out, 8 + (NG - 1) * TILES + 2 * tb + 2)
            if tb == 0:
                act.wait_ge(o_full, TILES * NG + 2 * TILES)
            if tb >= 4:
                act.wait_ge(sq_done, tb - 3)
            act.activation(v_sb[0][:, tb % 4, :], h_sb[:, tb, :], ACT.Square, accum_out=stat[:, tb:tb + 1]).then_inc(sq_done, 1)

    @block.tensor
    def _(pe):
        pe.sem_inc(o_full, 2 * TILES)
        with pe.Fori(0, NG // 2) as i:
            for b in range(2):
                q = 2 * i + b
                pe.wait_ge(vlo_made, CG * q + 3 * CG)
                pe.wait_ge(alo_made, CG * q + 3 * CG)
                for n in range(TILES):
                    tb, hf = divmod(n, 2)
                    tok, col = slice(tb * P, (tb + 1) * P), slice(hf * HALF, (hf + 1) * HALF)
                    pe.wait_ge(o_out, TILES * q + n + 1)
                    bank = ps[n % 8][:, :]
                    for c in range(CG):
                        pe.matmul(bank, a_hi[b][:, c, tok], v_hi[b][:, c, col], start=c == 0, stop=False)
                        pe.matmul(bank, a_hi[b][:, c, tok], v_lo[b][:, c, col], start=False, stop=False)
                        mm = pe.matmul(bank, a_lo[b][:, c, tok], v_hi[b][:, c, col], start=False, stop=c == CG - 1)
                    mm.then_inc(o_full, 1)

    @block.vector
    def _(dve):
        dve.sem_inc(o_out, 8)
        dve.sem_inc(alo_made, 2 * CG)

        def activations(q, i, b):
            dve.wait_ge(loaded[b], 48 * i + 48)
            dve.wait_ge(o_full, TILES * q + TILES)
            for c in range(CG):
                g = g_sb[b][:, c, :].rearrange("p (g t) -> p g t", g=NW)
                dve.tensor_tensor(g, g, w_sb[b][:, :, c, :], ALU.mult).then_inc(act_made, 1)
            for c in range(CG):
                dve.wait_ge(ahi_made, CG * q + c + 1)
                dve.tensor_tensor(a_lo[b][:, c, :], g_sb[b][:, c, :], a_hi[b][:, c, :], ALU.subtract).then_inc(alo_made, 1)

        def join(q, tiles):
            for n in tiles:
                tb, hf = divmod(n, 2)
                acc = h_sb[:, tb, hf * HALF:(hf + 1) * HALF]
                dve.wait_ge(o_full, TILES * q + 2 * TILES + n + 1)
                dve.tensor_tensor(acc, acc, ps[n % 8][:, :], ALU.add).then_inc(o_out, 1)

        activations(0, 0, 0)
        with dve.Fori(0, NG // 2 - 1) as i:
            activations(2 * i + 1, i, 1)
            join(2 * i, range(TILES))
            activations(2 * i + 2, i + 1, 0)
            join(2 * i + 1, range(TILES))
        activations(NG - 1, NG // 2 - 1, 1)
        join(NG - 2, range(TILES))
        join(NG - 1, range(TILES))
        dve.wait_ge(gain_in, 16)
        for tb in range(TB):
            dve.wait_ge(rs_done, tb + 1)
            dve.scalar_tensor_tensor(h_sb[:, tb, :], h_sb[:, tb, :], stat[:, 16 + tb:17 + tb], gain[:, :],
                                     ALU.mult, ALU.mult).then_inc(y_ready, 1)
    ctx.close()


BASE = 16512


def regions(*parts):
    out, at = {}, BASE
    for name, kib in parts:
        out[name], out[name + "_size"] = at, int(kib * 1024)
        at += int(kib * 1024)
    assert at <= 229344
    return out


MIX_MAP = regions(("const", 5.75), ("nt", 32), ("x", 32), ("w", 48), ("stage", 8), ("zt", 16), ("ret", 16),
                  ("s5c", 20), ("tmp", 24), ("sg", 6))
SCORE_MAP = regions(("const", 5.75), ("nt", 32), ("xhl", 32), ("s", 64), ("xnt", 32), ("wq", 16),
                    ("keys", 8), ("qt", 8))
HIDDEN_MAP = regions(("const", 5.75), ("nt", 32), ("xhl", 32), ("s", 64), ("u", 16), ("g", 8),
                     ("sel", 16), ("hot", 24))
OUT_MAP = regions(("const", 5.75), ("nt", 32), ("b", 160))


def build_program(nc, ins, out):
    h_sb = nc.alloc_sbuf_tensor_at("h", [P, TB, D], F32, offset=MIX_MAP["nt"])
    xh = nc.alloc_sbuf_tensor_at("xh", [P, KD, SEQ], BF16, offset=SCORE_MAP["xhl"])
    xl = nc.alloc_sbuf_tensor_at("xl", [P, KD, SEQ], BF16, offset=SCORE_MAP["xhl"] + KD * SEQ * 2)
    s_sb = nc.alloc_sbuf_tensor_at("scores", [P, TB, HC, NK], F32, offset=SCORE_MAP["s"])
    g_dram = nc.dram_tensor("g_scratch", [CH, P, SEQ], F32).ap()
    w_dram = nc.dram_tensor("w_scratch", [SEQ // WT, P, NK, WT], F32).ap()
    build_mixer(nc, ins, h_sb, MIX_MAP)
    build_scores(nc, ins, h_sb, xh, xl, s_sb, SCORE_MAP)
    build_hidden(nc, ins, xh, xl, s_sb, g_dram, w_dram, HIDDEN_MAP)
    build_output(nc, ins, h_sb, g_dram, w_dram, out, OUT_MAP)


def columns(a):
    return a.reshape(-1, P).T


def s5_blocks(a):
    out = np.zeros((P, S5T, P), a.dtype)
    for group in range(a.shape[0]):
        s, g = divmod(group, 2)
        c = 32 * (s % 4) + 16 * g
        out[64 * g:64 * g + 64, s, c:c + 16] = a[group]
    return out


def layout(a):
    g = {n: a[n][0] for n in ("x", "mem", "w_in", "w_mem_kv", "s5_w_glu", "w_branch_ret", "w_branch_s5",
                              "w_branch_mem", "w_out", "peer_w_q")}
    g["norm_final"] = a["norm_final"]
    for n in ("positions", "norm_mix", "norm_mem", "norm_ffn", "s5_d"):
        g[n] = columns(a[n][0])
    for n in ("s5_a_re", "s5_a_im"):
        g[n] = columns(a[n][0].reshape(-1))
    g["s5_log_dt"] = columns(np.repeat(a["s5_log_dt"][0], 64))
    for n in ("s5_b_re", "s5_b_im"):
        g[n] = s5_blocks(a[n][0])
    for n in ("s5_c_re", "s5_c_im"):
        g[n] = s5_blocks(a[n][0].transpose(0, 2, 1))
    g["peer_keys"] = a["peer_keys"][0].reshape(HC, NK, P).transpose(2, 0, 1)
    g["peer_u"] = a["peer_u"][0].reshape(NK, NK, KD, P).transpose(1, 3, 2, 0)
    g["peer_v"] = a["peer_v"][0].reshape(NK, NK, D).transpose(1, 0, 2)
    g["consts"] = constants()
    return {n: np.ascontiguousarray(v) for n, v in g.items()}


def kernel(**inputs):
    import concourse.bacc as bacc
    from concourse.bass_utils import run_bass_kernel_spmd

    nc = bacc.Bacc("TRN2", target_bir_lowering=False, num_devices=1)
    arrays = layout({n: np.asarray(v) for n, v in inputs.items()})
    ins = {n: nc.dram_tensor("in_" + n, v.shape, mybir.dt.from_np(v.dtype), kind="ExternalInput").ap()
           for n, v in arrays.items()}
    out = nc.dram_tensor("out", [SEQ, D], F32, kind="ExternalOutput").ap()
    build_program(nc, ins, out)
    r = run_bass_kernel_spmd(nc, [{"in_" + n: v for n, v in arrays.items()}], core_ids=[0])
    return r.results[0]["out"].reshape(1, SEQ, D)
```

```python
import math
from contextlib import ExitStack

import numpy as np
import concourse.bass as bass
from concourse import mybir

F32 = mybir.dt.float32
BF16 = mybir.dt.bfloat16
I32 = mybir.dt.int32
U32 = mybir.dt.uint32
ALU = mybir.AluOpType
ACT = mybir.ActivationFunctionType
AX = mybir.AxisListType

P = 128
SEQ, D = 1024, 1024
TB = SEQ // P
KD = D // P
MEM = 256
EPS = 1e-6
HALF = 512
RH, RD = 4, 128
S5T = 8
MH, MD = 4, 64
Q0, K0, V0, G0, U0, GATE0 = 0, 512, 1024, 1536, 2048, 2560
MAGIC = 12582912.0
TWO_PI_HI, TWO_PI_MID, TWO_PI_LO = 6.28125, 0.0019350051879882812, 3.0199159819e-07
PI_BELOW = 3.1415925

GAMMA = [1.0 - 2.0 ** (-5.0 - h) for h in range(RH)]


def constants():
    i = np.arange(P)
    decay = np.zeros((P, RH, P))
    kfac, qfac = np.zeros((P, RH)), np.zeros((P, RH))
    for h, g in enumerate(GAMMA):
        decay[:, h, :] = np.where(i[:, None] <= i[None, :], (g ** -(i + 1.0))[:, None], 0.0) * RD ** -0.5
        kfac[:, h] = g ** (P - 1.0 - i) * RD ** -0.5
        qfac[:, h] = g ** (i + 1.0)
    inv = (10000.0 ** (-np.arange(64, dtype=np.float32) / np.float32(64))).astype(np.float32)
    rows = [np.eye(P), decay.reshape(P, RH * P), kfac, qfac, np.tile(inv, (P, 1)),
            np.tile(np.arange(P, dtype=np.float64), (P, 1)),
            np.tile(np.arange(50, dtype=np.float64), (P, 1))]
    return np.ascontiguousarray(np.concatenate(rows, 1).astype(np.float32))


C_ID, C_DEC, C_KF, C_QF, C_INV, C_IOTA, C_IOTA50 = 0, 128, 640, 644, 648, 712, 840
C_COLS = 890


QUARTERS = 4


def mixer_steps():
    main = [("z", ct, hf) for hf in range(2) for ct in range(4)]
    for hp in range(2):
        for tb in range(TB):
            main += [("qk", hp, tb), ("vg", hp, tb)]
    for dh in range(2):
        for br in range(3):
            main += [("gate", dh, br, tb) for tb in range(TB)]
    first = 8
    extra = {}

    def put(slot, job):
        extra.setdefault(slot, []).append(job)

    for hp in range(2):
        for tb in range(TB):
            at = 2 * (first + hp * 16 + 2 * tb)
            put(at + 4, ("turn", hp, tb))
            put(at + 6, ("score", hp, tb))
            put(at + 7, ("mix", hp, tb))
            put(at + 10, ("flip", hp, tb))
    chain = [(tb, mp) for tb in range(TB) for mp in range(2)]
    for c, (tb, mp) in enumerate(chain):
        for k, name in enumerate(("ascore", "aturn", "amix", "aflip")):
            put(2 * first + 7 + 4 * c + k, (name, tb, mp))
    for s in range(S5T):
        at = 2 * first + 6 * s
        if s:
            put(at - 2, ("tables", s, 0))
            put(at - 1, ("tables", s, 1))
            put(at, ("tables", s, 2))
        for hf in range(2):
            put(at + 2 * hf, ("bu", s, hf))
            put(at + 2 * hf + 1, ("scan", s, hf))
            put(at + 2 * hf + 2, ("states", s, hf))
            put(at + 3 * hf + 6, ("y", s, hf))
    glu = 2 * first + 6 * S5T + 8
    put(glu, ("glu", 0))
    put(glu + 2, ("glu", 1))
    last = {}
    steps = []
    plan = split_plan()

    def splits(n):
        return [("split", n, i) for i in range(4)]

    steps += [("xturn", tb, kh) for tb in range(4) for kh in range(2)] + [("param", 0)]
    for m, unit in enumerate(main):
        small = extra.pop(2 * m, []) + extra.pop(2 * m + 1, [])
        if m < first:
            steps.append(unit)
            assert not small
        else:
            n = len(small)
            pieces = plan.get(m, [])
            pieces = [None] * (QUARTERS - len(pieces)) + pieces
            for q in range(QUARTERS):
                steps.append(("open", unit, q) if q < QUARTERS - 1 else unit)
                steps += small[n * q // QUARTERS:n * (q + 1) // QUARTERS]
                steps += [pieces[q]] if pieces[q] else []
        steps += [("xturn", tb, kh) for tb in {1: (4,), 2: (5, 6), 3: (7,)}.get(m, ()) for kh in range(2)]
        if m in (1, 2):
            steps += splits(1)[2 * m - 2:2 * m]
        if m == 3:
            steps += [("param", 1)]
        if m == 4:
            steps += splits(2)[:2]
        if m == 7:
            steps += splits(2)[2:]
        if m == 6:
            steps += [("mturn", mt, kh) for mt in range(2) for kh in range(2)]
        if m == 7:
            steps += [("bturn", s) for s in range(0, S5T, 2)] + [("tables", 0, part) for part in range(3)]
        if m == 10:
            steps += [("mk", 0), ("mk", 1), ("mv", 0), ("mv", 1)]
        if unit[0] == "gate" and unit[2] == 2 and unit[3] >= 2:
            steps.append(("gturn", unit[1], unit[3] - 2))
            if unit[3] == TB - 1:
                if unit[1] == 1:
                    steps += [("gturn", 1, TB - 2), ("gturn", 1, TB - 1)]
        if unit[0] == "gate" and unit[1] == 1 and unit[2] == 0 and unit[3] < 2:
            steps.append(("gturn", 0, TB - 2 + unit[3]))
    assert not extra, extra
    steps += [("out", dh, tb) for dh in range(2) for tb in range(TB)]
    return steps


LOADS = [("z", None, ("z", 3, 1)), ("qk", 0, ("qk", 0, TB - 1)), ("vg", 0, ("vg", 0, TB - 1)),
         ("mem", None, ("mv", 1)), ("qk", 1, ("qk", 1, TB - 1)), ("vg", 1, ("vg", 1, TB - 1))]
LOADS += [("gate", (dh, br), ("gate", dh, br, TB - 1)) for dh in range(2) for br in range(3)]
LOADS += [("out", dh, ("out", dh, TB - 1)) for dh in range(2)]
LOAD_NO = {(k, a): n for n, (k, a, _) in enumerate(LOADS)}
BUFFER = [2, 0, 1, 2, 2, 0, 1, 2, 0, 1, 2, 0, 1, 2]


def split_plan():
    plan = {}
    for m, n in ((13, 4), (25, 6), (39, 7), (43, 8), (48, 9), (56, 10), (64, 11), (72, 12), (80, 13)):
        for i in range(4):
            plan.setdefault(m + i, []).append(("split", n, i))
    plan[22] = [("split", 5, 0)]
    plan[23] = [("split", 5, i) for i in (1, 2, 3)]
    for m, row in ((37, 4), (38, 5), (39, 6), (40, 7), (44, 0), (45, 1), (46, 2), (47, 3)):
        plan.setdefault(m, []).append(("split", "br", row))
    return plan


MAIN = ("z", "qk", "vg", "gate")
OWN_BANK = ("bu", "y", "split", "param", "open", "tables", "scan", "states")


def build_mixer(nc, ins, h_sb, root_h, gain_h, mem_map):
    steps = mixer_steps()
    main_no = {s: n for n, s in enumerate([s for s in steps if s[0] in MAIN])}
    misc_no = {s: n for n, s in enumerate([s for s in steps if s[0] not in MAIN + OWN_BANK])}
    gate_no = {s: n for n, s in enumerate([s for s in steps if s[0] == "gate"])}
    bu_no = {s: n for n, s in enumerate([s for s in steps if s[0] == "bu"])}
    chain_no = {(tb, mp): 2 * tb + mp for tb in range(TB) for mp in range(2)}
    turn_no = {(hp, tb): hp * TB + tb for hp in range(2) for tb in range(TB)}

    ctx = ExitStack()
    ctx.enter_context(nc.allow_non_contiguous_dma("small parameter columns"))
    at = {k: v for k, v in mem_map.items()}

    def sb(region, name, shape, dt=F32):
        size = int(np.prod(shape[1:])) * (2 if dt == BF16 else 4)
        off = at[region]
        at[region] = off + (size + 31) // 32 * 32
        assert at[region] <= mem_map[region] + mem_map[region + "_size"], (region, name, at[region] - mem_map[region])
        return nc.alloc_sbuf_tensor_at(name, shape, dt, offset=off)

    def sem(name):
        return ctx.enter_context(nc.semaphore(name))

    def again(region, skip=0):
        at[region] = mem_map[region] + skip

    con = sb("const", "con", [P, C_COLS])
    small = sb("const", "small", [P, 22, 8])
    levels = sb("const", "levels", [P, 2, 9, S5T])
    gains = sb("const", "gains", [P, 2, KD])
    stat = sb("const", "stat", [P, 64])
    nhl = sb("nt", "nhl", [P, KD, TB, 2, P], BF16)
    nT = sb("x", "nT", [P, KD, SEQ])
    again("x")
    tab = sb("x", "tab", [P, 2, HALF])
    kmT = sb("x", "kmT", [P, 2, 2, MEM])
    vm = sb("x", "vm", [P, 2, MEM])
    psc = sb("x", "psc", [P, HALF])
    qkT = sb("x", "qkT", [P, 2, HALF])
    prod = sb("x", "prod", [P, 4, HALF])
    ysc = sb("x", "ysc", [P, 2, 2, HALF])
    again("x")
    wbr = sb("x", "wbr", [P, 8, 2, D], BF16)
    wring = [sb("w", f"w{i}", [P, KD, 2, HALF], BF16) for i in range(3)]
    again("w")
    xs = sb("w", "xs", [P, TB, D])
    wfull = sb("w", "wfull", [P, KD, HALF])
    stage = sb("stage", "stage", [P, 2, 2 * HALF])
    zT = sb("zt", "zT", [P, 4, SEQ])
    again("zt")
    zhl = sb("zt", "zhl", [P, 4, TB, 2, P], BF16)
    again("zt")
    merT_hi = sb("zt", "merT_hi", [P, 4, TB, 2, P], BF16)
    memT = sb("ret", "memT", [P, KD, MEM])
    mem_x = sb("ret", "mem_x", [P, 2, D])
    again("ret")
    retT = sb("ret", "retT", [P, RH, TB, 2, P], BF16)
    bbT = sb("s5c", "bbT", [P, 2, S5T, P])
    cT = sb("s5c", "cT", [P, 2, S5T, P])
    wglu = sb("s5c", "wglu", [P, 2, 512])
    again("s5c")
    merged = sb("s5c", "merged", [P, TB, HALF])
    btab = sb("tmp", "btab", [P, 2, S5T, 16])
    rope = sb("tmp", "rope", [P, 2, TB, 64])
    bsrc = sb("tmp", "bsrc", [P, 2, S5T, P])
    btmp = sb("tmp", "btmp", [P, 2, S5T, P])
    again("tmp", 5120)
    qk = sb("tmp", "qk", [P, 2, HALF])
    vg = sb("tmp", "vg", [P, 2, HALF])
    qkr = sb("tmp", "qkr", [P, HALF])
    kdec = sb("tmp", "kdec", [P, 2, 256])
    sT = sb("tmp", "sT", [P, 256])
    ret = sb("tmp", "ret", [P, 256])
    state = sb("tmp", "state", [P, RH, P])
    pT = sb("tmp", "pT", [P, HALF])
    mo = sb("tmp", "mo", [P, P])
    junk = sb("tmp", "junk", [P, P])
    again("tmp")
    merT_lo = sb("tmp", "merT_lo", [P, 4, TB, 2, P], BF16)
    gp = sb("tmp", "gp", [P, 2, HALF])
    xr = sb("tmp", "xr", [P, 2, HALF])
    sg = sb("sg", "sg", [P, 2, HALF])
    rt = sb("sg", "rt", [P, 2, 256])

    main_ps = [ctx.enter_context(nc.psum_tensor(f"main{i}", [P, HALF], F32)) for i in range(2)]
    misc_ps = [ctx.enter_context(nc.psum_tensor(f"misc{i}", [P, HALF], F32)) for i in range(2)]
    bu_ps = [ctx.enter_context(nc.psum_tensor(f"bu{i}", [P, HALF], F32)) for i in range(2)]
    p_ps = bu_ps
    y_ps = [ctx.enter_context(nc.psum_tensor(f"y{i}", [P, HALF], F32)) for i in range(2)]

    x_in = [sem(f"x_in{i}") for i in range(TB)]
    con_in = sem("con_in")
    par_in = sem("par_in")
    gain_in = sem("gain_in")
    hgain_in = sem("hgain_in")
    b_in = sem("b_in")
    c_in = sem("c_in")
    mem_in = sem("mem_in")
    wfull_in = sem("wfull_in")
    staged = [sem(f"staged{i}") for i in range(2)]
    split_hi, split_done = sem("split_hi"), sem("split_done")
    nh_done, nl_done = sem("nh_done"), sem("nl_done")
    xr_in = [sem(f"xr_in{i}") for i in range(2)]
    hsq_done, hrs_done = sem("hsq_done"), sem("hrs_done")
    sq_done = sem("sq_done")
    rs_done = sem("rs_done")
    n_ready = sem("n_ready")
    main_full, main_out = sem("main_full"), sem("main_out")
    misc_full, misc_out = sem("misc_full"), sem("misc_out")
    p_full, p_out = sem("p_full"), sem("p_out")
    bu_full, bu_out = sem("bu_full"), sem("bu_out")
    y_full = sem("y_full")
    scan_done = sem("scan_done")
    rows_used = sem("rows_used")
    half_used = sem("half_used")
    xst_ready, xsi_ready = sem("xst_ready"), sem("xsi_ready")
    bb_ready = sem("bb_ready")
    cneg_ready = sem("cneg_ready")
    ydu_ready = sem("ydu_ready")
    gelu_ready = sem("gelu_ready")
    exp_ready = sem("exp_ready")
    gsig_ready = sem("gsig_ready")
    lam_ready = sem("lam_ready")
    ang_ready = sem("ang_ready")
    rope_ready = sem("rope_ready")
    rot_done = sem("rot_done")
    kdec_done = sem("kdec_done")
    vgate_done = sem("vgate_done")
    ret_done = sem("ret_done")
    retraw_done = sem("retraw_done")
    glu_tanh = sem("glu_tanh")
    merged_done = sem("merged_done")
    dchain, pchain, achain = sem("dve_step"), sem("pool_step"), sem("act_step")

    split_no = {s: n for n, s in enumerate([s for s in steps if s[0] == "split"])}

    def weights(eng, kind, arg):
        n = LOAD_NO[(kind, arg)]
        eng.wait_ge(split_done, split_no[("split", n, 3)] + 1)
        return wring[BUFFER[n]]

    def branch_weights(eng, row):
        eng.wait_ge(split_done, split_no[("split", "br", row)] + 1)

    STAGED, per = {}, [0, 0]
    for s in [s for s in steps if s[0] == "split"]:
        per[split_no[s] % 2] += 2 if s[1] != "br" and LOADS[s[1]][0] in ("qk", "vg") else 1
        STAGED[s] = 16 * per[split_no[s] % 2]

    def split_target(s):
        _, n, i = s
        if n == "br":
            return wbr[:, i, 0, :], wbr[:, i, 1, :]
        w = wring[BUFFER[n]][:, 2 * i:2 * i + 2, :, :]
        return w[:, :, 0, :], w[:, :, 1, :]

    def split_source(s):
        t = stage[:, split_no[s] % 2, :]
        return t if s[1] == "br" else t.rearrange("p (k n) -> p k n", k=2)

    def target_free(eng, s):
        _, n, i = s
        if n == "br":
            for last in (("glu", 1),) if i >= 4 else (("aflip", TB - 1, 1), ("flip", 1, TB - 1)):
                eng.wait_ge(misc_out, misc_no[last] + 1)
            return
        before = [m for m in range(n) if BUFFER[m] == BUFFER[n]]
        if before:
            done_by_pe(eng, LOADS[before[-1]][2])
        if n in (1, 2):
            done_by_pe(eng, ("xturn", TB // 2 * n - 1, 1))

    def done_by_pe(eng, step):
        if step[0] in MAIN:
            eng.wait_ge(main_full, main_no[step] + 1)
        else:
            eng.wait_ge(misc_full, misc_no[step] + 1)

    (S_ARE, S_AIM, S_LDT, S_DT, S_MAG, S_TH, S_COS, S_SIN, S_LRE, S_LIM, S_DEN, S_CR, S_CI,
     S_T0, S_T1, S_T2, S_T3, S_D, S_POS, S_CN, S_SN, S_POSI) = range(22)
    block = ctx.enter_context(nc.Block())

    @block.sync
    def _(sp):
        w_in = ins["w_in"].rearrange("(k p) n -> p k n", p=P)
        w_out = ins["w_out"].rearrange("(k p) n -> p k n", p=P)
        for tb in range(TB):
            if tb == TB // 2:
                sp.dma_start(wfull[:, :, :], w_in[:, :, U0:U0 + HALF]).then_inc(wfull_in, 16)
            sp.dma_start(xs[:, tb, :], ins["x"][tb * P:(tb + 1) * P, :]).then_inc(x_in[tb], 16)
            if tb == 0:
                sp.dma_start(con[:, :], ins["consts"]).then_inc(con_in, 16)
            if tb == 1:
                for k, name in ((S_ARE, "s5_a_re"), (S_AIM, "s5_a_im"), (S_LDT, "s5_log_dt"), (S_D, "s5_d")):
                    sp.dma_start(small[:, k, 0:ins[name].shape[1]], ins[name]).then_inc(par_in, 16)
                sp.dma_start(small[:, S_POSI, :].bitcast(I32), ins["positions"]).then_inc(par_in, 16)
        sp.dma_start(gain_h[:, :], ins["norm_ffn"]).then_inc(hgain_in, 16)
        sp.dma_start(mem_x[:, :, :], ins["mem"].rearrange("(b p) n -> p b n", p=P)).then_inc(mem_in, 16)
        for k, name in enumerate(("s5_b_re", "s5_b_im")):
            sp.dma_start(bsrc[:, k, :, :], ins[name]).then_inc(b_in, 16)
        for k, name in enumerate(("s5_c_re", "s5_c_im")):
            sp.dma_start(cT[:, k, :, :], ins[name]).then_inc(c_in, 16)
        sp.dma_start(wglu[:, :, :], ins["s5_w_glu"].rearrange("(k p) n -> p k n", p=P)).then_inc(c_in, 16)
        branch_name = {0: ("w_branch_ret", 0), 4: ("w_branch_s5", 4), 6: ("w_branch_mem", 6)}
        for s in [s for s in steps if s[0] == "split"]:
            k = split_no[s]
            if k >= 2:
                sp.wait_ge(split_done, k - 1)
            dst, ready = stage[:, k % 2, :], staged[k % 2]
            _, n, i = s
            if n == "br":
                name, first = branch_name[0 if i < 4 else 4 if i < 6 else 6]
                sp.dma_start(dst, ins[name][(i - first) * P:(i - first + 1) * P, :]).then_inc(ready, 16)
                continue
            kind, arg, _ = LOADS[n]
            dst = dst.rearrange("p (k n) -> p k n", k=2)
            if kind in ("qk", "vg"):
                for j, base in enumerate((Q0, K0) if kind == "qk" else (V0, G0)):
                    sp.dma_start(dst[:, :, 256 * j:256 * j + 256],
                                 w_in[:, 2 * i:2 * i + 2, base + 256 * arg:base + 256 * arg + 256]).then_inc(ready, 16)
            elif kind == "gate":
                col = GATE0 + (1, 2, 0)[arg[1]] * D + arg[0] * HALF
                sp.dma_start(dst, w_in[:, 2 * i:2 * i + 2, col:col + HALF]).then_inc(ready, 16)
            else:
                sp.dma_start(dst, w_out[:, 2 * i:2 * i + 2, arg * HALF:(arg + 1) * HALF]).then_inc(ready, 16)
            if s == ("split", 2, 3):
                done_by_pe(sp, ("z", 3, 1))
                sp.dma_start(wfull[:, :, :], ins["w_mem_kv"].rearrange("(k p) n -> p k n", p=P)).then_inc(wfull_in, 16)
        for n in range(2 * TB):
            dh, tb = divmod(n, TB)
            if n >= 2:
                sp.wait_ge(misc_out, misc_no[("out", *divmod(n - 2, TB))] + 1)
            sp.dma_start(xr[:, n % 2, :],
                         ins["x"][tb * P:(tb + 1) * P, dh * HALF:(dh + 1) * HALF]).then_inc(xr_in[n % 2], 16)

        sp.wait_ge(hgain_in, 16)

    @block.gpsimd
    def _(pool):
        for k, name in enumerate(("norm_mix", "norm_mem")):
            pool.dma_start(gains[:, k, :], ins[name]).then_inc(gain_in, 16)
        chain = 0

        def link(i):
            nonlocal chain
            i.then_inc(pchain, 1)
            chain += 1
            pool.wait_ge(pchain, chain)

        link(pool.memset(stat[:, 32:48], -0.5))
        def root(n):
            pool.wait_ge(sq_done, n + 1)
            link(pool.tensor_scalar(stat[:, n:n + 1], stat[:, n:n + 1], 1.0 / D, EPS, ALU.mult, ALU.add))
            pool.tensor_tensor(stat[:, 16 + n:17 + n], stat[:, n:n + 1], stat[:, 32:33], ALU.pow).then_inc(rs_done, 1)

        for n in range(TB):
            root(n)

        for n, (_, tb, kh) in enumerate([s for s in steps if s[0] == "xturn"]):
            pool.wait_ge(nh_done, n + 1)
            pool.tensor_tensor(nhl[:, 4 * kh:4 * kh + 4, tb, 1, :], nT[:, 4 * kh:4 * kh + 4, tb * P:(tb + 1) * P],
                               nhl[:, 4 * kh:4 * kh + 4, tb, 0, :], ALU.subtract).then_inc(nl_done, 1)
        root(TB)
        root(TB + 1)
        pool.wait_ge(rope_ready, 2)

        def rotate(hp, tb):
            n = turn_no[(hp, tb)]
            pool.wait_ge(main_out, main_no[("qk", hp, tb)] + 1)
            if n >= 1:
                done_by_pe(pool, ("turn", *divmod(n - 1, TB)))
                pool.wait_ge(kdec_done, n)
            src = qk[:, n % 2, :].rearrange("p (h c d) -> p h c d", h=4, c=2)
            dst = qkr[:, :].rearrange("p (h c d) -> p h c d", h=4, c=2)
            cos = rope[:, 0, tb, :].unsqueeze(1).to_broadcast([P, 4, 64])
            sin = rope[:, 1, tb, :].unsqueeze(1).to_broadcast([P, 4, 64])
            t = [rt[:, i, :].rearrange("p (h d) -> p h d", h=4) for i in range(2)]
            pool.tensor_tensor(dst[:, :, 0, :], src[:, :, 0, :], cos, ALU.mult)
            pool.tensor_tensor(dst[:, :, 1, :], src[:, :, 0, :], sin, ALU.mult)
            pool.tensor_tensor(t[0], src[:, :, 1, :], sin, ALU.mult)
            link(pool.tensor_tensor(t[1], src[:, :, 1, :], cos, ALU.mult))
            pool.tensor_tensor(dst[:, :, 0, :], dst[:, :, 0, :], t[0], ALU.subtract)
            pool.tensor_tensor(dst[:, :, 1, :], dst[:, :, 1, :], t[1], ALU.add).then_inc(rot_done, 1)

        def gate_value(hp, tb):
            n = turn_no[(hp, tb)]
            pool.wait_ge(gsig_ready, n + 1)
            pool.wait_ge(main_out, main_no[("vg", hp, tb)] + 1)
            th = sg[:, n % 2, 0:256]
            link(pool.tensor_scalar(th, th, 1.0, 0.5, ALU.add, ALU.mult))
            g = vg[:, n % 2, 256:512]
            pool.tensor_tensor(g, g, th, ALU.mult).then_inc(vgate_done, 1)

        def normed(hp, tb):
            n = turn_no[(hp, tb)]
            pool.wait_ge(retraw_done, 2 * n + 2)
            s2, s3 = stat[:, 48:50], stat[:, 50:52]
            link(pool.tensor_scalar(s2, s2, 1.0 / RD, EPS, ALU.mult, ALU.add))
            link(pool.tensor_tensor(s3, s2, stat[:, 32:34], ALU.pow))
            g = vg[:, n % 2, 256:512]
            link(pool.tensor_tensor(g.rearrange("p (h d) -> p h d", h=2), g.rearrange("p (h d) -> p h d", h=2),
                                    s3.unsqueeze(2).to_broadcast([P, 2, P]), ALU.mult))
            pool.tensor_tensor(ret[:, :], ret[:, :], g, ALU.mult).then_inc(ret_done, 1)

        def imaginary(st, hf):
            n = bu_no[("bu", st, hf)]
            pool.wait_ge(scan_done, n + 1)
            pool.tensor_tensor(prod[:, 2, :], ysc[:, hf, 0, :], tab[:, 1, :], ALU.mult).then_inc(half_used, 1)
            link(pool.tensor_tensor(prod[:, 3, :], ysc[:, hf, 1, :], tab[:, 0, :], ALU.mult))
            pool.wait_ge(half_used, n + 1)
            pool.wait_ge(rows_used, n + 1)
            pool.tensor_tensor(ysc[:, hf, 1, :], prod[:, 2, :], prod[:, 3, :], ALU.add).then_inc(xsi_ready, 1)

        for s in steps:
            if s[0] == "states":
                imaginary(s[1], s[2])
            if s[0] == "qk":
                rotate(s[1], s[2])
            if s[0] == "vg":
                gate_value(s[1], s[2])
            if s[0] == "mix":
                normed(s[1], s[2])
            if s[0] == "gate" and s[2] > 0:
                _, dh, br, tb = s
                n = gate_no[s]
                pool.wait_ge(p_out, n + 1)
                pool.tensor_tensor(merged[:, tb, :], merged[:, tb, :], gp[:, n % 2, :], ALU.add).then_inc(merged_done, 1)
            if s[0] == "out" and s[1] == 1:
                tb = s[2]
                pool.wait_ge(hsq_done, tb + 1)
                link(pool.tensor_scalar(root_h[:, tb:tb + 1], root_h[:, tb:tb + 1], 1.0 / D, EPS, ALU.mult, ALU.add))
                pool.tensor_tensor(root_h[:, 8 + tb:9 + tb], root_h[:, tb:tb + 1], stat[:, 32:33], ALU.pow).then_inc(hrs_done, 1)

    @block.scalar
    def _(act):
        chain = 0

        def link(i):
            nonlocal chain
            i.then_inc(achain, 1)
            chain += 1
            act.wait_ge(achain, chain)

        def squares(n, src):
            act.activation(zT[:, n % 2, :], src, ACT.Square, accum_out=stat[:, n:n + 1]).then_inc(sq_done, 1)

        def square_rows(blocks):
            for tb in blocks:
                act.wait_ge(x_in[tb], 16)
                if tb >= 2:
                    act.wait_ge(sq_done, tb - 1)
                squares(tb, xs[:, tb, :])

        square_rows(range(TB // 2))


        sm = lambda k: small[:, k, :]

        def memory_squares():
            act.wait_ge(mem_in, 16)
            act.wait_ge(rope_ready, 1)
            for m in range(2):
                act.activation(btmp[:, m, :, :].rearrange("p s q -> p (s q)"), mem_x[:, m, :], ACT.Square,
                               accum_out=stat[:, TB + m:TB + m + 1]).then_inc(sq_done, 1)

        def parameters():
            act.wait_ge(par_in, 16 * 5)
            act.activation(sm(S_DT), sm(S_LDT), ACT.Exp).then_inc(lam_ready, 1)
            act.wait_ge(ang_ready, 1)
            act.activation(sm(S_MAG), sm(S_T0), ACT.Exp).then_inc(lam_ready, 1)
            act.wait_ge(ang_ready, 2)
            act.activation(sm(S_SIN), sm(S_T1), ACT.Sin).then_inc(lam_ready, 1)
            act.activation(sm(S_COS), sm(S_T2), ACT.Sin).then_inc(lam_ready, 1)
            act.wait_ge(rope_ready, 1)
            act.activation(rope[:, :, :, :], rope[:, :, :, :], ACT.Sin).then_inc(rope_ready, 1)

        for s in steps:
            if s[0] == "param":
                (parameters, memory_squares)[s[1]]()
                if s[1] == 0:
                    square_rows(range(TB // 2, TB))
            if s[0] == "split":
                k = split_no[s]
                target_free(act, s)
                act.wait_ge(staged[k % 2], STAGED[s])
                act.activation(split_target(s)[0], split_source(s), ACT.Copy).then_inc(split_hi, 1)
            if s[0] == "xturn":
                _, tb, kh = s
                act.wait_ge(misc_out, misc_no[s] + 1)
                act.activation(nhl[:, 4 * kh:4 * kh + 4, tb, 0, :], nT[:, 4 * kh:4 * kh + 4, tb * P:(tb + 1) * P],
                               ACT.Copy).then_inc(nh_done, 1)
            if s[0] in MAIN:
                m = main_no[s]
                act.wait_ge(main_full, m + 1)
                src = main_ps[m % 2][:, :]
            if s[0] == "z":
                _, ct, hf = s
                act.wait_ge(sq_done, TB)
                act.activation(zT[:, ct, hf * HALF:(hf + 1) * HALF], src, ACT.Copy).then_inc(main_out, 1)
            elif s[0] == "qk":
                n = turn_no[(s[1], s[2])]
                if n >= 2:
                    act.wait_ge(rot_done, n - 1)
                if n == 0:
                    done_by_pe(act, ("bturn", S5T - 2))
                act.activation(qk[:, n % 2, :], src, ACT.Copy).then_inc(main_out, 1)
            elif s[0] == "vg":
                n = turn_no[(s[1], s[2])]
                if n >= 2:
                    done_by_pe(act, ("mix", *divmod(n - 2, TB)))
                    act.wait_ge(ret_done, n - 1)
                    act.wait_ge(vgate_done, n - 1)
                act.activation(sg[:, n % 2, 0:256], src[:, 256:512], ACT.Tanh, scale=0.5).then_inc(gsig_ready, 1)
                act.activation(vg[:, n % 2, :], src, ACT.Copy).then_inc(main_out, 1)
            elif s[0] == "gate":
                n = gate_no[s]
                if n >= 2:
                    act.wait_ge(p_out, n - 1)
                else:
                    act.wait_ge(vgate_done, 2 * TB)
                act.activation(sg[:, n % 2, :], src, ACT.Tanh, scale=0.5).then_inc(main_out, 1)
            elif s[0] == "turn":
                _, hp, tb = s
                n = turn_no[(hp, tb)]
                act.wait_ge(rot_done, n + 1)
                if n >= 2:
                    done_by_pe(act, ("mix", *divmod(n - 2, TB)))
                for h in range(2):
                    i = act.activation(kdec[:, n % 2, h * P:(h + 1) * P], qkr[:, 256 + h * P:256 + (h + 1) * P], ACT.Copy,
                                       scale=con[:, C_KF + 2 * hp + h:C_KF + 2 * hp + h + 1])
                i.then_inc(kdec_done, 1)
            elif s[0] == "mix":
                _, hp, tb = s
                n = turn_no[(hp, tb)]
                done_by_pe(act, s)
                if n:
                    done_by_pe(act, ("flip", *divmod(n - 1, TB)))
                for h in range(2):
                    src = misc_ps[misc_no[s] % 2][:, h * P:(h + 1) * P]
                    qf = con[:, C_QF + 2 * hp + h:C_QF + 2 * hp + h + 1]
                    act.activation(ret[:, h * P:(h + 1) * P], src, ACT.Copy, scale=qf)
                    if n or h:
                        act.wait_ge(retraw_done, 2 * n + h)
                    act.activation(junk[:, :], src, ACT.Square, scale=qf, accum_out=stat[:, 48 + h:49 + h]).then_inc(retraw_done, 1)
            elif s[0] == "ascore":
                act.wait_ge(misc_out, misc_no[s] + 1)
                act.activation(psc[:, :], psc[:, :], ACT.Exp, scale=MD ** -0.5).then_inc(exp_ready, 1)
            elif s[0] == "y" and s[1] % 4 == 3:
                ct, hf = s[1] // 4, s[2]
                act.wait_ge(ydu_ready, 2 * ct + hf + 1)
                u = zT[:, ct, hf * HALF:(hf + 1) * HALF]
                act.activation(u, u, ACT.Gelu_apprx_tanh).then_inc(gelu_ready, 1)
            elif s[0] == "out" and s[1] == 1:
                tb = s[2]
                act.wait_ge(misc_out, misc_no[s] + 1)
                if tb >= 2:
                    act.wait_ge(hsq_done, tb - 1)
                act.activation(nT[:, tb % 2, :], h_sb[:, tb, :], ACT.Square,
                               accum_out=root_h[:, tb:tb + 1]).then_inc(hsq_done, 1)
            elif s[0] == "glu":
                hf = s[1]
                done_by_pe(act, s)
                for o, ps in enumerate((misc_ps[misc_no[s] % 2], bu_ps[1])):
                    act.activation(zT[:, o, hf * HALF:(hf + 1) * HALF], ps[:, :], ACT.Tanh, scale=0.5).then_inc(glu_tanh, 1)

    @block.tensor
    def _(pe):
        ident = con[:, C_ID:C_ID + P]

        def free(s):
            n = misc_no[s]
            if n >= 2:
                pe.wait_ge(misc_out, n - 1)
            return misc_ps[n % 2]

        def main_free(s):
            m = main_no[s]
            if m >= 2:
                pe.wait_ge(main_out, m - 1)
            return main_ps[m % 2]

        def three(ps, a, b, first, last):
            pe.matmul(ps, a(0), b(0), start=first, stop=False)
            pe.matmul(ps, a(0), b(1), start=False, stop=False)
            return pe.matmul(ps, a(1), b(0), start=False, stop=last)

        def projection(unit, q):
            kind, arg, tb = unit[0], unit[1:-1], unit[-1]
            if q == 0:
                pe.wait_ge(nl_done, 2 * TB)
                main_free(unit)
                weights(pe, kind, arg[0] if kind != "gate" else arg)
            w = wring[BUFFER[LOAD_NO[(kind, arg[0] if kind != "gate" else arg)]]]
            ps = main_ps[main_no[unit] % 2]
            for kd in range(q * KD // QUARTERS, (q + 1) * KD // QUARTERS):
                mm = three(ps[:, :], lambda i: nhl[:, kd, tb, i, :], lambda i: w[:, kd, i, :], kd == 0, kd == KD - 1)
            return mm

        pe.wait_ge(con_in, 16)
        for s in steps:
            k = s[0]
            if k == "xturn":
                _, tb, kh = s
                ps = free(s)
                pe.wait_ge(n_ready, tb + 1)
                for i in range(4):
                    mm = pe.transpose(ps[:, i * P:(i + 1) * P], xs[:, tb, (4 * kh + i) * P:(4 * kh + i + 1) * P], ident)
                mm.then_inc(misc_full, 1)
            elif k == "mturn":
                _, mt, kh = s
                ps = free(s)
                pe.wait_ge(n_ready, TB + mt + 1)
                for i in range(4):
                    mm = pe.transpose(ps[:, i * P:(i + 1) * P], mem_x[:, mt, (4 * kh + i) * P:(4 * kh + i + 1) * P], ident)
                mm.then_inc(misc_full, 1)
            elif k == "bturn":
                ps = free(s)
                pe.wait_ge(bb_ready, 1)
                for i in range(4):
                    mm = pe.transpose(ps[:, i * P:(i + 1) * P], bsrc[:, i // 2, s[1] + i % 2, :], ident)
                mm.then_inc(misc_full, 1)
            elif k == "z":
                _, ct, hf = s
                w = wfull
                pe.wait_ge(wfull_in, 16)
                ps = main_free(s)
                pe.wait_ge(misc_out, misc_no[("xturn", 4 * hf + 3, 1)] + 1)
                for kd in range(KD):
                    mm = pe.matmul(ps[:, :], w[:, kd, ct * P:(ct + 1) * P], nT[:, kd, hf * HALF:(hf + 1) * HALF],
                                   start=kd == 0, stop=kd == KD - 1)
                mm.then_inc(main_full, 1)
            elif k == "open":
                projection(*s[1:])
            elif k in ("qk", "vg"):
                projection(s, QUARTERS - 1).then_inc(main_full, 1)
            elif k == "mk":
                w = wfull
                pe.wait_ge(wfull_in, 32)
                ps = free(s)
                pe.wait_ge(misc_out, misc_no[("mturn", 1, 1)] + 1)
                for kd in range(KD):
                    mm = pe.matmul(ps[:, 0:MEM], w[:, kd, s[1] * P:(s[1] + 1) * P], memT[:, kd, :],
                                   start=kd == 0, stop=kd == KD - 1)
                mm.then_inc(misc_full, 1)
            elif k == "mv":
                w = wfull
                pe.wait_ge(wfull_in, 32)
                ps = free(s)
                for kd in range(KD):
                    mm = pe.matmul(ps[:, 0:256], memT[:, kd, s[1] * P:(s[1] + 1) * P], w[:, kd, 256:512],
                                   start=kd == 0, stop=kd == KD - 1)
                mm.then_inc(misc_full, 1)
            elif k == "turn":
                _, hp, tb = s
                ps = free(s)
                pe.wait_ge(rot_done, turn_no[(hp, tb)] + 1)
                for i in range(4):
                    mm = pe.transpose(ps[:, i * P:(i + 1) * P], qkr[:, i * P:(i + 1) * P], ident)
                mm.then_inc(misc_full, 1)
            elif k == "score":
                _, hp, tb = s
                n = turn_no[(hp, tb)]
                ps = free(s)
                pe.wait_ge(misc_out, misc_no[("turn", hp, tb)] + 1)
                for h in range(2):
                    mm = pe.matmul(ps[:, h * P:(h + 1) * P], qkT[:, n % 2, 256 + h * P:256 + (h + 1) * P],
                                   qkT[:, n % 2, h * P:(h + 1) * P], start=True, stop=True)
                mm.then_inc(misc_full, 1)
            elif k == "mix":
                _, hp, tb = s
                n = turn_no[(hp, tb)]
                ps = free(s)
                pe.wait_ge(misc_out, misc_no[("score", hp, tb)] + 1)
                pe.wait_ge(kdec_done, n + 1)
                pe.wait_ge(main_out, main_no[("vg", hp, tb)] + 1)
                for h in range(2):
                    v = vg[:, n % 2, h * P:(h + 1) * P]
                    pe.matmul(ps[:, h * P:(h + 1) * P], sT[:, h * P:(h + 1) * P], v, start=True, stop=tb == 0)
                    if tb:
                        pe.matmul(ps[:, h * P:(h + 1) * P], qkT[:, n % 2, h * P:(h + 1) * P],
                                  state[:, 2 * hp + h, :], start=False, stop=True)
                    mm = pe.matmul(ps[:, 256 + h * P:256 + (h + 1) * P], kdec[:, n % 2, h * P:(h + 1) * P], v,
                                   start=True, stop=True)
                mm.then_inc(misc_full, 1)
            elif k == "flip":
                _, hp, tb = s
                ps = free(s)
                pe.wait_ge(ret_done, turn_no[(hp, tb)] + 1)
                for h in range(2):
                    mm = pe.transpose(ps[:, h * P:(h + 1) * P], ret[:, h * P:(h + 1) * P], ident)
                mm.then_inc(misc_full, 1)
            elif k == "ascore":
                _, tb, mp = s
                ps = free(s)
                pe.wait_ge(main_out, main_no[("z", 3, 1)] + 1)
                pe.wait_ge(misc_out, misc_no[("mv", 1)] + 1)
                for h in range(2):
                    mm = pe.matmul(ps[:, h * MEM:(h + 1) * MEM],
                                   zT[:, 2 + mp, tb * P:(tb + 1) * P], kmT[:, mp, h, :], start=True, stop=True)
                mm.then_inc(misc_full, 1)
            elif k == "aturn":
                _, tb, mp = s
                ps = free(s)
                pe.wait_ge(exp_ready, chain_no[(tb, mp)] + 1)
                for i in range(4):
                    mm = pe.transpose(ps[:, i * P:(i + 1) * P], psc[:, i * P:(i + 1) * P], ident)
                mm.then_inc(misc_full, 1)
            elif k == "amix":
                _, tb, mp = s
                ps = free(s)
                pe.wait_ge(misc_out, misc_no[("aturn", tb, mp)] + 1)
                for h in range(2):
                    for mt in range(2):
                        mm = pe.matmul(ps[:, h * MD:(h + 1) * MD], pT[:, (2 * h + mt) * P:(2 * h + mt + 1) * P],
                                       vm[:, mt, (2 * mp + h) * MD:(2 * mp + h + 1) * MD],
                                       start=mt == 0, stop=mt == 1)
                mm.then_inc(misc_full, 1)
            elif k == "aflip":
                _, tb, mp = s
                ps = free(s)
                pe.wait_ge(misc_out, misc_no[("amix", tb, mp)] + 1)
                pe.transpose(ps[:, 0:P], mo[:, :], ident).then_inc(misc_full, 1)
            elif k == "bu":
                _, st, hf = s
                n = bu_no[s]
                if n:
                    pe.wait_ge(bu_out, n)
                pe.wait_ge(misc_out, misc_no[("bturn", 6)] + 1)
                pe.wait_ge(main_out, main_no[("z", 3, 1)] + 1)
                for c in range(2):
                    mm = pe.matmul(bu_ps[c][:, :], bbT[:, c, st, :], zT[:, st // 4, hf * HALF:(hf + 1) * HALF],
                                   start=True, stop=True)
                mm.then_inc(bu_full, 1)
            elif k == "y":
                _, st, hf = s
                pe.wait_ge(xst_ready, 2 * st + hf + 1)
                pe.wait_ge(xsi_ready, 2 * st + hf + 1)
                pe.wait_ge(cneg_ready, 1)
                if st == 4:
                    pe.wait_ge(ydu_ready, hf + 1)
                for c in range(2):
                    mm = pe.matmul(y_ps[hf][:, :], cT[:, c, st, :], ysc[:, hf, c, :],
                                   start=st % 4 == 0 and c == 0, stop=st % 4 == 3 and c == 1)
                mm.then_inc(y_full, 1)
            elif k == "glu":
                hf = s[1]
                ps = free(s)
                pe.wait_ge(gelu_ready, 4)
                if hf:
                    pe.wait_ge(misc_out, misc_no[("glu", 0)] + 1)
                for bank, col in ((ps, 2), (bu_ps[1], 3), (bu_ps[0], 0), (y_ps[hf], 1)):
                    for c in range(2):
                        mm = pe.matmul(bank[:, :], wglu[:, c, col * P:(col + 1) * P],
                                       zT[:, c, hf * HALF:(hf + 1) * HALF], start=c == 0, stop=c == 1)
                mm.then_inc(misc_full, 1)
            elif k == "gate":
                _, dh, br, tb = s
                n = gate_no[s]
                projection(s, QUARTERS - 1).then_inc(main_full, 1)
                if n >= 2:
                    pe.wait_ge(p_out, n - 1)
                src, first, rows = ((zhl[:, 0:2], 4, 2), (zhl[:, 2:4], 6, 2), (retT, 0, 4))[br]
                if tb == 0 and dh == 0:
                    last = (("glu", 1), ("aflip", TB - 1, 1), ("flip", 1, TB - 1))[br]
                    pe.wait_ge(misc_out, misc_no[last] + 1)
                    branch_weights(pe, first + rows - 1)
                cols = slice(dh * HALF, (dh + 1) * HALF)
                for i in range(rows):
                    mm = three(p_ps[n % 2][:, :], lambda c: src[:, i, tb, c, :], lambda c: wbr[:, first + i, c, cols],
                               i == 0, i == rows - 1)
                mm.then_inc(p_full, 1)
            elif k == "gturn":
                _, dh, tb = s
                ps = free(s)
                pe.wait_ge(merged_done, dh * 2 * TB + TB + tb + 1)
                for i in range(4):
                    mm = pe.transpose(ps[:, i * P:(i + 1) * P], merged[:, tb, i * P:(i + 1) * P], ident)
                mm.then_inc(misc_full, 1)
            elif k == "out":
                _, dh, tb = s
                w = weights(pe, "out", dh)
                ps = free(s)
                pe.wait_ge(misc_out, misc_no[("gturn", 1, TB - 1)] + 1)
                for kd in range(KD):
                    src = merT_lo if kd < 4 else merT_hi
                    mm = three(ps[:, :], lambda i: src[:, kd % 4, tb, i, :], lambda i: w[:, kd, i, :],
                               kd == 0, kd == KD - 1)
                mm.then_inc(misc_full, 1)


    @block.vector
    def _(dve):
        chain = 0

        def link(i):
            nonlocal chain
            i.then_inc(dchain, 1)
            chain += 1
            dve.wait_ge(dchain, chain)

        sm = lambda k: small[:, k, :]
        tt, ts, stt = dve.tensor_tensor, dve.tensor_scalar, dve.scalar_tensor_tensor

        def reduced(dst_sin, dst_cos, ang, tmp):
            link(ts(tmp, ang, 1.0 / (2.0 * math.pi), MAGIC, ALU.mult, ALU.add))
            link(ts(tmp, tmp, -MAGIC, None, ALU.add))
            link(stt(dst_sin, tmp, -TWO_PI_HI, ang, ALU.mult, ALU.add))
            link(stt(dst_sin, tmp, -TWO_PI_MID, dst_sin, ALU.mult, ALU.add))
            link(stt(dst_sin, tmp, -TWO_PI_LO, dst_sin, ALU.mult, ALU.add))
            link(ts(dst_sin, dst_sin, PI_BELOW, -PI_BELOW, ALU.min, ALU.max))
            link(stt(dst_cos, dst_sin, -1.0, dst_sin, ALU.mult, ALU.max))
            return ts(dst_cos, dst_cos, -1.0, math.pi / 2, ALU.mult, ALU.add)

        def norm(tb):
            dve.wait_ge(rs_done, tb + 1)
            ts(xs[:, tb, :], xs[:, tb, :], stat[:, 16 + tb:17 + tb], None, ALU.mult).then_inc(n_ready, 1)

        def parameters():
            dve.wait_ge(lam_ready, 1)
            tt(sm(S_T0), sm(S_ARE), sm(S_DT), ALU.mult).then_inc(ang_ready, 1)
            link(tt(sm(S_TH), sm(S_AIM), sm(S_DT), ALU.mult))
            reduced(sm(S_T1), sm(S_T2), sm(S_TH), sm(S_T3)).then_inc(ang_ready, 1)
            link(dve.tensor_copy(sm(S_POS), sm(S_POSI).bitcast(I32)))
            ang, tmp = btmp[:, 0, :, 0:64], btmp[:, 1, :, 0:64]
            inv = con[:, C_INV:C_INV + 64].unsqueeze(1).to_broadcast([P, TB, 64])
            pos = sm(S_POS).unsqueeze(2).to_broadcast([P, TB, 64])
            link(tt(ang, pos, inv, ALU.mult))
            reduced(rope[:, 1, :, :], rope[:, 0, :, :], ang, tmp).then_inc(rope_ready, 1)
            dve.wait_ge(rope_ready, 1)
            dve.wait_ge(lam_ready, 4)
            link(tt(sm(S_LRE), sm(S_MAG), sm(S_COS), ALU.mult))
            link(tt(sm(S_LIM), sm(S_MAG), sm(S_SIN), ALU.mult))
            link(ts(sm(S_LRE), sm(S_LRE), -1.0, None, ALU.add))
            link(tt(sm(S_T0), sm(S_ARE), sm(S_ARE), ALU.mult))
            link(tt(sm(S_T3), sm(S_AIM), sm(S_AIM), ALU.mult))
            link(tt(sm(S_DEN), sm(S_T0), sm(S_T3), ALU.add))
            link(dve.reciprocal(sm(S_DEN), sm(S_DEN)))
            link(tt(sm(S_T0), sm(S_LRE), sm(S_ARE), ALU.mult))
            link(tt(sm(S_T3), sm(S_LIM), sm(S_AIM), ALU.mult))
            link(tt(sm(S_T0), sm(S_T0), sm(S_T3), ALU.add))
            link(tt(sm(S_CR), sm(S_T0), sm(S_DEN), ALU.mult))
            link(tt(sm(S_T0), sm(S_LIM), sm(S_ARE), ALU.mult))
            link(tt(sm(S_T3), sm(S_LRE), sm(S_AIM), ALU.mult))
            link(tt(sm(S_T0), sm(S_T0), sm(S_T3), ALU.subtract))
            link(tt(sm(S_CI), sm(S_T0), sm(S_DEN), ALU.mult))

        def input_matrices():
            dve.wait_ge(sq_done, TB + 2)
            dve.wait_ge(b_in, 32)
            cr = sm(S_CR).unsqueeze(2).to_broadcast([P, S5T, P])
            ci = sm(S_CI).unsqueeze(2).to_broadcast([P, S5T, P])
            re, im, t0, t1 = bsrc[:, 0, :, :], bsrc[:, 1, :, :], btmp[:, 0, :, :], btmp[:, 1, :, :]
            tt(t0, im, ci, ALU.mult)
            link(tt(t1, re, ci, ALU.mult))
            tt(re, re, cr, ALU.mult)
            link(tt(im, im, cr, ALU.mult))
            tt(re, re, t0, ALU.subtract)
            tt(im, im, t1, ALU.add).then_inc(bb_ready, 1)
            dve.wait_ge(c_in, 48)
            ts(cT[:, 1, :, :], cT[:, 1, :, :], -1.0, None, ALU.mult).then_inc(cneg_ready, 1)
            dve.tensor_copy(levels[:, 0, 0, :], sm(S_COS))
            link(dve.tensor_copy(levels[:, 1, 0, :], sm(S_SIN)))
            for k in range(8):
                cn, sn, c2, s2 = levels[:, 0, k, :], levels[:, 1, k, :], levels[:, 0, k + 1, :], levels[:, 1, k + 1, :]
                tt(sm(S_T0), sn, sn, ALU.mult)
                tt(sm(S_T1), cn, sn, ALU.mult)
                link(tt(c2, cn, cn, ALU.mult))
                tt(c2, c2, sm(S_T0), ALU.subtract)
                link(ts(s2, sm(S_T1), 2.0, None, ALU.mult))
            dve.memset(btab[:, 0, :, 0:1], 1.0)
            link(dve.memset(btab[:, 1, :, 0:1], 0.0))
            for k in range(4):
                n = 1 << k
                cn = levels[:, 0, k, :].unsqueeze(2).to_broadcast([P, S5T, n])
                sn = levels[:, 1, k, :].unsqueeze(2).to_broadcast([P, S5T, n])
                c, s_, t0, t1 = btab[:, 0, :, 0:n], btab[:, 1, :, 0:n], btmp[:, 0, :, 0:n], btmp[:, 1, :, 0:n]
                tt(t0, s_, sn, ALU.mult)
                tt(t1, c, sn, ALU.mult)
                tt(btab[:, 0, :, n:2 * n], c, cn, ALU.mult)
                link(tt(btab[:, 1, :, n:2 * n], s_, cn, ALU.mult))
                tt(btab[:, 0, :, n:2 * n], btab[:, 0, :, n:2 * n], t0, ALU.subtract)
                link(tt(btab[:, 1, :, n:2 * n], btab[:, 1, :, n:2 * n], t1, ALU.add))
            for m in range(2):
                dve.wait_ge(rs_done, TB + m + 1)
                ts(mem_x[:, m, :], mem_x[:, m, :], stat[:, 24 + m:25 + m], None, ALU.mult).then_inc(n_ready, 1)

        def tables(st, part):
            if part == 0 and st:
                dve.wait_ge(xst_ready, 2 * st)
                dve.wait_ge(xsi_ready, 2 * st)
            if part == 0 and st == 0:
                done_by_pe(dve, ("z", 3, 1))
                dve.wait_ge(nl_done, 2 * TB)
            c, s_ = tab[:, 0, :], tab[:, 1, :]
            if part == 0:
                link(dve.tensor_copy(tab[:, :, 0:16], btab[:, :, st, :]))
            for k in ((4, 5, 6), (7,), (8,))[part]:
                n = 1 << k
                cn, sn = levels[:, 0, k, st:st + 1], levels[:, 1, k, st:st + 1]
                tmp_c, tmp_s = prod[:, 0, 0:n], prod[:, 1, 0:n]
                ts(tmp_c, s_[:, 0:n], sn, None, ALU.mult)
                link(ts(tmp_s, c[:, 0:n], sn, None, ALU.mult))
                stt(c[:, n:2 * n], c[:, 0:n], cn, tmp_c, ALU.mult, ALU.subtract)
                link(stt(s_[:, n:2 * n], s_[:, 0:n], cn, tmp_s, ALU.mult, ALU.add))

        def pair_out(hi, lo, src, factor=None):
            if factor is None:
                link(dve.tensor_copy(hi, src))
                return tt(lo, src, hi, ALU.subtract)
            link(ts(hi, src, factor, None, ALU.mult))
            return stt(lo, src, factor, hi, ALU.mult, ALU.subtract)

        def copy_out(s, dst, cols=HALF):
            n = misc_no[s]
            dve.wait_ge(misc_full, n + 1)
            dve.tensor_copy(dst, misc_ps[n % 2][:, 0:cols]).then_inc(misc_out, 1)

        dve.wait_ge(gain_in, 16 * 2)
        norm(0)
        for s in steps:
            k = s[0]
            if k in ("xturn", "mturn"):
                n = misc_no[s]
                _, b, kh = s
                if k == "xturn" and kh == 0 and b == TB // 2:
                    norm(b)
                if k == "xturn" and kh == 0 and b + 1 < TB and b + 1 != TB // 2:
                    norm(b + 1)
                dve.wait_ge(misc_full, n + 1)
                dst = (nT if k == "xturn" else memT)[:, 4 * kh:4 * kh + 4, b * P:(b + 1) * P]
                g = gains[:, 0 if k == "xturn" else 1, 4 * kh:4 * kh + 4].unsqueeze(2).to_broadcast([P, 4, P])
                tt(dst, misc_ps[n % 2][:, :].rearrange("p (k t) -> p k t", k=4), g, ALU.mult).then_inc(misc_out, 1)
            elif k == "param":
                (parameters, input_matrices)[s[1]]()
            elif k == "split":
                n = split_no[s]
                dve.wait_ge(split_hi, n + 1)
                hi, lo = split_target(s)
                tt(lo, split_source(s), hi, ALU.subtract).then_inc(split_done, 1)
            elif k == "bturn":
                n = misc_no[s]
                dve.wait_ge(misc_full, n + 1)
                dve.tensor_copy(bbT[:, :, s[1]:s[1] + 2, :],
                                misc_ps[n % 2][:, :].rearrange("p (c s q) -> p c s q", c=2, s=2)).then_inc(misc_out, 1)
            elif k == "mk":
                n = misc_no[s]
                link(dve.memset(kmT[:, s[1], :, :], 0.0))
                dve.wait_ge(misc_full, n + 1)
                for h in range(2):
                    rows = slice(h * MD, (h + 1) * MD)
                    i = dve.tensor_copy(kmT[rows, s[1], h, :], misc_ps[n % 2][rows, 0:MEM])
                i.then_inc(misc_out, 1)
            elif k == "mv":
                copy_out(s, vm[:, s[1], :], 256)
            elif k == "turn":
                _, hp, tb = s
                n = turn_no[(hp, tb)]
                if n >= 2:
                    done_by_pe(dve, ("mix", *divmod(n - 2, TB)))
                copy_out(s, qkT[:, n % 2, :])
            elif k == "score":
                _, hp, tb = s
                n = turn_no[(hp, tb)]
                if n:
                    done_by_pe(dve, ("mix", *divmod(n - 1, TB)))
                dve.wait_ge(misc_full, misc_no[s] + 1)
                dec = con[:, C_DEC + 2 * hp * P:C_DEC + (2 * hp + 2) * P]
                tt(sT[:, :], misc_ps[misc_no[s] % 2][:, 0:256], dec, ALU.mult).then_inc(misc_out, 1)
            elif k == "mix":
                _, hp, tb = s
                n = turn_no[(hp, tb)]
                dve.wait_ge(misc_full, misc_no[s] + 1)
                ps = misc_ps[misc_no[s] % 2]
                dve.wait_ge(retraw_done, 2 * n + 2)
                for h in range(2):
                    kv, st = ps[:, 256 + h * P:256 + (h + 1) * P], state[:, 2 * hp + h, :]
                    if tb == 0:
                        i = dve.tensor_copy(st, kv)
                    else:
                        i = stt(st, st, GAMMA[2 * hp + h] ** P, kv, ALU.mult, ALU.add)
                i.then_inc(misc_out, 1)
            elif k == "flip":
                _, hp, tb = s
                n = misc_no[s]
                dve.wait_ge(misc_full, n + 1)
                if n == misc_no[("flip", 0, 0)]:
                    done_by_pe(dve, ("mv", 1))
                dst = retT[:, 2 * hp:2 * hp + 2, tb, :, :]
                src = misc_ps[n % 2][:, 0:256].rearrange("p (h t) -> p h t", h=2)
                pair_out(dst[:, :, 0, :], dst[:, :, 1, :], src).then_inc(misc_out, 1)
            elif k == "ascore":
                _, tb, mp = s
                c = chain_no[(tb, mp)]
                dve.wait_ge(misc_full, misc_no[s] + 1)
                ps = misc_ps[misc_no[s] % 2][:, :].rearrange("p (h m) -> p h m", h=2)
                link(dve.tensor_reduce(stat[:, 52:54], ps, AX.X, ALU.max))
                tt(psc[:, :].rearrange("p (h m) -> p h m", h=2), ps,
                   stat[:, 52:54].unsqueeze(2).to_broadcast([P, 2, MEM]), ALU.subtract).then_inc(misc_out, 1)
            elif k == "aturn":
                _, tb, mp = s
                dve.wait_ge(exp_ready, chain_no[(tb, mp)] + 1)
                link(dve.tensor_reduce(stat[:, 54:56], psc[:, :].rearrange("p (h m) -> p h m", h=2), AX.X, ALU.add))
                link(dve.reciprocal(stat[:, 56:58], stat[:, 54:56]))
                copy_out(s, pT[:, :])
            elif k == "amix":
                n = misc_no[s]
                dve.wait_ge(misc_full, n + 1)
                tt(mo[:, :].rearrange("p (h d) -> p h d", h=2), misc_ps[n % 2][:, 0:P].rearrange("p (h d) -> p h d", h=2),
                   stat[:, 56:58].unsqueeze(2).to_broadcast([P, 2, MD]), ALU.mult).then_inc(misc_out, 1)
            elif k == "aflip":
                _, tb, mp = s
                n = misc_no[s]
                dve.wait_ge(misc_full, n + 1)
                pair_out(zhl[:, 2 + mp, tb, 0, :], zhl[:, 2 + mp, tb, 1, :], misc_ps[n % 2][:, 0:P]).then_inc(misc_out, 1)
            elif k == "bu":
                _, st, hf = s
                n = bu_no[s]
                c, sn_t = tab[:, 0, :], tab[:, 1, :]
                dve.wait_ge(bu_full, n + 1)
                if n:
                    dve.wait_ge(xsi_ready, n)
                tt(prod[:, 0, :], bu_ps[0][:, :], c, ALU.mult)
                tt(prod[:, 1, :], bu_ps[1][:, :], sn_t, ALU.mult)
                tt(prod[:, 2, :], bu_ps[1][:, :], c, ALU.mult)
                tt(prod[:, 3, :], bu_ps[0][:, :], sn_t, ALU.mult).then_inc(bu_out, 1)
            elif k == "tables":
                tables(*s[1:])
            elif k == "scan":
                _, st, hf = s
                dve.wait_ge(bu_out, bu_no[("bu", st, hf)] + 1)
                tt(prod[:, 0, :], prod[:, 0, :], prod[:, 1, :], ALU.add)
                link(tt(prod[:, 2, :], prod[:, 2, :], prod[:, 3, :], ALU.subtract))
                if st:
                    dve.wait_ge(y_full, 2 * (st - 1) + hf + 1)
                mag = small[:, S_MAG, st:st + 1].to_broadcast([P, HALF])
                if hf == 1:
                    dve.wait_ge(xsi_ready, 2 * st + 1)
                    cn, sn = levels[:, 0, 0, st:st + 1], levels[:, 1, 0, st:st + 1]
                    xr_, xi_ = ysc[:, 0, 0, HALF - 1:HALF], ysc[:, 0, 1, HALF - 1:HALF]
                    tt(small[:, S_T0, 0:1], xi_, sn, ALU.mult)
                    link(tt(small[:, S_T1, 0:1], xr_, sn, ALU.mult))
                    stt(small[:, S_CN, 1:2], xr_, cn, small[:, S_T0, 0:1], ALU.mult, ALU.subtract)
                    link(stt(small[:, S_SN, 1:2], xi_, cn, small[:, S_T1, 0:1], ALU.mult, ALU.add))
                for c2 in range(2):
                    init = 0.0 if hf == 0 else small[:, S_CN + c2, 1:2]
                    i = dve.tensor_tensor_scan(ysc[:, hf, c2, :], mag, prod[:, 2 * c2, :], init, ALU.mult, ALU.add)
                i.then_inc(scan_done, 1)
            elif k == "states":
                _, st, hf = s
                n = bu_no[("bu", st, hf)]
                dve.wait_ge(scan_done, n + 1)
                tt(prod[:, 0, :], ysc[:, hf, 0, :], tab[:, 0, :], ALU.mult)
                tt(prod[:, 1, :], ysc[:, hf, 1, :], tab[:, 1, :], ALU.mult).then_inc(rows_used, 1)
                dve.wait_ge(rows_used, n + 1)
                dve.wait_ge(half_used, n + 1)
                tt(ysc[:, hf, 0, :], prod[:, 0, :], prod[:, 1, :], ALU.subtract).then_inc(xst_ready, 1)
                dve.wait_ge(xst_ready, n + 1)
            elif k == "y" and s[1] % 4 == 3:
                ct, hf = s[1] // 4, s[2]
                dve.wait_ge(y_full, 2 * s[1] + hf + 1)
                u = zT[:, ct, hf * HALF:(hf + 1) * HALF]
                stt(u, u, small[:, S_D, ct:ct + 1], y_ps[hf][:, :], ALU.mult, ALU.add).then_inc(ydu_ready, 1)
            elif k == "glu":
                hf = s[1]
                dve.wait_ge(glu_tanh, 2 * hf + 2)
                done_by_pe(dve, s)
                both = zT[:, 0:2, hf * HALF:(hf + 1) * HALF]
                link(ts(both, both, 1.0, 0.5, ALU.add, ALU.mult))
                for o, bank in enumerate((bu_ps[0], y_ps[hf])):
                    i = tt(prod[:, o, :], zT[:, o, hf * HALF:(hf + 1) * HALF], bank[:, :], ALU.mult)
                link(i)
                dst = zhl[:, 0:2, 4 * hf:4 * hf + 4, :, :]
                for o in range(2):
                    src = prod[:, o, :].rearrange("p (b t) -> p b t", b=4)
                    i = pair_out(dst[:, o, :, 0, :], dst[:, o, :, 1, :], src)
                i.then_inc(misc_out, 1)
            elif k == "gate":
                _, dh, br, tb = s
                n = gate_no[s]
                dve.wait_ge(p_full, n + 1)
                dve.wait_ge(main_out, main_no[s] + 1)
                if br == 0:
                    if dh:
                        done_by_pe(dve, ("gturn", 0, tb))
                    elif tb == 0:
                        done_by_pe(dve, ("glu", 1))
                    dst = merged[:, tb, :]
                else:
                    if (dh, br, tb) == (0, 1, 0):
                        done_by_pe(dve, ("flip", 1, TB - 1))
                        done_by_pe(dve, ("aflip", TB - 1, 1))
                    if n - TB * (dh + 1) >= 2:
                        dve.wait_ge(merged_done, n - TB * (dh + 1) - 1)
                    dst = gp[:, n % 2, :]
                i = stt(dst, sg[:, n % 2, :], 1.0, p_ps[n % 2][:, :], ALU.add, ALU.mult)
                i.then_inc(p_out, 1)
            elif k == "gturn":
                _, dh, tb = s
                n = misc_no[s]
                dve.wait_ge(misc_full, n + 1)
                dst = (merT_lo, merT_hi)[dh][:, :, tb, :, :]
                src = misc_ps[n % 2][:, :].rearrange("p (k t) -> p k t", k=4)
                pair_out(dst[:, :, 0, :], dst[:, :, 1, :], src, 0.5).then_inc(misc_out, 1)
            elif k == "out":
                _, dh, tb = s
                n = misc_no[s]
                j = dh * TB + tb
                dve.wait_ge(misc_full, n + 1)
                dve.wait_ge(xr_in[j % 2], 16 * (j // 2 + 1))
                tt(h_sb[:, tb, dh * HALF:(dh + 1) * HALF], misc_ps[n % 2][:, :], xr[:, j % 2, :],
                   ALU.add).then_inc(misc_out, 1)
    ctx.close()


PH, PK, NK = 8, 16, 128
HC = 2 * PH
PAIRS = [(0, 1, 16), (1, 1, 8), (2, 1, 5), (3, 1, 4), (4, 1, 3), (5, 3, 2), (8, 8, 1)]
NCAND = sum(na * nb for _, na, nb in PAIRS)
NEG = -3.0e38
CH = NK
GT = 16
WT = 64
CG = 4
NW = SEQ // WT
SEL = 6
SEL_END = SEL * TB
HOT_BEGIN = SEL_END + 2
HOT_END = HOT_BEGIN + SEQ // GT


def build_scores(nc, ins, h_sb, root_h, gain, xh, xl, s_sb, u_first, mem_map):
    ctx = ExitStack()
    at = dict(mem_map)

    def sb(region, name, shape, dt=F32):
        size = int(np.prod(shape[1:])) * (2 if dt == BF16 else 4)
        off = at[region]
        at[region] = off + (size + 31) // 32 * 32
        assert at[region] <= mem_map[region] + mem_map[region + "_size"], (region, name)
        return nc.alloc_sbuf_tensor_at(name, shape, dt, offset=off)

    def sem(name):
        return ctx.enter_context(nc.semaphore(name))

    ident = sb("const", "ident2", [P, P])
    xnT = sb("xnt", "xnT", [P, 4, 4, P])
    wq = [sb("wst", f"wq{i}", [P, KD, 256]) for i in range(2)]
    wq_hl = [sb("wq", f"wq_hl{i}", [P, KD, 2, 256], BF16) for i in range(2)]
    keys = sb("keys", "keys", [P, HC, NK])
    qT = sb("qt", "qT", [P, 2, SEQ])
    xn = nc.alloc_sbuf_tensor_at("xn", [P, 2, D], F32, offset=mem_map["s"])
    main_ps = [ctx.enter_context(nc.psum_tensor(f"q_ps{i}", [P, HALF], F32)) for i in range(2)]
    misc_ps = [ctx.enter_context(nc.psum_tensor(f"t_ps{i}", [P, HALF], F32)) for i in range(2)]
    par_in, keys_in = sem("par2_in"), sem("keys_in")
    wq_in = [sem(f"wq_in{i}") for i in range(2)]
    xn_ready = sem("xn_ready")
    u_in_ready, u_hi_done, u_lo_done = sem("u_first_in"), sem("u_first_hi"), sem("u_first_lo")
    turned, turned_out = sem("turned"), sem("turned_out")
    hi_done, lo_done = sem("xh_done"), sem("xl_done")
    whi_done, wlo_done = sem("wq_hi_done"), sem("wq_lo_done")
    q_full, q_out = sem("q_full"), sem("q_out")
    s_full, s_out = sem("s_full"), sem("s_out")
    turns = [(tb, kh) for tb in range(TB) for kh in range(2)]
    block = ctx.enter_context(nc.Block())

    @block.sync
    def _(sp):
        sp.dma_start(ident[:, :], ins["consts"][:, 0:P]).then_inc(par_in, 16)
        w = ins["peer_w_q"].rearrange("(k p) n -> p k n", p=P)
        for n in range(HC // 2):
            if n >= 2:
                sp.wait_ge(wlo_done, n - 1)
            sp.dma_start(wq[n % 2][:, :, :], w[:, :, n * 256:(n + 1) * 256]).then_inc(wq_in[n % 2], 16)
            if n == 0:
                sp.dma_start(keys[:, :, :], ins["peer_keys"]).then_inc(keys_in, 16)
        for c, (u_in, _, _) in enumerate(u_first):
            sp.dma_start(u_in[:, :, :], ins["peer_u"][c]).then_inc(u_in_ready, 16)

    @block.gpsimd
    def _(pool):
        def weights_low(n):
            pool.wait_ge(whi_done, n + 1)
            w = wq_hl[n % 2]
            pool.tensor_tensor(w[:, :, 1, :], wq[n % 2][:, :, :], w[:, :, 0, :], ALU.subtract).then_inc(wlo_done, 1)

        for n, (tb, kh) in enumerate(turns):
            pool.wait_ge(hi_done, n + 1)
            part = (slice(None), slice(4 * kh, 4 * kh + 4), slice(tb * P, (tb + 1) * P))
            pool.tensor_tensor(xl[part], xnT[:, n % 4, :, :], xh[part], ALU.subtract).then_inc(lo_done, 1)
        pool.wait_ge(wlo_done, 1)
        for n in range(1, HC // 2):
            weights_low(n)
        for c, (u_in, u_hi, u_lo) in enumerate(u_first):
            pool.wait_ge(u_hi_done, c + 1)
            pool.tensor_tensor(u_lo[:, :, :], u_in[:, :, :], u_hi[:, :, :], ALU.subtract).then_inc(u_lo_done, 1)
        pool.wait_ge(u_lo_done, 2)

    @block.scalar
    def _(act):
        def weights_high(n):
            act.wait_ge(wq_in[n % 2], 16 * (n // 2 + 1))
            if n >= 2:
                act.wait_ge(q_full, 4 * (n - 1))
            act.activation(wq_hl[n % 2][:, :, 0, :], wq[n % 2][:, :, :], ACT.Copy).then_inc(whi_done, 1)

        for n, (tb, kh) in enumerate(turns):
            if n == 4:
                weights_high(0)
            act.wait_ge(turned_out, n + 1)
            part = (slice(None), slice(4 * kh, 4 * kh + 4), slice(tb * P, (tb + 1) * P))
            act.activation(xh[part], xnT[:, n % 4, :, :], ACT.Copy).then_inc(hi_done, 1)
        weights_high(1)
        for hc in range(HC):
            for hf in range(2):
                n = 2 * hc + hf
                act.wait_ge(q_full, n + 1)
                if hf and hc % 2 == 0 and 2 <= hc < HC - 2:
                    weights_high(hc // 2 + 1)
                if hf == 0 and hc == HC - 2:
                    act.wait_ge(u_in_ready, 32)
                    for u_in, u_hi, _ in u_first:
                        act.activation(u_hi[:, :, :], u_in[:, :, :], ACT.Copy).then_inc(u_hi_done, 1)
                if hc >= 2:
                    act.wait_ge(s_full, 2 * (hc - 1))
                act.activation(qT[:, hc % 2, hf * HALF:(hf + 1) * HALF], main_ps[n % 2][:, :], ACT.Copy).then_inc(q_out, 1)

    @block.tensor
    def _(pe):
        pe.wait_ge(par_in, 16)

        def turn(n):
            tb, kh = turns[n]
            pe.wait_ge(xn_ready, tb + 1)
            if n >= 2:
                pe.wait_ge(turned_out, n - 1)
            for i in range(4):
                mm = pe.transpose(misc_ps[n % 2][:, i * P:(i + 1) * P],
                                  xn[:, tb % 2, (4 * kh + i) * P:(4 * kh + i + 1) * P], ident[:, :])
            mm.then_inc(turned, 1)

        def scores(hc):
            pe.wait_ge(keys_in, 16)
            for g in range(2):
                n = 2 * hc + g
                if n >= 2:
                    pe.wait_ge(s_out, n - 1)
                else:
                    pe.wait_ge(turned_out, 2 * TB)
                pe.wait_ge(q_out, 2 * hc + g + 1)
                for i in range(4):
                    tb = 4 * g + i
                    mm = pe.matmul(misc_ps[n % 2][:, i * P:(i + 1) * P], qT[:, hc % 2, tb * P:(tb + 1) * P],
                                   keys[:, hc, :], start=True, stop=True)
                mm.then_inc(s_full, 1)

        for n in range(10):
            turn(n)
        for hc in range(HC):
            for hf in range(2):
                n = 2 * hc + hf
                if n == 1:
                    for m in range(10, len(turns)):
                        turn(m)
                pe.wait_ge(wlo_done, hc // 2 + 1)
                pe.wait_ge(lo_done, 8 * hf + 8)
                if n >= 2:
                    pe.wait_ge(q_out, n - 1)
                ps, w = main_ps[n % 2][:, :], wq_hl[hc // 2 % 2][:, :, :, (hc % 2) * P:(hc % 2 + 1) * P]
                cols = slice(hf * HALF, (hf + 1) * HALF)
                for kd in range(KD):
                    pe.matmul(ps, w[:, kd, 0, :], xh[:, kd, cols], start=kd == 0, stop=False)
                    pe.matmul(ps, w[:, kd, 0, :], xl[:, kd, cols], start=False, stop=False)
                    mm = pe.matmul(ps, w[:, kd, 1, :], xh[:, kd, cols], start=False, stop=kd == KD - 1)
                mm.then_inc(q_full, 1)
            if hc:
                scores(hc - 1)
        scores(HC - 1)

    @block.vector
    def _(dve):
        def norm(tb):
            if tb >= 2:
                dve.wait_ge(turned, 2 * (tb - 1))
            dve.tensor_scalar(xn[:, tb % 2, :], h_sb[:, tb, :], root_h[:, 8 + tb:9 + tb], None, ALU.mult).then_inc(xn_ready, 1)

        norm(0)
        for n, (tb, kh) in enumerate(turns):
            if kh == 0 and tb + 1 < TB:
                norm(tb + 1)
            dve.wait_ge(turned, n + 1)
            if n >= 4:
                dve.wait_ge(lo_done, n - 3)
            dve.tensor_tensor(xnT[:, n % 4, :, :],
                              misc_ps[n % 2][:, :].rearrange("p (k t) -> p k t", k=4),
                              gain[:, 4 * kh:4 * kh + 4].unsqueeze(2).to_broadcast([P, 4, P]),
                              ALU.mult).then_inc(turned_out, 1)
            if n == 5:
                dve.wait_ge(whi_done, 1)
                dve.tensor_tensor(wq_hl[0][:, :, 1, :], wq[0][:, :, :], wq_hl[0][:, :, 0, :],
                                  ALU.subtract).then_inc(wlo_done, 1)
        for hc in range(HC):
            for g in range(2):
                n = 2 * hc + g
                dve.wait_ge(s_full, n + 1)
                dve.tensor_copy(s_sb[:, 4 * g:4 * g + 4, hc, :],
                                misc_ps[n % 2][:, :].rearrange("p (b n) -> p b n", b=4)).then_inc(s_out, 1)
    ctx.close()


def build_hidden(nc, ins, xh, xl, s_sb, g_dram, w_dram, u_first, first, mem_map):
    ctx = ExitStack()
    at = dict(mem_map)

    def sb(region, name, shape, dt=F32):
        size = int(np.prod(shape[1:])) * (2 if dt == BF16 else 4)
        off = at[region]
        at[region] = off + (size + 31) // 32 * 32
        assert at[region] <= mem_map[region] + mem_map[region + "_size"], (region, name)
        return nc.alloc_sbuf_tensor_at(name, shape, dt, offset=off)

    def sem(name):
        return ctx.enter_context(nc.semaphore(name))

    con = sb("const", "con3", [P, C_COLS - C_IOTA])
    ident = sb("const", "ident3", [P, P])
    iota = sb("const", "iota_bf", [P, P], BF16)
    iota50 = con[:, C_IOTA50 - C_IOTA:C_IOTA50 - C_IOTA + NCAND]
    u_in, u_hi, u_lo = zip(*u_first)
    g_out = [sb("g", f"g_out{i}", [P, SEQ]) for i in range(2)]
    codeT = sb("sel", "codeT", [P, SEQ])
    rowT = sb("sel", "rowT", [P, SEQ])
    wT = sb("sel", "wT", [P, SEQ])
    whT = sb("sel", "whT", [P, SEQ])
    sc = sb("hot", "sc", [P, HC, NK])
    top = sb("hot", "top", [P, HC, PK])
    topi = sb("hot", "topi", [P, HC, PK], U32)
    topf = sb("hot", "topf", [P, HC, PK])
    cand = sb("hot", "cand", [P, PH, NCAND])
    code = sb("hot", "code", [P, PH, NCAND])
    fin = sb("hot", "fin", [P, PH, PK])
    posi = sb("hot", "posi", [P, PH, PK], U32)
    posf = sb("hot", "posf", [P, PH, PK])
    wrow = sb("hot", "wrow", [P, PH, PK])
    crow = sb("hot", "crow", [P, PH, PK])
    wsum = sb("hot", "wsum", [P, 2, PH])
    match = sb("hot", "match", [P, 2, PK, NCAND])
    at["hot"] = mem_map["hot"]
    hot = [[sb("hot", f"hot_{n}{i}", [P, GT, P], BF16) for n in ("ihi", "ilo", "j")] for i in range(2)]
    wbuf = [nc.alloc_sbuf_tensor_at(f"wbuf{i}", [P, NK, WT], F32, offset=mem_map["s"] + i * NK * WT * 4) for i in range(2)]
    hid_ps = [ctx.enter_context(nc.psum_tensor(f"hid_ps{i}", [P, 2, HALF], F32)) for i in range(2)]
    w_ps = [ctx.enter_context(nc.psum_tensor(f"w_ps{i}", [P, HALF], F32)) for i in range(4)]

    one = sb("const", "one", [P, KD])
    par_in, iota_ready, one_ready = sem("par3_in"), sem("iota_ready"), sem("one_ready")
    u_loaded = [sem(f"u_loaded{i}") for i in range(2)]
    u_cast, u_ready = sem("u_cast"), sem("u_ready")
    hid_full, hid_out = sem("hid_full"), sem("hid_out")
    g_stored = [sem(f"g_stored{i}") for i in range(2)]
    w_stored = [sem(f"w_stored{i}") for i in range(2)]
    first_in = sem("first_in")
    fin_ready, exp_ready = sem("fin_ready"), sem("fin_exp")
    sel_ready, sel_turned, sel_out = sem("sel_ready"), sem("sel_turned"), sem("sel_out")
    hot_ready, w_full, w_out = sem("hot_ready"), sem("w_full"), sem("w_out")
    step = sem("dve_step3")
    block = ctx.enter_context(nc.Block())

    @block.sync
    def _(sp):
        sp.dma_start(con[:, :], ins["consts"][:, C_IOTA:C_COLS]).then_inc(par_in, 16)
        sp.dma_start(ident[:, :], ins["consts"][:, 0:P]).then_inc(par_in, 16)

        def load_u(i):
            for u in range(2):
                sp.wait_ge(u_ready, 2 * i + u + 1)
                sp.dma_start(u_in[u][:, :, :], ins["peer_u"][2 * i + u]).then_inc(u_loaded[u], 16)

        with sp.Fori(1, HOT_END // 2 + 2) as i:
            load_u(i)
        for i in range(2):
            sp.wait_ge(w_stored[i], 16 + 16 * (SEQ // WT // 2))
        w0, g0, v0 = first
        sp.dma_start(v0[:, :, :], ins["peer_v"][0:CG].rearrange("c p n -> p c n")).then_inc(first_in, 16)
        sp.dma_start(g0[:, :, :], g_dram[0:CG].rearrange("c p n -> p c n")).then_inc(first_in, 16)
        sp.dma_start(w0[:, :, :, :].rearrange("p g c t -> p g (c t)"),
                     w_dram[:, :, 0:CG, :].rearrange("g p c t -> p g (c t)")).then_inc(first_in, 16)
        with sp.Fori(HOT_END // 2 + 2, CH // 2) as i:
            load_u(i)
        sp.wait_ge(first_in, 48)

    @block.gpsimd
    def _(pool):
        pool.sem_inc(u_ready, 4)
        pool.memset(one[:, :], 1.0).then_inc(one_ready, 1)
        pool.wait_ge(one_ready, 1)
        with pool.Fori(1, CH // 2) as i:
            for u in range(2):
                pool.wait_ge(u_loaded[u], 16 * i)
                pool.wait_ge(hid_full, 2 * i + u + 1)
                pool.tensor_tensor(u_hi[u][:, :, :], u_in[u][:, :, :],
                                   one[:, :].unsqueeze(2).to_broadcast([P, KD, P]), ALU.mult).then_inc(u_cast, 1)
                pool.wait_ge(u_cast, 2 * i + u - 1)
                pool.tensor_tensor(u_lo[u][:, :, :], u_in[u][:, :, :], u_hi[u][:, :, :],
                                   ALU.subtract).then_inc(u_ready, 1)

    @block.scalar
    def _(act):
        act.sem_inc(hid_out, 2)
        act.sem_inc(w_out, 4)
        act.sem_inc(sel_out, 1)
        for i in range(2):
            act.sem_inc(g_stored[i], 16)
            act.sem_inc(w_stored[i], 16)

        def gelu(c, pair, u):
            act.wait_ge(hid_full, c + 3)
            act.wait_ge(g_stored[u], 16 * pair + 16)
            act.activation(g_out[u][:, :], hid_ps[u][:, :, :].rearrange("p a b -> p (a b)"),
                           ACT.Gelu_apprx_tanh).then_inc(hid_out, 1)
            act.wait_ge(hid_out, c + 3)
            act.dma_start(g_dram[c], g_out[u][:, :]).then_inc(g_stored[u], 16)

        with act.Fori(0, TB) as tb:
            for v in range(SEL):
                gelu(tb * SEL + v, tb * (SEL // 2) + v // 2, v % 2)
                if v == SEL - 2:
                    act.wait_ge(fin_ready, tb + 1)
                    act.activation(wrow[:, :, :], wrow[:, :, :], ACT.Exp).then_inc(exp_ready, 1)
            act.wait_ge(sel_turned, tb + 2)
            act.activation(codeT[:, bass.ts(tb, P)], w_ps[0][:, 0:P], ACT.Copy)
            act.activation(wT[:, bass.ts(tb, P)], w_ps[0][:, P:2 * P], ACT.Copy).then_inc(sel_out, 1)
        for v in range(2):
            gelu(SEL_END + v, SEL_END // 2, v)
        with act.Fori(0, (HOT_END - HOT_BEGIN) // 8) as it:
            for v in range(8):
                gelu(HOT_BEGIN + 8 * it + v, HOT_BEGIN // 2 + 4 * it + v // 2, v % 2)
                b = v // 4
                if v % 4 == 0:
                    act.wait_ge(w_stored[b], 16 * it + 16)
                for k in range(4):
                    act.wait_ge(w_full, 8 + 4 * (8 * it + v) + k + 1)
                    t0 = GT * (v % 4) + 4 * k
                    act.activation(wbuf[b][:, :, t0:t0 + 4],
                                   w_ps[k][:, :].rearrange("p (t j) -> p j t", t=4), ACT.Copy).then_inc(w_out, 1)
                if v % 4 == 3:
                    act.wait_ge(w_out, 4 + 4 * (8 * it + v) + 4)
                    act.dma_start(w_dram[2 * it + b], wbuf[b][:, :, :]).then_inc(w_stored[b], 16)
        with act.Fori(HOT_END // 2, CH // 2) as i:
            for v in range(2):
                gelu(2 * i + v, i, v)
        for i in range(2):
            act.wait_ge(g_stored[i], 16 + 16 * (CH // 2))
            act.wait_ge(w_stored[i], 16 + 16 * (SEQ // WT // 2))

    @block.tensor
    def _(pe):
        pe.sem_inc(hid_full, 2)
        pe.sem_inc(w_full, 8)
        pe.sem_inc(sel_turned, 1)

        def hidden(c, u):
            pe.wait_ge(u_ready, c + 3)
            pe.wait_ge(hid_out, c + 1)
            for hf in range(2):
                cols = slice(hf * HALF, (hf + 1) * HALF)
                for kd in range(KD):
                    pe.matmul(hid_ps[u][:, hf, :], u_hi[u][:, kd, :], xh[:, kd, cols], start=kd == 0, stop=False)
                    pe.matmul(hid_ps[u][:, hf, :], u_hi[u][:, kd, :], xl[:, kd, cols], start=False, stop=False)
                    mm = pe.matmul(hid_ps[u][:, hf, :], u_lo[u][:, kd, :], xh[:, kd, cols], start=False,
                                   stop=kd == KD - 1)
            mm.then_inc(hid_full, 1)

        with pe.Fori(0, TB) as tb:
            for v in range(SEL):
                hidden(tb * SEL + v, v % 2)
            pe.wait_ge(sel_ready, tb + 1)
            pe.wait_ge(sel_out, tb + 1)
            pe.wait_ge(par_in, 32)
            pe.transpose(w_ps[0][:, 0:P], crow[:, :, :].rearrange("p h k -> p (h k)"), ident[:, :])
            pe.transpose(w_ps[0][:, P:2 * P], wrow[:, :, :].rearrange("p h k -> p (h k)"),
                         ident[:, :]).then_inc(sel_turned, 1)
        for v in range(2):
            hidden(SEL_END + v, v)
        pe.wait_ge(sel_out, TB + 1)
        with pe.Fori(0, (HOT_END - HOT_BEGIN) // 8) as it:
            for v in range(8):
                hidden(HOT_BEGIN + 8 * it + v, v % 2)
                g = 8 * it + v
                hi, lo, hj = hot[v % 2]
                pe.wait_ge(hot_ready, g + 1)
                for k in range(4):
                    pe.wait_ge(w_out, 4 * g + k + 1)
                    for i in range(4):
                        t = 4 * k + i
                        dst = w_ps[k][:, i * P:(i + 1) * P]
                        pe.matmul(dst, hi[:, t, :], hj[:, t, :], start=True, stop=False)
                        mm = pe.matmul(dst, lo[:, t, :], hj[:, t, :], start=False, stop=True)
                    mm.then_inc(w_full, 1)
        with pe.Fori(HOT_END // 2, CH // 2) as i:
            for v in range(2):
                hidden(2 * i + v, v)

    @block.vector
    def _(dve):
        tt, ts = dve.tensor_tensor, dve.tensor_scalar
        dve.wait_ge(par_in, 32)
        dve.tensor_copy(iota[:, :], con[:, 0:P]).then_inc(iota_ready, 1)
        with dve.Fori(0, TB) as tb:
            n = 0

            def link(i):
                nonlocal n
                i.then_inc(step, 1)
                n += 1
                dve.wait_ge(step, n)

            def top16(src, vals, idx, rows):
                for r in rows:
                    i = dve.max(vals[:, r, 0:8], src[:, r, :])
                link(i)
                for r in rows:
                    i = dve.max_index(idx[:, r, 0:8], vals[:, r, 0:8], src[:, r, :])
                link(i)
                for r in rows:
                    i = dve.match_replace(src[:, r, :], vals[:, r, 0:8], src[:, r, :], NEG)
                link(i)
                for r in rows:
                    i = dve.max(vals[:, r, 8:16], src[:, r, :])
                link(i)
                for r in rows:
                    i = dve.max_index(idx[:, r, 8:16], vals[:, r, 8:16], src[:, r, :])
                link(i)

            link(dve.tensor_copy(sc[:, :, :], s_sb[:, bass.ds(tb, 1), :, :].rearrange("p o h n -> p (o h) n")))
            top16(sc, top, topi, range(HC))
            link(dve.tensor_copy(topf[:, :, :], topi[:, :, :]))
            v4 = top[:, :, :].rearrange("p (h c) k -> p h c k", c=2)
            i4 = topf[:, :, :].rearrange("p (h c) k -> p h c k", c=2)
            link(ts(i4[:, :, 0, :], i4[:, :, 0, :], float(NK), None, ALU.mult))
            dve.wait_ge(sel_turned, tb + 1)
            off = 0
            for a, na, nb in PAIRS:
                for dst, src in ((cand, v4), (code, i4)):
                    out = dst[:, :, off:off + na * nb].rearrange("p h (a b) -> p h a b", a=na)
                    x = src[:, :, 0, a:a + na].unsqueeze(3).to_broadcast([P, PH, na, nb])
                    y = src[:, :, 1, 0:nb].unsqueeze(2).to_broadcast([P, PH, na, nb])
                    i = tt(out, x, y, ALU.add)
                off += na * nb
            link(i)
            top16(cand, fin, posi, range(PH))
            tt(wrow[:, :, :], fin[:, :, :], fin[:, :, 0:1].to_broadcast([P, PH, PK]), ALU.subtract).then_inc(fin_ready, 1)
            link(dve.tensor_copy(posf[:, :, :], posi[:, :, :]))
            for h in range(0, PH, 2):
                link(tt(match[:, :, :, :], posf[:, h:h + 2, :].unsqueeze(3).to_broadcast([P, 2, PK, NCAND]),
                        iota50.unsqueeze(1).unsqueeze(1).to_broadcast([P, 2, PK, NCAND]), ALU.is_equal))
                link(tt(match[:, :, :, :], match[:, :, :, :],
                        code[:, h:h + 2, :].unsqueeze(2).to_broadcast([P, 2, PK, NCAND]), ALU.mult))
                link(dve.tensor_reduce(crow[:, h:h + 2, :], match[:, :, :, :], AX.X, ALU.add))
            dve.wait_ge(exp_ready, tb + 1)
            link(dve.tensor_reduce(wsum[:, 0, :], wrow[:, :, :], AX.X, ALU.add))
            link(dve.reciprocal(wsum[:, 1, :], wsum[:, 0, :]))
            dve.sem_clear(step)
            tt(wrow[:, :, :], wrow[:, :, :], wsum[:, 1, :].unsqueeze(2).to_broadcast([P, PH, PK]),
               ALU.mult).then_inc(sel_ready, 1)
        dve.wait_ge(sel_out, TB + 1)
        base = [0]

        def link(i):
            i.then_inc(step, 1)
            base[0] += 1
            dve.wait_ge(step, base[0])

        link(ts(rowT[:, :], codeT[:, :], 1.0 / NK, -(NK - 1) / (2.0 * NK), ALU.mult, ALU.add))
        link(ts(rowT[:, :], rowT[:, :], MAGIC, None, ALU.add))
        link(ts(rowT[:, :], rowT[:, :], -MAGIC, None, ALU.add))
        link(dve.scalar_tensor_tensor(codeT[:, :], rowT[:, :], -float(NK), codeT[:, :], ALU.mult, ALU.add))
        half = hot[0][0][:, 0:8, :].rearrange("p a b -> p (a b)")
        link(dve.tensor_copy(half, wT[:, :]))
        link(dve.tensor_copy(whT[:, :], half))
        link(tt(wT[:, :], wT[:, :], whT[:, :], ALU.subtract))
        with dve.Fori(0, (HOT_END - HOT_BEGIN) // 2) as q:
            for b in range(2):
                hi, lo, hj = hot[b]
                dve.wait_ge(w_full, 4 * (2 * q + b) + 4)
                for i in range(GT):
                    t = (2 * q + b) * GT + i
                    at_t = lambda x: x[:, bass.ds(t, 1)]
                    ts(hi[:, i, :], iota[:, :], at_t(rowT), at_t(whT), ALU.is_equal, ALU.mult)
                    ts(lo[:, i, :], iota[:, :], at_t(rowT), at_t(wT), ALU.is_equal, ALU.mult)
                    last = ts(hj[:, i, :], iota[:, :], at_t(codeT), None, ALU.is_equal)
                last.then_inc(hot_ready, 1)
    ctx.close()


def build_output(nc, ins, h_sb, g_dram, w_dram, first, out, mem_map):
    ctx = ExitStack()
    at = dict(mem_map)

    def sb(region, name, shape, dt=F32):
        size = int(np.prod(shape[1:])) * (2 if dt == BF16 else 4)
        off = at[region]
        at[region] = off + (size + 31) // 32 * 32
        assert at[region] <= mem_map[region] + mem_map[region + "_size"], (region, name)
        return nc.alloc_sbuf_tensor_at(name, shape, dt, offset=off)

    def sem(name):
        return ctx.enter_context(nc.semaphore(name))

    stat = sb("const", "stat4", [P, 64])
    gain = sb("const", "gain4", [P, D])
    w_sb, g_sb, v_sb = ([f] for f in first)
    names = ("a_hi", "a_lo", "v_hi", "v_lo")
    halves = [[sb("b", f"{n}0", [P, CG, SEQ], BF16) for n in names]]
    at["b"] += 3 * CG * SEQ * 4
    w_sb.append(sb("b", "w_sb1", [P, NW, CG, WT]))
    g_sb.append(sb("b", "g_sb1", [P, CG, SEQ]))
    v_sb.append(sb("b", "v_sb1", [P, CG, D]))
    halves.append([sb("b", f"{n}1", [P, CG, SEQ], BF16) for n in names])
    a_hi, a_lo, v_hi, v_lo = zip(*halves)
    ps = [ctx.enter_context(nc.psum_tensor(f"o_ps{i}", [P, HALF], F32)) for i in range(8)]
    gain_in = sem("gain4_in")
    loaded = [sem(f"gwv_loaded{i}") for i in range(2)]
    act_made = sem("act_made")
    ahi_made, alo_made = sem("ahi_made"), sem("alo_made")
    vhi_made, vlo_made = sem("vhi_made"), sem("vlo_made")
    o_full, o_out = sem("o_full"), sem("o_out")
    sq_done, rs_done, y_ready = sem("sq4_done"), sem("rs4_done"), sem("y_ready")
    half_set, pstep = sem("half_set4"), sem("pool_step4")
    stored = sem("y_stored")
    NG = CH // CG
    TILES = 2 * TB
    block = ctx.enter_context(nc.Block())

    @block.sync
    def _(sp):
        def chunks(src, first, count):
            return src[bass.ds(first, count)].rearrange("c p n -> p c n")

        def load(q, b):
            sp.wait_ge(alo_made, CG * q + CG)
            sp.wait_ge(vlo_made, CG * q + CG)
            sp.dma_start(v_sb[b][:, :, :], chunks(ins["peer_v"], CG * q, CG)).then_inc(loaded[b], 16)
            sp.dma_start(g_sb[b][:, :, :], chunks(g_dram, CG * q, CG)).then_inc(loaded[b], 16)
            sp.dma_start(w_sb[b][:, :, :, :].rearrange("p g c t -> p g (c t)"),
                         w_dram[:, :, bass.ds(CG * q, CG), :].rearrange("g p c t -> p g (c t)")).then_inc(loaded[b], 16)

        load(1, 1)
        with sp.Fori(1, NG // 2) as i:
            for b in range(2):
                load(2 * i + b, b)
        sp.dma_start(gain[:, :], ins["norm_final"].partition_broadcast(P)).then_inc(gain_in, 16)
        for tb in range(TB):
            sp.wait_ge(y_ready, tb + 1)
            sp.dma_start(out[tb * P:(tb + 1) * P, :], h_sb[:, tb, :]).then_inc(stored, 16)
        sp.wait_ge(stored, 16 * TB)

    @block.gpsimd
    def _(pool):
        pool.sem_inc(vlo_made, 2 * CG)
        pool.memset(stat[:, 32:33], -0.5).then_inc(half_set, 1)
        pool.wait_ge(half_set, 1)
        with pool.Fori(0, NG // 2) as i:
            for b in range(2):
                q = 2 * i + b
                for c in range(CG):
                    pool.wait_ge(vhi_made, CG * q + c + 1)
                    pool.tensor_tensor(v_lo[b][:, c, :], v_sb[b][:, c, :], v_hi[b][:, c, :],
                                       ALU.subtract).then_inc(vlo_made, 1)
        for tb in range(TB):
            pool.wait_ge(sq_done, tb + 1)
            pool.tensor_scalar(stat[:, tb:tb + 1], stat[:, tb:tb + 1], 1.0 / D, EPS, ALU.mult, ALU.add).then_inc(pstep, 1)
            pool.wait_ge(pstep, tb + 1)
            pool.tensor_tensor(stat[:, 16 + tb:17 + tb], stat[:, tb:tb + 1], stat[:, 32:33], ALU.pow).then_inc(rs_done, 1)

    @block.scalar
    def _(act):
        def upper(q, i, b):
            act.wait_ge(loaded[b], 48 * i + 48 * b)
            act.wait_ge(o_full, TILES * q + TILES)
            for c in range(CG):
                act.activation(v_hi[b][:, c, :], v_sb[b][:, c, :], ACT.Copy).then_inc(vhi_made, 1)
            for c in range(CG):
                act.wait_ge(act_made, CG * q + c + 1)
                act.activation(a_hi[b][:, c, :], g_sb[b][:, c, :], ACT.Copy).then_inc(ahi_made, 1)

        for c in range(CG):
            act.activation(v_hi[0][:, c, :], v_sb[0][:, c, :], ACT.Copy).then_inc(vhi_made, 1)
            act.wait_ge(act_made, c + 1)
            act.activation(a_hi[0][:, c, :], g_sb[0][:, c, :], ACT.Copy).then_inc(ahi_made, 1)
        upper(1, 0, 1)
        with act.Fori(1, NG // 2) as i:
            for b in range(2):
                upper(2 * i + b, i, b)
        act.wait_ge(vlo_made, 2 * CG + CG * (NG - 1))
        for tb in range(TB):
            act.wait_ge(o_out, 8 + (NG - 1) * TILES + 2 * tb + 2)
            if tb >= 4:
                act.wait_ge(sq_done, tb - 3)
            act.activation(v_sb[0][:, tb % 4, :], h_sb[:, tb, :], ACT.Square, accum_out=stat[:, tb:tb + 1]).then_inc(sq_done, 1)

    @block.tensor
    def _(pe):
        pe.sem_inc(o_full, 2 * TILES)
        def product(b, n, c):
            tb, hf = divmod(n, 2)
            tok, col = slice(tb * P, (tb + 1) * P), slice(hf * HALF, (hf + 1) * HALF)
            bank = ps[n % 8][:, :]
            pe.matmul(bank, a_hi[b][:, c, tok], v_hi[b][:, c, col], start=c == 0, stop=False)
            pe.matmul(bank, a_hi[b][:, c, tok], v_lo[b][:, c, col], start=False, stop=False)
            return pe.matmul(bank, a_lo[b][:, c, tok], v_hi[b][:, c, col], start=False, stop=c == CG - 1)

        def group(q, b):
            pe.wait_ge(vlo_made, CG * q + 3 * CG)
            pe.wait_ge(alo_made, CG * q + 3 * CG)
            for n in range(TILES):
                pe.wait_ge(o_out, TILES * q + n + 1)
                for c in range(CG):
                    mm = product(b, n, c)
                mm.then_inc(o_full, 1)

        for c in range(CG):
            pe.wait_ge(vlo_made, 2 * CG + c + 1)
            pe.wait_ge(alo_made, 2 * CG + c + 1)
            for n in range(8):
                mm = product(0, n, c)
                if c == CG - 1:
                    mm.then_inc(o_full, 1)
        for n in range(8, TILES):
            pe.wait_ge(o_out, n + 1)
            for c in range(CG):
                mm = product(0, n, c)
            mm.then_inc(o_full, 1)
        group(1, 1)
        with pe.Fori(1, NG // 2) as i:
            for b in range(2):
                group(2 * i + b, b)

    @block.vector
    def _(dve):
        dve.sem_inc(o_out, 8)
        dve.sem_inc(alo_made, 2 * CG)

        def activations(q, i, b):
            dve.wait_ge(loaded[b], 48 * i + 48 * b)
            dve.wait_ge(o_full, TILES * q + TILES)
            for c in range(CG):
                g = g_sb[b][:, c, :].rearrange("p (g t) -> p g t", g=NW)
                dve.tensor_tensor(g, g, w_sb[b][:, :, c, :], ALU.mult).then_inc(act_made, 1)
            for c in range(CG):
                dve.wait_ge(ahi_made, CG * q + c + 1)
                dve.tensor_tensor(a_lo[b][:, c, :], g_sb[b][:, c, :], a_hi[b][:, c, :], ALU.subtract).then_inc(alo_made, 1)

        def join(q, tiles):
            for n in tiles:
                tb, hf = divmod(n, 2)
                acc = h_sb[:, tb, hf * HALF:(hf + 1) * HALF]
                dve.wait_ge(o_full, TILES * q + 2 * TILES + n + 1)
                dve.tensor_tensor(acc, acc, ps[n % 8][:, :], ALU.add).then_inc(o_out, 1)

        def gated(c):
            g = g_sb[0][:, c, :].rearrange("p (g t) -> p g t", g=NW)
            dve.tensor_tensor(g, g, w_sb[0][:, :, c, :], ALU.mult).then_inc(act_made, 1)

        gated(0)
        for c in range(CG):
            if c + 1 < CG:
                gated(c + 1)
            dve.wait_ge(ahi_made, c + 1)
            dve.tensor_tensor(a_lo[0][:, c, :], g_sb[0][:, c, :], a_hi[0][:, c, :], ALU.subtract).then_inc(alo_made, 1)
        join(0, range(8))
        activations(1, 0, 1)
        join(0, range(8, TILES))
        activations(2, 1, 0)
        join(1, range(TILES))
        with dve.Fori(1, NG // 2 - 1) as i:
            activations(2 * i + 1, i, 1)
            join(2 * i, range(TILES))
            activations(2 * i + 2, i + 1, 0)
            join(2 * i + 1, range(TILES))
        activations(NG - 1, NG // 2 - 1, 1)
        join(NG - 2, range(TILES))

        def final_norm(tb):
            dve.wait_ge(rs_done, tb + 1)
            dve.scalar_tensor_tensor(h_sb[:, tb, :], h_sb[:, tb, :], stat[:, 16 + tb:17 + tb], gain[:, :],
                                     ALU.mult, ALU.mult).then_inc(y_ready, 1)

        dve.wait_ge(gain_in, 16)
        for tb in range(TB):
            join(NG - 1, (2 * tb, 2 * tb + 1))
            if tb:
                final_norm(tb - 1)
        final_norm(TB - 1)
    ctx.close()


BASE = 16512


def regions(*parts):
    out, at = {}, BASE
    for name, kib in parts:
        out[name], out[name + "_size"] = at, int(kib * 1024)
        at += int(kib * 1024)
    assert at <= 229344
    return out


MIX_MAP = regions(("const", 5.75), ("nt", 32), ("x", 32), ("w", 48), ("stage", 8), ("zt", 16), ("ret", 16),
                  ("s5c", 20), ("tmp", 24), ("sg", 6))
SCORE_MAP = regions(("const", 5.75), ("nt", 32), ("xhl", 32), ("s", 64), ("xnt", 8), ("wst", 16), ("wq", 16),
                    ("keys", 8), ("qt", 8))
HIDDEN_MAP = regions(("const", 5.75), ("nt", 32), ("xhl", 32), ("s", 64), ("g", 8),
                     ("sel", 16), ("hot", 24), ("pad", 8), ("u", 16))
OUT_MAP = regions(("const", 5.75), ("nt", 32), ("b", 160))


def build_program(nc, ins, out):
    h_sb = nc.alloc_sbuf_tensor_at("h", [P, TB, D], F32, offset=MIX_MAP["nt"])
    xh = nc.alloc_sbuf_tensor_at("xh", [P, KD, SEQ], BF16, offset=SCORE_MAP["xhl"])
    xl = nc.alloc_sbuf_tensor_at("xl", [P, KD, SEQ], BF16, offset=SCORE_MAP["xhl"] + KD * SEQ * 2)
    s_sb = nc.alloc_sbuf_tensor_at("scores", [P, TB, HC, NK], F32, offset=SCORE_MAP["s"])
    g_dram = nc.dram_tensor("g_scratch", [CH, P, SEQ], F32).ap()
    w_dram = nc.dram_tensor("w_scratch", [SEQ // WT, P, NK, WT], F32).ap()
    at = OUT_MAP["b"] + 4 * CG * SEQ * 2
    first = [nc.alloc_sbuf_tensor_at(n, shape, F32, offset=at + i * CG * SEQ * 4)
             for i, (n, shape) in enumerate((("w_sb0", [P, NW, CG, WT]), ("g_sb0", [P, CG, SEQ]), ("v_sb0", [P, CG, D])))]
    root_h = nc.alloc_sbuf_tensor_at("root_h", [P, 2 * TB], F32, offset=BASE + 5632)
    gain_h = nc.alloc_sbuf_tensor_at("gain_h", [P, KD], F32, offset=BASE + 5632 + 8 * TB)
    u_at = HIDDEN_MAP["u"]
    u_first = [(nc.alloc_sbuf_tensor_at(f"u_in{i}", [P, KD, P], F32, offset=u_at + i * 4096),
                nc.alloc_sbuf_tensor_at(f"u_hi{i}", [P, KD, P], BF16, offset=u_at + 8192 + i * 2048),
                nc.alloc_sbuf_tensor_at(f"u_lo{i}", [P, KD, P], BF16, offset=u_at + 12288 + i * 2048)) for i in range(2)]
    build_mixer(nc, ins, h_sb, root_h, gain_h, MIX_MAP)
    build_scores(nc, ins, h_sb, root_h, gain_h, xh, xl, s_sb, u_first, SCORE_MAP)
    build_hidden(nc, ins, xh, xl, s_sb, g_dram, w_dram, u_first, first, HIDDEN_MAP)
    build_output(nc, ins, h_sb, g_dram, w_dram, first, out, OUT_MAP)


def columns(a):
    return a.reshape(-1, P).T


def s5_blocks(a):
    out = np.zeros((P, S5T, P), a.dtype)
    for group in range(a.shape[0]):
        s, g = divmod(group, 2)
        c = 32 * (s % 4) + 16 * g
        out[64 * g:64 * g + 64, s, c:c + 16] = a[group]
    return out


def layout(a):
    g = {n: a[n][0] for n in ("x", "mem", "w_in", "w_mem_kv", "s5_w_glu", "w_branch_ret", "w_branch_s5",
                              "w_branch_mem", "w_out", "peer_w_q")}
    g["norm_final"] = a["norm_final"]
    for n in ("positions", "norm_mix", "norm_mem", "norm_ffn", "s5_d"):
        g[n] = columns(a[n][0])
    for n in ("s5_a_re", "s5_a_im"):
        g[n] = columns(a[n][0].reshape(-1))
    g["s5_log_dt"] = columns(np.repeat(a["s5_log_dt"][0], 64))
    for n in ("s5_b_re", "s5_b_im"):
        g[n] = s5_blocks(a[n][0])
    for n in ("s5_c_re", "s5_c_im"):
        g[n] = s5_blocks(a[n][0].transpose(0, 2, 1))
    g["peer_keys"] = a["peer_keys"][0].reshape(HC, NK, P).transpose(2, 0, 1)
    g["peer_u"] = a["peer_u"][0].reshape(NK, NK, KD, P).transpose(1, 3, 2, 0)
    g["peer_v"] = a["peer_v"][0].reshape(NK, NK, D).transpose(1, 0, 2)
    g["consts"] = constants()
    return {n: np.ascontiguousarray(v) for n, v in g.items()}


def kernel(**inputs):
    import concourse.bacc as bacc
    from concourse.bass_utils import run_bass_kernel_spmd

    nc = bacc.Bacc("TRN2", target_bir_lowering=False, num_devices=1)
    arrays = layout({n: np.asarray(v) for n, v in inputs.items()})
    ins = {n: nc.dram_tensor("in_" + n, v.shape, mybir.dt.from_np(v.dtype), kind="ExternalInput").ap()
           for n, v in arrays.items()}
    out = nc.dram_tensor("out", [SEQ, D], F32, kind="ExternalOutput").ap()
    build_program(nc, ins, out)
    r = run_bass_kernel_spmd(nc, [{"in_" + n: v for n, v in arrays.items()}], core_ids=[0])
    return r.results[0]["out"].reshape(1, SEQ, D)
```
